# Optimizing a Trainium2 kernel written in Bass

```python
import math
import jax, jax.numpy as jnp
from jax import lax
import numpy as np

D_MODEL = 1024
BATCH = 1
SEQ = 1024
DEPTH = 1

GRID_W = 64
CTX_LEN = 256

CONV_CH = 256
HY_CH = 256
RW_HEADS = 8
RW_HEAD_DIM = 64
RW_CH = RW_HEADS * RW_HEAD_DIM
MIX_W = CONV_CH + HY_CH + RW_CH
RW_DECAY_RANK = 64
RW_ICLR_RANK = 64
RW_GATE_RANK = 128
RW_COLS = 3 * RW_CH + 2 * RW_DECAY_RANK + 2 * RW_ICLR_RANK + RW_GATE_RANK
P_IN = 3 * CONV_CH + 3 * HY_CH + RW_COLS
RW_GN_EPS = 64e-5
HY_ORDER = 2
HY_EMB = 33
HY_BANDS = (HY_EMB - 1) // 2
HY_HID = 64
HY_TARGET = 1e-2
HY_FAST = 0.3
HY_SLOW = 1.5
N_EXPERTS = 64
TOP_K = 8
EXPERT_FF = 256
SHARED_FF = 256
ROUTED_SCALE = 2.5
EXPERT_BLOCK = 256
DN_ALPHA = (2 * DEPTH) ** 0.25
DN_BETA = (8 * DEPTH) ** -0.25
LN_EPS = 1e-5

kernel_name = 'hybrid_conv_hyena_rwkv7_moe_dit'

F32 = jnp.float32

def layer_norm(x, g, b):
    xf = x.astype(F32)
    mu = jnp.mean(xf, -1, keepdims=True)
    var = jnp.mean(jnp.square(xf - mu), -1, keepdims=True)
    return ((xf - mu) * lax.rsqrt(var + LN_EPS) * g + b).astype(x.dtype)

def rms_norm(y, g):
    yf = y.astype(F32)
    return (yf * lax.rsqrt(jnp.mean(yf * yf, -1, keepdims=True) + LN_EPS) * g).astype(y.dtype)

def dwconv3(u, w, axis=1):
    n = u.shape[axis]
    pad = [(0, 0)] * u.ndim
    pad[axis] = (1, 1)
    up = jnp.pad(u, pad)
    tap = lambda s: lax.slice_in_dim(up, s, s + n, axis=axis)
    return tap(0) * w[0] + tap(1) * w[1] + tap(2) * w[2]

def short_conv_mixer(u, conv_w, rows):
    b_gate, c_gate, xin = jnp.split(u, 3, axis=-1)
    z = c_gate * xin
    if rows is None:
        z = dwconv3(z, conv_w, axis=1)
    else:
        bsz, n, ch = z.shape
        z = dwconv3(z.reshape(bsz, rows, GRID_W, ch), conv_w, axis=1).reshape(bsz, n, ch)
    return b_gate * z

def hyena_filters(L, w1, b1, w2, b2, w3, b3, w_out, freq):
    w1, b1, w2, b2, w3, b3, w_out, freq = (a.astype(F32) for a in (w1, b1, w2, b2, w3, b3, w_out, freq))
    t = jnp.linspace(0.0, 1.0, L, dtype=F32)[:, None]
    pos = jnp.arange(L, dtype=F32)[:, None]
    bands = jnp.linspace(1e-4, HY_BANDS - 1, HY_BANDS, dtype=F32)[None, :]
    ang = (2.0 * math.pi / L) * pos * bands
    z = jnp.concatenate([t, jnp.cos(ang), -jnp.sin(ang)], axis=-1)
    h = jnp.sin(freq * (z @ w1 + b1))
    h = jnp.sin(freq * (h @ w2 + b2))
    h = jnp.sin(freq * (h @ w3 + b3))
    h = (h @ w_out).reshape(L, HY_ORDER, 2, HY_CH)
    deltas = jnp.abs(jnp.linspace(math.log(HY_TARGET) / HY_SLOW, math.log(HY_TARGET) / HY_FAST, HY_CH, dtype=F32))
    h = h * jnp.exp(-t * deltas)[:, None, None, :]
    k_two = jnp.concatenate([h[:, :, 0], jnp.zeros((1, HY_ORDER, HY_CH), F32), jnp.flip(h[1:, :, 1], axis=0)], axis=0)
    return jnp.fft.rfft(k_two, axis=0)

def fft_long_conv(u, kf, skip):
    L = u.shape[1]
    uf32 = u.astype(F32)
    uf = jnp.fft.rfft(uf32, n=2 * L, axis=1)
    y = jnp.fft.irfft(uf * kf[None], n=2 * L, axis=1)[:, :L]
    return y + uf32 * skip.astype(F32)

def hyena_mixer(u, sconv_w, sconv_b, kf, skip):
    u = dwconv3(u, sconv_w) + sconv_b
    v, x1, x2 = jnp.split(u, 3, axis=-1)
    z = fft_long_conv(v, kf[:, 0], skip[0]) * x1
    z = fft_long_conv(z, kf[:, 1], skip[1]) * x2
    return z.astype(u.dtype)

def _heads(t):
    return t.reshape(t.shape[:-1] + (RW_HEADS, RW_HEAD_DIM))

def rwkv_inputs(u, mu, w0, w_up, a0, a_up, k_k, k_a):
    bsz, n, _ = u.shape
    shift_w = jnp.stack([mu[0], 1.0 - mu[0] - mu[1], mu[1]])
    u = dwconv3(u, shift_w)
    r = u[..., :RW_CH]
    k = u[..., RW_CH:2 * RW_CH]
    v = u[..., 2 * RW_CH:3 * RW_CH]
    o = 3 * RW_CH
    wd = u[..., o:o + 2 * RW_DECAY_RANK].reshape(bsz, n, 2, RW_DECAY_RANK)
    o += 2 * RW_DECAY_RANK
    ad = u[..., o:o + 2 * RW_ICLR_RANK].reshape(bsz, n, 2, RW_ICLR_RANK)
    gd = u[..., o + 2 * RW_ICLR_RANK:]
    w_log = -jax.nn.softplus(-(w0 + jnp.einsum('bldr,drc->bldc', jnp.tanh(wd), w_up))) - 0.5
    decay = jnp.exp(-jnp.exp(w_log.astype(F32)))
    a = jax.nn.sigmoid(a0 + jnp.einsum('bldr,drc->bldc', ad, a_up))
    kd = k[:, :, None, :] * (1.0 + (a - 1.0) * k_a)
    kk = _heads(k * k_k).astype(F32)
    kk = kk * lax.rsqrt(jnp.maximum(jnp.sum(kk * kk, -1, keepdims=True), 1e-24))
    return (_heads(r), _heads(decay), _heads(kd), _heads(v), kk, _heads(a), gd)

def _wkv_step(S, inp):
    r, w, k, v, kk, a = inp
    sk = jnp.einsum('dbhvk,dbhk->dbhv', S, kk)
    S = S * w[..., None, :] - sk[..., None] * (kk * a)[..., None, :] + v[..., None] * k[..., None, :]
    y = jnp.einsum('dbhvk,dbhk->dbhv', S, r)
    return S, y

def wkv_bidir(s0, r, decay, kd, v, kk, a):
    def to_scan(t):
        t = jnp.stack([t[:, :, 0], jnp.flip(t[:, :, 1], axis=1)], axis=0).astype(F32)
        return jnp.moveaxis(t, 2, 0)
    dup = lambda t: jnp.stack([t, t], axis=2)
    xs = tuple(to_scan(t) for t in (dup(r), decay, kd, dup(v), dup(kk), a))
    S, ys = lax.scan(_wkv_step, s0, xs)
    y = ys[:, 0] + jnp.flip(ys[:, 1], axis=0)
    return S, jnp.moveaxis(y, 0, 1)

def rwkv_output(y, r, kd, v, gd, g_up, r_k, lnx_g, lnx_b):
    bsz, n = y.shape[:2]
    mu = jnp.mean(y, -1, keepdims=True)
    var = jnp.mean(jnp.square(y - mu), -1, keepdims=True)
    yn = ((y - mu) * lax.rsqrt(var + RW_GN_EPS)).reshape(bsz, n, RW_CH) * lnx_g + lnx_b
    s = jnp.einsum('blhn,bldhn,hn->blh', r.astype(F32), kd.astype(F32), r_k.astype(F32))
    bonus = (s[..., None] * v.astype(F32)).reshape(bsz, n, RW_CH)
    g = jax.nn.sigmoid(gd) @ g_up
    return ((yn + bonus) * g).astype(gd.dtype)

def token_mixer(hl, hc, lp, need_ctx):
    L_lat, L_ctx = hl.shape[1], hc.shape[1]
    rows = L_lat // GRID_W
    cut = [3 * CONV_CH, 3 * CONV_CH + 3 * HY_CH]
    pl_a, pl_h, pl_r = jnp.split(hl @ lp['w_in'], cut, axis=-1)
    pc_a, pc_h, pc_r = jnp.split(hc @ lp['w_in'], cut, axis=-1)
    rw_p = (lp['rw_mu'], lp['rw_w0'], lp['rw_w_up'], lp['rw_a0'], lp['rw_a_up'], lp['rw_k_k'], lp['rw_k_a'])
    rc = rwkv_inputs(pc_r, *rw_p)
    rl = rwkv_inputs(pl_r, *rw_p)
    s0 = jnp.zeros((2, hl.shape[0], RW_HEADS, RW_HEAD_DIM, RW_HEAD_DIM), F32)
    s_ctx, y_ctx = wkv_bidir(s0, *rc[:6])
    _, y_lat = wkv_bidir(s_ctx, *rl[:6])

    def merge(p_a, p_h, rw, y, grid_rows, L):
        ya = short_conv_mixer(p_a, lp['conv_a'], grid_rows)
        kf = hyena_filters(L, lp['hf_w1'], lp['hf_b1'], lp['hf_w2'], lp['hf_b2'],
                           lp['hf_w3'], lp['hf_b3'], lp['hf_wout'], lp['hf_freq'])
        yh = hyena_mixer(p_h, lp['hy_sconv_w'], lp['hy_sconv_b'], kf, lp['hf_skip'])
        r, _, kd, v, _, _, gd = rw
        yr = rwkv_output(y, r, kd, v, gd, lp['rw_g_up'], lp['rw_r_k'], lp['rw_lnx_g'], lp['rw_lnx_b'])
        g = lp['mix_norm_g']
        ycat = jnp.concatenate([rms_norm(ya, g[:CONV_CH]), rms_norm(yh, g[CONV_CH:]), yr], axis=-1)
        return ycat @ lp['w_out']

    out_l = merge(pl_a, pl_h, rl, y_lat, rows, L_lat)
    out_c = merge(pc_a, pc_h, rc, y_ctx, None, L_ctx) if need_ctx else None
    return out_l, out_c

def swiglu(t, wg, wu, wd):
    return (jax.nn.silu(t @ wg) * (t @ wu)) @ wd

def routed_experts(t, idx, gate, w_gate, w_up, w_down):
    n_tok, d = t.shape
    m = n_tok * TOP_K
    flat_e = idx.reshape(m)
    flat_tok = jnp.arange(m, dtype=jnp.int32) // TOP_K
    flat_gate = gate.reshape(m)
    order = jnp.argsort(flat_e)
    e_sorted = flat_e[order]
    counts = jnp.bincount(flat_e, length=N_EXPERTS)
    padded = (counts + EXPERT_BLOCK - 1) // EXPERT_BLOCK * EXPERT_BLOCK
    pad_end = jnp.cumsum(padded)
    pad_start = pad_end - padded
    cnt_start = jnp.cumsum(counts) - counts
    slot = pad_start[e_sorted] + jnp.arange(m, dtype=jnp.int32) - cnt_start[e_sorted]
    n_blocks = -(-(m + N_EXPERTS * (EXPERT_BLOCK - 1)) // EXPERT_BLOCK)
    cap = n_blocks * EXPERT_BLOCK
    slot_tok = jnp.full((cap,), n_tok, jnp.int32).at[slot].set(flat_tok[order])
    slot_gate = jnp.zeros((cap,), t.dtype).at[slot].set(flat_gate[order])
    block_e = jnp.minimum(jnp.searchsorted(pad_end, jnp.arange(n_blocks, dtype=jnp.int32) * EXPERT_BLOCK, side='right'), N_EXPERTS - 1)
    t_pad = jnp.concatenate([t, jnp.zeros((1, d), t.dtype)], axis=0)

    def block_step(acc, blk):
        tok, g, e = blk
        y = swiglu(t_pad[tok], w_gate[e], w_up[e], w_down[e]) * g[:, None]
        return acc.at[tok].add(y), None

    acc, _ = lax.scan(block_step, jnp.zeros((n_tok + 1, d), t.dtype),
                      (slot_tok.reshape(n_blocks, EXPERT_BLOCK), slot_gate.reshape(n_blocks, EXPERT_BLOCK), block_e))
    return acc[:n_tok]

def moe_ffn(t, w_router, e_bias, w_e_gate, w_e_up, w_e_down, w_s_gate, w_s_up, w_s_down):
    scores = jax.nn.sigmoid((t @ w_router).astype(F32))
    _, idx = lax.top_k(scores + e_bias.astype(F32), TOP_K)
    sel = jnp.take_along_axis(scores, idx, axis=-1)
    gate = (ROUTED_SCALE * sel / jnp.sum(sel, -1, keepdims=True)).astype(t.dtype)
    return routed_experts(t, idx, gate, w_e_gate, w_e_up, w_e_down) + swiglu(t, w_s_gate, w_s_up, w_s_down)

def setup_inputs(seed: int = 0) -> dict:
    key = jax.random.key(seed)
    ks = iter(jax.random.split(key, 64))
    D = D_MODEL

    def nrm(shape, std):
        return std * jax.random.normal(next(ks), shape, F32)

    x = nrm((BATCH, SEQ, D), 1.0)
    c = nrm((BATCH, D), 1.0)
    ctx = nrm((BATCH, CTX_LEN, D), 1.0)
    c_ctx = nrm((D,), 1.0)
    w_ada = nrm((DEPTH, D, 6 * D), D ** -0.5)
    b_ada = nrm((DEPTH, 6 * D), 0.02)
    w_in = nrm((DEPTH, D, P_IN), D ** -0.5)
    conv_a = nrm((DEPTH, 3, CONV_CH), 3 ** -0.5)
    hy_sconv_w = nrm((DEPTH, 3, 3 * HY_CH), 3 ** -0.5)
    hy_sconv_b = nrm((DEPTH, 3 * HY_CH), 0.02)
    hf_w1 = nrm((DEPTH, HY_EMB, HY_HID), HY_EMB ** -0.5)
    hf_b1 = nrm((DEPTH, HY_HID), 0.1)
    hf_w2 = nrm((DEPTH, HY_HID, HY_HID), HY_HID ** -0.5)
    hf_b2 = nrm((DEPTH, HY_HID), 0.1)
    hf_w3 = nrm((DEPTH, HY_HID, HY_HID), HY_HID ** -0.5)
    hf_b3 = nrm((DEPTH, HY_HID), 0.1)
    hf_wout = nrm((DEPTH, HY_HID, HY_ORDER * 2 * HY_CH), 0.02)
    hf_freq = 1.0 + nrm((DEPTH, HY_HID), 0.05)
    hf_skip = nrm((DEPTH, HY_ORDER, HY_CH), 1.0)
    rw_mu = jax.random.uniform(next(ks), (DEPTH, 2, RW_COLS), F32, 0.0, 0.4)
    ramp = jnp.linspace(0.0, 1.0, RW_CH, dtype=F32) ** 0.85
    rw_w0 = (-6.5 + 5.0 * ramp)[None, None, :] + nrm((DEPTH, 2, RW_CH), 0.1)
    rw_w_up = nrm((DEPTH, 2, RW_DECAY_RANK, RW_CH), 0.1 * RW_DECAY_RANK ** -0.5)
    rw_a0 = nrm((DEPTH, 2, RW_CH), 0.1)
    rw_a_up = nrm((DEPTH, 2, RW_ICLR_RANK, RW_CH), 0.5 * RW_ICLR_RANK ** -0.5)
    rw_g_up = nrm((DEPTH, RW_GATE_RANK, RW_CH), RW_GATE_RANK ** -0.5)
    rw_k_k = 0.85 + nrm((DEPTH, RW_CH), 0.02)
    rw_k_a = 1.0 + nrm((DEPTH, RW_CH), 0.02)
    rw_r_k = nrm((DEPTH, RW_HEADS, RW_HEAD_DIM), 0.1)
    rw_lnx_g = 1.0 + nrm((DEPTH, RW_CH), 0.02)
    rw_lnx_b = nrm((DEPTH, RW_CH), 0.02)
    mix_norm_g = 1.0 + nrm((DEPTH, CONV_CH + HY_CH), 0.02)
    w_out = nrm((DEPTH, MIX_W, D), DN_BETA * MIX_W ** -0.5)
    ln_g = 1.0 + nrm((DEPTH, 2, D), 0.02)
    ln_b = nrm((DEPTH, 2, D), 0.02)
    w_router = nrm((DEPTH, D, N_EXPERTS), D ** -0.5)
    e_bias = nrm((DEPTH, N_EXPERTS), 0.01)
    w_e_gate = nrm((DEPTH, N_EXPERTS, D, EXPERT_FF), D ** -0.5)
    w_e_up = nrm((DEPTH, N_EXPERTS, D, EXPERT_FF), D ** -0.5)
    w_e_down = nrm((DEPTH, N_EXPERTS, EXPERT_FF, D), DN_BETA * EXPERT_FF ** -0.5)
    w_s_gate = nrm((DEPTH, D, SHARED_FF), D ** -0.5)
    w_s_up = nrm((DEPTH, D, SHARED_FF), D ** -0.5)
    w_s_down = nrm((DEPTH, SHARED_FF, D), DN_BETA * SHARED_FF ** -0.5)
    return {'x': x, 'c': c, 'ctx': ctx, 'c_ctx': c_ctx, 'w_ada': w_ada, 'b_ada': b_ada, 'w_in': w_in,
            'conv_a': conv_a, 'hy_sconv_w': hy_sconv_w, 'hy_sconv_b': hy_sconv_b,
            'hf_w1': hf_w1, 'hf_b1': hf_b1, 'hf_w2': hf_w2, 'hf_b2': hf_b2, 'hf_w3': hf_w3, 'hf_b3': hf_b3,
            'hf_wout': hf_wout, 'hf_freq': hf_freq, 'hf_skip': hf_skip,
            'rw_mu': rw_mu, 'rw_w0': rw_w0, 'rw_w_up': rw_w_up, 'rw_a0': rw_a0, 'rw_a_up': rw_a_up,
            'rw_g_up': rw_g_up, 'rw_k_k': rw_k_k, 'rw_k_a': rw_k_a, 'rw_r_k': rw_r_k,
            'rw_lnx_g': rw_lnx_g, 'rw_lnx_b': rw_lnx_b, 'mix_norm_g': mix_norm_g, 'w_out': w_out,
            'ln_g': ln_g, 'ln_b': ln_b, 'w_router': w_router, 'e_bias': e_bias,
            'w_e_gate': w_e_gate, 'w_e_up': w_e_up, 'w_e_down': w_e_down,
            'w_s_gate': w_s_gate, 'w_s_up': w_s_up, 'w_s_down': w_s_down}

def reference(x, c, ctx, c_ctx, w_ada, b_ada, w_in, conv_a, hy_sconv_w, hy_sconv_b,
              hf_w1, hf_b1, hf_w2, hf_b2, hf_w3, hf_b3, hf_wout, hf_freq, hf_skip,
              rw_mu, rw_w0, rw_w_up, rw_a0, rw_a_up, rw_g_up, rw_k_k, rw_k_a, rw_r_k,
              rw_lnx_g, rw_lnx_b, mix_norm_g, w_out, ln_g, ln_b, w_router, e_bias,
              w_e_gate, w_e_up, w_e_down, w_s_gate, w_s_up, w_s_down):
    B, L, D = x.shape
    xc = ctx
    for l in range(DEPTH):
        last = l == DEPTH - 1
        lp = {'w_in': w_in[l], 'conv_a': conv_a[l], 'hy_sconv_w': hy_sconv_w[l], 'hy_sconv_b': hy_sconv_b[l],
              'hf_w1': hf_w1[l], 'hf_b1': hf_b1[l], 'hf_w2': hf_w2[l], 'hf_b2': hf_b2[l],
              'hf_w3': hf_w3[l], 'hf_b3': hf_b3[l], 'hf_wout': hf_wout[l], 'hf_freq': hf_freq[l],
              'hf_skip': hf_skip[l], 'rw_mu': rw_mu[l], 'rw_w0': rw_w0[l], 'rw_w_up': rw_w_up[l],
              'rw_a0': rw_a0[l], 'rw_a_up': rw_a_up[l], 'rw_g_up': rw_g_up[l], 'rw_k_k': rw_k_k[l],
              'rw_k_a': rw_k_a[l], 'rw_r_k': rw_r_k[l], 'rw_lnx_g': rw_lnx_g[l], 'rw_lnx_b': rw_lnx_b[l],
              'mix_norm_g': mix_norm_g[l], 'w_out': w_out[l]}
        mod_l = jax.nn.silu(c) @ w_ada[l] + b_ada[l]
        mod_c = jax.nn.silu(c_ctx) @ w_ada[l] + b_ada[l]
        sh1, sc1, g1, sh2, sc2, g2 = jnp.split(mod_l[:, None, :], 6, axis=-1)
        csh1, csc1, cg1, csh2, csc2, cg2 = jnp.split(mod_c, 6)
        hl = x * (1.0 + sc1) + sh1
        hc = xc * (1.0 + csc1) + csh1
        ol, oc = token_mixer(hl, hc, lp, not last)
        x = layer_norm(DN_ALPHA * x + g1 * ol, ln_g[l, 0], ln_b[l, 0])
        hl = (x * (1.0 + sc2) + sh2).reshape(B * L, D)
        moe_w = (w_router[l], e_bias[l], w_e_gate[l], w_e_up[l], w_e_down[l], w_s_gate[l], w_s_up[l], w_s_down[l])
        if last:
            fl = moe_ffn(hl, *moe_w)
        else:
            xc = layer_norm(DN_ALPHA * xc + cg1 * oc, ln_g[l, 0], ln_b[l, 0])
            hc = (xc * (1.0 + csc2) + csh2).reshape(-1, D)
            f_all = moe_ffn(jnp.concatenate([hl, hc], axis=0), *moe_w)
            fl = f_all[:B * L]
            xc = layer_norm(DN_ALPHA * xc + cg2 * f_all[B * L:].reshape(xc.shape), ln_g[l, 1], ln_b[l, 1])
        x = layer_norm(DN_ALPHA * x + g2 * fl.reshape(B, L, D), ln_g[l, 1], ln_b[l, 1])
    return x


_drawn_inputs = setup_inputs


def setup_inputs(seed=0):
    import zlib

    import numpy as np

    out = dict(_drawn_inputs(seed))
    spreads = {}
    factors = {'rw_w_up': 4.274,
     'rw_a0': 2.948,
     'rw_lnx_g': 4.118,
     'rw_lnx_b': 4.767,
     'mix_norm_g': 3.061}
    for name, (base, spread) in spreads.items():
        noise = np.random.default_rng([zlib.crc32(name.encode()), seed]).standard_normal(out[name].shape)
        drawn = base * np.exp(spread * noise) if base else spread * noise
        out[name] = __import__('jax').numpy.asarray(drawn.astype(out[name].dtype))
    for name, factor in factors.items():
        out[name] = (out[name] * factor).astype(out[name].dtype)
    return out
```

```python
from contextlib import ExitStack

import math

import numpy as np

import concourse.bass as bass
from concourse import mybir

F32 = mybir.dt.float32
I32 = mybir.dt.int32
U32 = mybir.dt.uint32
ALU = mybir.AluOpType
ACT = mybir.ActivationFunctionType
AX_X = mybir.AxisListType.X

P = 128
D = 1024
KD = D // P
L = 1024
LC = 256
T = L + LC
NT = L // P
GRID = 64
NE = 64
TOPK = 8
FF = 256
NBLK = NE + L * TOPK // P - 1
HD = 64
NH = 8
RC = NH * HD
CH = 256
UW = 6 * CH + 3 * RC
PADR = GRID
ALPHA = 2.0 ** 0.25
LN_EPS = 1e-5
GN_EPS = 64e-5
ROUTED = 2.5
C = 64
LD = -math.exp(-0.5)
TWO_PI = 2.0 * math.pi
MAGIC = 1.5 * 2.0 ** 23


class Mem:

    def __init__(self, nc, ctx, tag):
        self.nc, self.ctx, self.tag = nc, ctx, tag

    def sb(self, name, shape, dt=F32):
        return self.ctx.enter_context(self.nc.sbuf_tensor(f"{self.tag}_{name}", shape, dt))

    def ps(self, name, cols=512):
        return self.ctx.enter_context(self.nc.psum_tensor(f"{self.tag}_{name}", [P, cols], F32))


class Count:

    def __init__(self, sem):
        self.sem, self.n = sem, 0

    def inc(self, ins, by=1):
        ins.then_inc(self.sem, by)
        self.n += by
        return self.n


def bc(ap, at, n):
    shape = list(ap.shape)
    u = ap.unsqueeze(at)
    return u.broadcast_to(shape[:at] + [n] + shape[at:])


def modulate(nc, sems, io, per):
    with ExitStack() as ctx:
        m = Mem(nc, ctx, "mod")
        NG = 12
        cc = m.sb("cc", [P, KD, 2])
        sg = m.sb("sg", [P, KD, 2])
        sc = m.sb("sc", [P, KD, 2])
        scb = m.sb("scb", [P, KD, P])
        bcol = m.sb("bcol", [P, 16])
        w = [m.sb(f"w{s}", [P, KD, 512]) for s in range(2)]
        cps = m.ps("cps")
        rps = [m.ps(f"rps{s}") for s in range(2)]
        c_in, w_in, acted, prepared, dve_did = (sems(x) for x in ("c_in", "w_in0", "acted", "prepared", "dve_did"))
        w_in = [w_in, sems("w_in1")]
        used = sems("ada_used")
        b_in = sems("b_in")
        block = ctx.enter_context(nc.Block())

        @block.sync
        def _(sp):
            sp.dma_start(cc[:], io["c_cols"]).then_inc(c_in, 16)
            for g in range(NG):
                if g >= 2:
                    sp.wait_ge(used, g - 1)
                sp.dma_start(w[g % 2][:], io["w_ada"][:, g * 512:(g + 1) * 512]
                             .rearrange("(k p) n -> p k n", p=P)).then_inc(w_in[g % 2], 16)

        @block.scalar
        def _(act):
            act.dma_start(bcol[:], io["b_cols"]).then_inc(b_in, 16)
            act.dma_start(per["rows"][:], io["b_rows"].partition_broadcast(P)).then_inc(b_in, 16)
            act.wait_ge(c_in, 16)
            act.activation(sg[:], cc[:], ACT.Sigmoid).then_inc(acted, 1)

        @block.vector
        def _(dve):
            dve.wait_ge(acted, 1)
            dve.tensor_tensor(sc[:], cc[:], sg[:], ALU.mult).then_inc(dve_did, 1)
            dve.wait_ge(dve_did, 1)
            dve.tensor_copy(scb[:], bc(sc[:, :, 0], 2, P)).then_inc(prepared, 1)
            dve.wait_ge(used, 4)
            dve.wait_ge(b_in, 32)
            dve.tensor_tensor(per["cols"][:], cps[:, 0:32].rearrange("p (m s) -> p m s", s=2),
                              bc(bcol[:], 2, 2), ALU.add).then_inc(dve_did, 1)
            dve.wait_ge(dve_did, 2)
            dve.tensor_scalar(per["cols"][:, 8:16, :], per["cols"][:, 8:16, :], 1.0, None, ALU.add)
            for g in range(4, NG):
                dve.wait_ge(used, g + 1)
                rows = per["rows"][:, (g - 4) * 512:(g - 3) * 512]
                dve.tensor_tensor(rows, rows, rps[g % 2][:], ALU.add).then_inc(dve_did, 1)
            dve.wait_ge(dve_did, 2 + NG - 4)
            dve.tensor_scalar(per["rows"][:, 2048:3072], per["rows"][:, 2048:3072], 1.0, None, ALU.add)

        @block.tensor
        def _(pe):
            pe.wait_ge(prepared, 1)
            for g in range(NG):
                pe.wait_ge(w_in[g % 2], 16 * (g // 2 + 1))
                if g < 4:
                    for q in range(4):
                        for k in range(KD):
                            mm = pe.matmul(cps[:, 2 * (4 * g + q):2 * (4 * g + q) + 2], w[g % 2][:, k, q * P:(q + 1) * P],
                                           sc[:, k, :], start=(k == 0), stop=(k == KD - 1))
                else:
                    if g >= 6:
                        pe.wait_ge(dve_did, 2 + g - 5)
                    for k in range(KD):
                        mm = pe.matmul(rps[g % 2][:], scb[:, k, :], w[g % 2][:, k, :],
                                       start=(k == 0), stop=(k == KD - 1))
                mm.then_inc(used, 1)


def project(nc, sems, io, per):
    with ExitStack() as ctx:
        m = Mem(nc, ctx, "prj")
        hT = m.sb("hT", [P, KD, T])
        w = [m.sb(f"w{s}", [P, KD, P]) for s in range(2)]
        coef = m.sb("coef", [P, 27, 4])
        uw = T + 3
        ub = [m.sb(f"ub{s}", [P, uw]) for s in range(2)]
        cv = [m.sb(f"cv{s}", [P, T]) for s in range(2)]
        ut = [m.sb(f"ut{s}", [P, 10, P]) for s in range(2)]
        zero = m.sb("zero", [GRID, 2 * CH])
        acc = [m.ps(f"acc{s}", 3 * 512) for s in range(2)]
        tp = [m.ps(f"tp{s}") for s in range(2)]
        x_in, coef_in, h_done, coef_done, zeroed, z_out = (
            sems(x) for x in ("x_in", "coef_in", "h_done", "coef_done", "zeroed", "z_out"))
        w_in, summed, copied, convolved, turned, stored = (
            [sems(f"{x}{s}") for s in range(2)] for x in ("pw_in", "summed", "copied", "convolved", "turned", "stored"))
        tp_full = sems("tp_full")
        tp_free = sems("tp_free")
        step = sems("conv_step")
        block = ctx.enter_context(nc.Block())
        LAT = [(LC + 512 * n, 512) for n in range(2)]
        TILES_LAT, TILES = 16, 24

        def parts(ctx_too):
            return ([(0, LC)] if ctx_too else []) + LAT

        def groups(ctx_too):
            return ([(0, 2)] if ctx_too else []) + [(2, 6), (6, 10)]

        def gbase(j, s, ctx_too):
            return 3 * (2 * j + s) - TILES_LAT if ctx_too else 2 * (2 * j + s)

        LOOPS = [(0, TILES_LAT // 2, False), (TILES_LAT // 2, TILES // 2, True)]

        @block.sync
        def _(sp):
            for k in range(KD):
                sp.dma_start(hT[:, k, :], io["hT"][:, k, :]).then_inc(x_in, 16)
            for lo, hi, ctx_too in LOOPS:
                with sp.Fori(lo, hi) as j:
                    for s in range(2):
                        sp.wait_ge(summed[s], j + 1)
                        sp.dma_start(w[s][:], io["w_in"][bass.ds(2 * j + s, 1)].rearrange("o p k n -> p (o k) n")
                                     ).then_inc(w_in[s], 16)
            for n in range(3):
                s = n % 2
                sp.wait_ge(summed[s], 12 + n // 2 + 1)
                sp.dma_start(w[s][:], io["w_in"][24 + n]).then_inc(w_in[s], 16)

        @block.tensor
        def _(pe):
            for s in range(2):
                pe.sem_inc(summed[s], 1)
                pe.sem_inc(turned[s], 1)
            pe.wait_ge(h_done, KD)

            def sums(s, j, ctx_too):
                pe.wait_ge(w_in[s], 16 * (j + 1))
                pe.wait_ge(copied[s], j + 1)
                for n, (t0, tn) in enumerate(parts(ctx_too)):
                    b = 512 * (n if ctx_too else n + 1)
                    for k in range(KD):
                        mm = pe.matmul(acc[s][:, b:b + tn], w[s][:, k, :], hT[:, k, t0:t0 + tn],
                                       start=(k == 0), stop=(k == KD - 1))
                mm.then_inc(summed[s], 1)

            def turns(s, j, ctx_too):
                pe.wait_ge(convolved[s], j + 2)
                for q, (a, b) in enumerate(groups(ctx_too)):
                    g = gbase(j, s, ctx_too) + q
                    pe.wait_ge(tp_free, g + 1)
                    bank = tp[(q + (s if ctx_too else 0)) % 2]
                    for t in range(a, b):
                        mm = pe.transpose(bank[:, (t - a) * P:(t - a + 1) * P], cv[s][:, t * P:(t + 1) * P],
                                          per["ident"][:])
                    mm.then_inc(tp_full, 1)
                pe.wait_ge(tp_full, gbase(j, s, ctx_too) + len(groups(ctx_too)))
                pe.sem_inc(turned[s], 1)

            for lo, hi, ctx_too in LOOPS:
                with pe.Fori(lo, hi) as j:
                    for s in range(2):
                        sums(s, j, ctx_too)
                    for s in range(2):
                        turns(s, j, ctx_too)
            for n, ctx_too in ((0, True), (1, True), (2, False)):
                sums(n % 2, 12 + n // 2, ctx_too)

        @block.scalar
        def _(act):
            act.dma_start(coef[:], io["coef"]).then_inc(coef_in, 16)
            for s in range(2):
                act.sem_inc(copied[s], 1)
            act.sem_inc(tp_free, 2)
            for s in range(2):
                act.sem_inc(stored[s], 16)

            def copy(s, j, ctx_too):
                act.wait_ge(summed[s], j + 2)
                act.wait_ge(convolved[s], j + 1)
                if ctx_too:
                    act.copy(ub[s][:, 1:1 + LC], acc[s][:, 0:LC])
                act.copy(ub[s][:, 2 + LC:2 + LC + L], acc[s][:, 512:512 + L]).then_inc(copied[s], 1)

            def out(s, j, ctx_too):
                a0 = groups(ctx_too)[0][0]
                act.wait_ge(stored[s], 16 * (j + 1))
                for q, (a, b) in enumerate(groups(ctx_too)):
                    g = gbase(j, s, ctx_too) + q
                    act.wait_ge(tp_full, g + 1)
                    act.copy(ut[s][:, a:b, :], tp[(q + (s if ctx_too else 0)) % 2][:, 0:(b - a) * P]
                             .rearrange("p (t c) -> p t c", c=P)).then_inc(tp_free, 1)
                act.wait_ge(tp_free, gbase(j, s, ctx_too) + len(groups(ctx_too)) + 2)
                act.dma_start(io["u"][a0 * P:T, bass.ds((2 * j + s) * P, P)].rearrange("(t p) c -> p t c", p=P),
                              ut[s][:, a0:10, :]).then_inc(stored[s], 16)

            for lo, hi, ctx_too in LOOPS:
                with act.Fori(lo, hi) as j:
                    for s in range(2):
                        copy(s, j, ctx_too)
                    for s in range(2):
                        out(s, j, ctx_too)
            for n, ctx_too in ((0, True), (1, True), (2, False)):
                copy(n % 2, 12 + n // 2, ctx_too)
            for s in range(2):
                act.wait_ge(stored[s], 16 * 13)

        @block.vector
        def _(dve):
            for s in range(2):
                dve.memset(ub[s][:], 0.0)
            dve.memset(zero[:], 0.0).then_inc(zeroed, 1)
            for k in range(KD):
                dve.wait_ge(x_in, 16 * KD)
                for a, b, which in ((0, LC, 1), (LC, T, 0)):
                    ins = dve.tensor_scalar(hT[:, k, a:b], hT[:, k, a:b], per["cols"][:, 8 + k, which:which + 1],
                                            per["cols"][:, k, which:which + 1], ALU.mult, ALU.add)
                ins.then_inc(h_done, 1)
            dve.wait_ge(coef_in, 16)
            dve.tensor_tensor(coef[:, 12:27, 1], coef[:, 12:27, 1], coef[:, 12:27, 0], ALU.subtract).then_inc(coef_done, 1)
            dve.wait_ge(coef_done, 1)
            dve.tensor_tensor(coef[:, 12:27, 1], coef[:, 12:27, 1], coef[:, 12:27, 2], ALU.subtract).then_inc(coef_done, 1)
            dve.wait_ge(coef_done, 2)
            for s in range(2):
                dve.sem_inc(convolved[s], 1)

            cf = m_coef = per["coef_now"]

            def conv(s, j, ctx_too, tile, n_step, out=None):
                dve.wait_ge(copied[s], j + 2)
                if out is None:
                    dve.wait_ge(turned[s], j + 1)
                    out = cv[s]
                dve.tensor_copy(cf[:], coef[:, bass.ds(tile, 1), :].rearrange("p o c -> p (o c)")).then_inc(step, 1)
                dve.wait_ge(step, n_step + 1)
                spans = ([(0, LC, 1)] if ctx_too else []) + [(LC, T, 2)]
                for a, b, sh in spans:
                    ins = dve.tensor_scalar(out[:, a:b], ub[s][:, a + sh:b + sh], cf[:, 1:2], cf[:, 3:4],
                                            ALU.mult, ALU.add)
                ins.then_inc(step, 1)
                dve.wait_ge(step, n_step + 2)
                for a, b, sh in spans:
                    ins = dve.scalar_tensor_tensor(out[:, a:b], ub[s][:, a + sh - 1:b + sh - 1], cf[:, 0:1], out[:, a:b],
                                                   ALU.mult, ALU.add)
                ins.then_inc(step, 1)
                dve.wait_ge(step, n_step + 3)
                for a, b, sh in spans:
                    ins = dve.scalar_tensor_tensor(out[:, a:b], ub[s][:, a + sh + 1:b + sh + 1], cf[:, 2:3], out[:, a:b],
                                                   ALU.mult, ALU.add)
                ins.then_inc(step, 1)
                dve.wait_ge(step, n_step + 4)
                dve.sem_inc(convolved[s], 1)

            for lo, hi, ctx_too in LOOPS:
                with dve.Fori(lo, hi) as j:
                    for s in range(2):
                        conv(s, j, ctx_too, 2 * j + s, 8 * j + 4 * s)
            for n, ctx_too in ((0, True), (1, True), (2, False)):
                conv(n % 2, 12 + n // 2, ctx_too, 24 + n, 4 * (24 + n), per[("wd", "ad", "gd")[n]])

        @block.gpsimd
        def _(pool):
            pool.wait_ge(zeroed, 1)
            pool.dma_start(io["u"][LC - GRID:LC, CH:3 * CH], zero[:]).then_inc(z_out, 16)
            pool.dma_start(io["u"][T:T + PADR, CH:3 * CH], zero[:]).then_inc(z_out, 16)
            pool.wait_ge(z_out, 32)


def hyena(nc, sems, io, per):
    with ExitStack() as ctx:
        m = Mem(nc, ctx, "hy")
        NF = 2 * CH
        z = m.sb("z", [P, NT, CH])
        x12 = m.sb("x12", [P, 2, NT, CH])
        K = m.sb("K", [P, NT, 2, 3, CH])
        tmp = m.sb("tmp", [P, 2, 2, CH])
        skip = m.sb("skip", [P, 2, CH])
        work = m.sb("work", [P, 2, CH])
        banks = [m.ps(f"bank{s}") for s in range(6)]
        v_in, fil_in, pos_in, wout_in, skip_in = (sems(x) for x in ("v_in", "fil_in", "pos_in", "wout_in", "skip_in"))
        dft_in = [sems(f"dft_in{s}") for s in range(2)]
        x_in = sems("x12_in")
        y_out = sems("yh_out")

        with ExitStack() as ctx1:
            m1 = Mem(nc, ctx1, "hf")
            pos = m1.sb("pos", [33, L])
            w1 = m1.sb("w1", [33, 64])
            w23 = m1.sb("w23", [64, 2, 64])
            hb = m1.sb("hb", [64, 4])
            wout = m1.sb("wout", [64, 4 * CH])
            win = m1.sb("win", [P, NT, NF])
            h = [m1.sb(f"h{s}", [64, L]) for s in range(2)]
            q = m1.sb("q", [64, L])
            hw = m1.sb("hw", [P, 2, NF])
            both = m1.sb("both", [P, NT, 2, NF])
            fil = [m1.sb(f"fil{s}", [P, 2, NT, P]) for s in range(2)]
            lin, mapped, stp, out_done, windowed, added, kdone, ktaken = (
                sems(x) for x in ("lin", "mapped", "step", "out_done", "windowed", "added", "kdone", "ktaken"))
            block = ctx1.enter_context(nc.Block())

            @block.sync
            def _(sp):
                for dst, src in ((pos[:], io["posT"]), (w1[:], io["hf_w1"]), (w23[:, 0, :], io["hf_w2"]),
                                 (w23[:, 1, :], io["hf_w3"]), (hb[:], io["hf_b"])):
                    sp.dma_start(dst, src).then_inc(pos_in, 16)
                sp.dma_start(wout[:], io["hf_wout"]).then_inc(wout_in, 16)
                sp.dma_start(win[:], io["window"]).then_inc(wout_in, 16)
                for f in range(NT):
                    if f >= 2:
                        sp.wait_ge(kdone, f - 1)
                    sp.dma_start(fil[f % 2][:, 0], io["fil_cos"][f]).then_inc(dft_in[f % 2], 16)
                    sp.dma_start(fil[f % 2][:, 1], io["fil_sin"][f]).then_inc(dft_in[f % 2], 16)

            @block.tensor
            def _(pe):
                pe.wait_ge(pos_in, 80)
                for layer in range(3):
                    if layer:
                        pe.wait_ge(mapped, layer)
                    for n in range(2):
                        lhsT = w1[:] if layer == 0 else w23[:, layer - 1, :]
                        rhs = pos[:, n * 512:(n + 1) * 512] if layer == 0 else h[(layer - 1) % 2][:, n * 512:(n + 1) * 512]
                        mm = pe.matmul(banks[n][0:64, :], lhsT, rhs, start=True, stop=True)
                    mm.then_inc(lin, 1)
                pe.wait_ge(mapped, 3)
                pe.wait_ge(wout_in, 32)
                for t in range(NT):
                    for o in range(2):
                        n = 2 * t + o
                        if n >= 2:
                            pe.wait_ge(windowed, n - 1)
                        pe.matmul(banks[2 + n % 2][:], h[0][:, t * P:(t + 1) * P], wout[:, o * NF:(o + 1) * NF],
                                  start=True, stop=True).then_inc(out_done, 1)
                pe.wait_ge(added, 4 * NT)
                for f in range(NT):
                    pe.wait_ge(dft_in[f % 2], 32 * (f // 2 + 1))
                    if f >= 2:
                        pe.wait_ge(ktaken, 3 * (f - 1))
                    for part in range(2):
                        for t in range(NT):
                            mm = pe.matmul(banks[2 * (f % 2) + part][:], fil[f % 2][:, part, t, :], both[:, t, part, :],
                                           start=(t == 0), stop=(t == NT - 1))
                    mm.then_inc(kdone, 1)

            @block.vector
            def _(dve):
                st = Count(stp)
                for layer in range(3):
                    dve.wait_ge(lin, layer + 1)
                    src = banks
                    dst = h[layer % 2]
                    for n in range(2):
                        v = st.inc(dve.tensor_scalar(dst[:, n * 512:(n + 1) * 512], src[n][0:64, :], hb[:, layer:layer + 1],
                                                     hb[:, 3:4], ALU.add, ALU.mult))
                    dve.wait_ge(stp, v)
                    dve.wait_ge(stp, st.inc(dve.tensor_scalar(q[:], dst[:], 1.0 / TWO_PI, MAGIC, ALU.mult, ALU.add)))
                    dve.wait_ge(stp, st.inc(dve.tensor_scalar(q[:], q[:], MAGIC, None, ALU.subtract)))
                    dve.wait_ge(stp, st.inc(dve.scalar_tensor_tensor(dst[:], q[:], -6.28125, dst[:], ALU.mult, ALU.add)))
                    dve.wait_ge(stp, st.inc(dve.scalar_tensor_tensor(dst[:], q[:], -(TWO_PI - 6.28125), dst[:], ALU.mult, ALU.add)))
                    st.inc(dve.tensor_scalar(dst[:], dst[:], 3.1415925, -3.1415925, ALU.min, ALU.max))
                dve.wait_ge(wout_in, 32)
                for t in range(NT):
                    for o in range(2):
                        n = 2 * t + o
                        dve.wait_ge(out_done, n + 1)
                        if n >= 2:
                            dve.wait_ge(added, 2 * (n - 1))
                        dve.tensor_tensor(hw[:, n % 2, :], banks[2 + n % 2][:], win[:, t, :], ALU.mult).then_inc(windowed, 1)
                        dve.wait_ge(windowed, n + 1)
                        for part, op in ((0, ALU.add), (1, ALU.subtract)):
                            dve.tensor_tensor(both[:, t, part, o * CH:(o + 1) * CH], hw[:, n % 2, 0:CH], hw[:, n % 2, CH:NF],
                                              op).then_inc(added, 1)

            @block.scalar
            def _(act):
                act.dma_start(z[:], io["u"][LC:T, 3 * CH:4 * CH].rearrange("(t p) c -> p t c", p=P)).then_inc(v_in, 16)
                for o in range(2):
                    act.dma_start(x12[:, o], io["u"][LC:T, (4 + o) * CH:(5 + o) * CH].rearrange("(t p) c -> p t c", p=P)
                                  ).then_inc(x_in, 16)
                act.dma_start(skip[:].rearrange("p o c -> p (o c)"), io["hf_skip"].partition_broadcast(P)).then_inc(skip_in, 16)
                for layer in range(3):
                    act.wait_ge(stp, 7 * layer + 7)
                    act.activation(h[layer % 2][:], h[layer % 2][:], ACT.Sin).then_inc(mapped, 1)
                for f in range(NT):
                    act.wait_ge(kdone, f + 1)
                    for part, kinds in ((0, (0, 2)), (1, (1,))):
                        for kind in kinds:
                            act.copy(K[:, f, :, kind, :], banks[2 * (f % 2) + part][:].rearrange("p (o c) -> p o c", o=2)
                                     ).then_inc(ktaken, 1)
                act.wait_ge(v_in, 16)
                act.wait_ge(x_in, 32)
                act.wait_ge(skip_in, 16)
                act.wait_ge(ktaken, 3 * NT)

        with ExitStack() as ctx2:
            m2 = Mem(nc, ctx2, "hc")
            E = m2.sb("E", [P, NT, CH])
            F = m2.sb("F", [P, NT, CH])
            M = [m2.sb("cos", [P, NT, L]), m2.sb("sin", [P, NT, L])]
            fwd, mixed, inv, gated, stp = (sems(x) for x in ("fwd", "mixed", "inv", "gated", "cstep"))
            tab_in = sems("tab_in")
            block = ctx2.enter_context(nc.Block())

            @block.sync
            def _(sp):
                for t in range(NT):
                    sp.dma_start(M[0][:, t], io["dft_cos"][:, t]).then_inc(tab_in, 16)
                    sp.dma_start(M[1][:, t], io["dft_sin"][:, t]).then_inc(tab_in, 16)
                sp.wait_ge(gated, 2 * NT)
                sp.dma_start(io["yh"].rearrange("(t p) c -> p t c", p=P), z[:]).then_inc(y_out, 16)
                sp.wait_ge(y_out, 16)

            @block.tensor
            def _(pe):
                pe.wait_ge(tab_in, 32 * NT)
                for o in range(2):
                    if o:
                        pe.wait_ge(gated, NT)
                    for f in range(NT):
                        n = NT * o + f
                        if n >= 2:
                            pe.wait_ge(mixed, n - 1)
                        for part in range(2):
                            for t in range(NT):
                                mm = pe.matmul(banks[n % 2][:, part * CH:(part + 1) * CH], M[part][:, t, f * P:(f + 1) * P],
                                               z[:, t, :], start=(t == 0), stop=(t == NT - 1))
                        mm.then_inc(fwd, 1)
                    pe.wait_ge(mixed, NT * (o + 1))
                    for t in range(NT):
                        n = NT * o + t
                        if n >= 2:
                            pe.wait_ge(gated, n - 1)
                        for f in range(NT):
                            for part, src in ((0, E), (1, F)):
                                mm = pe.matmul(banks[2 + n % 2][:, 0:CH], M[part][:, f, t * P:(t + 1) * P], src[:, f, :],
                                               start=(f == 0 and part == 0), stop=(f == NT - 1 and part == 1))
                        mm.then_inc(inv, 1)

            @block.vector
            def _(dve):
                st = Count(stp)
                for o in range(2):
                    for f in range(NT):
                        n = NT * o + f
                        dve.wait_ge(fwd, n + 1)
                        pq = banks[n % 2][:].rearrange("p (a c) -> p a c", a=2)
                        st.inc(dve.tensor_tensor(tmp[:, 0], pq, K[:, f, o, 0:2, :], ALU.mult))
                        v = st.inc(dve.tensor_tensor(tmp[:, 1], pq, K[:, f, o, 1:3, :], ALU.mult))
                        dve.wait_ge(stp, v)
                        st.inc(dve.tensor_tensor(E[:, f, :], tmp[:, 0, 0, :], tmp[:, 0, 1, :], ALU.add))
                        dve.tensor_tensor(F[:, f, :], tmp[:, 1, 1, :], tmp[:, 1, 0, :], ALU.subtract).then_inc(mixed, 1)
                        dve.wait_ge(mixed, n + 1)
                        dve.wait_ge(stp, st.n)
                    for t in range(NT):
                        n = NT * o + t
                        v = st.inc(dve.tensor_tensor(work[:, 0], z[:, t, :], skip[:, o, :], ALU.mult))
                        dve.wait_ge(inv, n + 1)
                        dve.wait_ge(stp, v)
                        dve.wait_ge(stp, st.inc(dve.tensor_tensor(work[:, 1], work[:, 0], banks[2 + n % 2][:, 0:CH], ALU.add)))
                        dve.tensor_tensor(z[:, t, :], work[:, 1], x12[:, o, t, :], ALU.mult).then_inc(gated, 1)
                        dve.wait_ge(gated, n + 1)


NSTEP = T // C


def scan(nc, sems, io, per):
    with ExitStack() as ctx:
        m = Mem(nc, ctx, "sc")
        H2 = NH // 2
        lora = m.sb("lora", [P, NSTEP, 2, C])
        lnow = m.sb("lnow", [P, 2, C])
        w_up = m.sb("w_up", [P, RC])
        a_up = m.sb("a_up", [P, RC])
        wa0 = m.sb("wa0", [P, 2, RC])
        rows = m.sb("rows", [P, 3, RC])
        tri = m.sb("tri", [P, 2, C])
        tot = m.sb("tot", [P, 1])
        causal = m.sb("causal", [P, 2, C])
        level = m.sb("level", [P, 7, C])
        eye = m.sb("eye", [P, C])
        rkv = [m.sb(f"rkv{s}", [P, 3, RC]) for s in range(2)]
        pre = m.sb("pre", [P, 2, RC])
        sig = m.sb("sig", [P, 2, RC])
        e_in, e_ng, e_ex = (m.sb(x, [P, RC]) for x in ("e_in", "e_ng", "e_ex"))
        kkr, sq, kk, kka, krest, rrk, akk, kd, bon = (
            m.sb(x, [P, RC]) for x in ("kkr", "sq", "kk", "kka", "krest", "rrk", "akk", "kd", "bon"))
        ss, rn = m.sb("ss", [P, NH]), m.sb("rn", [P, NH])
        alpha, rho = m.sb("alpha", [P, RC]), m.sb("rho", [P, RC])
        beta = [m.sb(f"beta{s}", [P, RC]) for s in range(2)]
        kap = [m.sb(f"kap{s}", [P, RC]) for s in range(2)]
        arT = [m.sb(f"arT{s}", [P, NH, 2, C]) for s in range(2)]
        bT = [m.sb(f"bT{s}", [P, NH, C]) for s in range(2)]
        kT = [m.sb(f"kT{s}", [P, NH, C]) for s in range(2)]
        dec = [m.sb(f"dec{s}", [P, NH]) for s in range(2)]
        ab = m.sb("ab", [P, NH, 2, C])
        ak = m.sb("ak", [P, NH, 2, C])
        abi = m.sb("abi", [P, NH, C])
        dd = m.sb("dd", [P, 2, 2, H2 * C])
        xm = m.sb("xm", [P, 2, H2 * C])
        gs = m.sb("gs", [P, RC])
        us = m.sb("us", [P, RC])
        st = m.sb("st", [P, RC])
        sm = m.sb("sm", [P, RC])
        yb = [m.sb(f"yb{s}", [P, RC + NH]) for s in range(2)]
        B = [m.ps(f"B{n}") for n in range(8)]

        con_in, rkv_in0, rkv_in1 = sems("con_in"), sems("rkv_in0"), sems("rkv_in1")
        rkv_in = [rkv_in0, rkv_in1]
        names = ("lora_ready lora_now lora_sum pre_done sig_done cum_done exp_done raw_k pool_k sqd ssd clamped rooted rnd kk_done akk_done "
                 "kd_done kd_part op_done turned_up tev_a tev_d a_sum a_masked abi_done adir d_step d0 dt0 z_sum x_done d_sum "
                 "d_copied g_sum g_copied u_sum u_copied s_sum s_added s_done y_sum y_copied bon_m bon_done zeroed0 passed passed_sp")
        q = {x: sems(x) for x in names.split()}
        y_out = [sems(f"y_out{s}") for s in range(2)]
        block = ctx.enter_context(nc.Block())
        K = (slice(0, 64), slice(64, 128))

        def wait(eng, name, c, per_step, k):
            v = c * per_step + k
            if not (isinstance(v, int) and v <= 0):
                eng.wait_ge(q[name], v)
                if eng is nc.tensor and not isinstance(v, int):
                    eng.sem_inc(q["passed"], 1)

        def hd(h):
            return slice(h * C, (h + 1) * C)

        def half(ap, g):
            return ap[:, g * H2 * C:(g + 1) * H2 * C]

        @block.sync
        def _(sp):
            for dst, src in ((w_up[:], io["w_up"]), (a_up[:], io["a_up"]), (wa0[:, 0], io["w0"]), (wa0[:, 1], io["a0"]),
                             (rows[:].rearrange("p a c -> p (a c)"), io["rw_rows"].partition_broadcast(P)),
                             (tri[:], io["tri"]), (tot[:], io["tot"]), (causal[:], io["causal"]), (level[:], io["level"]),
                             (eye[:], io["eye2"])):
                sp.dma_start(dst, src).then_inc(con_in, 16)

            R0 = 6 * CH

            def load(c, s, t_back, context):
                wait(sp, "s_sum", c - 2, 2, 2)
                wait(sp, "y_sum", c - 2, 2, 2)
                wait(sp, "bon_done", c - 2, 1, 1)
                sp.sem_inc(q["passed_sp"], 1)
                for d, t in ((0, c * C), (1, t_back)):
                    src = io["u"][bass.ds(t, C)]
                    sp.dma_start(rkv[s][K[d], 1:3, :], src[:, R0 + RC:R0 + 3 * RC].rearrange("t (a c) -> t a c", a=2)
                                 ).then_inc(rkv_in[s], 16)
                    r = src[:, R0 + RC:R0 + 2 * RC] if context else src[:, R0:R0 + RC]
                    sp.dma_start(rkv[s][K[d], 0, :], r).then_inc(rkv_in[s], 16)

            def store(c, s, t_back):
                sp.wait_ge(q["y_copied"], 2 * c + 2)
                sp.sem_inc(q["passed_sp"], 1)
                sp.wait_ge(q["bon_done"], c + 1)
                sp.sem_inc(q["passed_sp"], 1)
                sp.dma_start(io["ys0"][bass.ds(c * C - LC, C)], yb[s][K[0], :]).then_inc(y_out[s], 16)
                sp.dma_start(io["ys1"][bass.ds(t_back - LC, C)], yb[s][K[1], :]).then_inc(y_out[s], 16)

            NC = LC // C
            for c in range(NC):
                load(c, c % 2, LC - C * (c + 1), True)
            for c in range(NC, NC + 2):
                load(c, c % 2, T + LC - C * (c + 1), False)
            with sp.Fori(NC // 2, NSTEP // 2 - 1) as j:
                for s in range(2):
                    store(2 * j + s, s, T + LC - C - C * (2 * j + s))
                    load(2 * j + s + 2, s, T + LC - C - C * (2 * j + s + 2), False)
            for c in range(NSTEP - 2, NSTEP):
                store(c, c % 2, T + LC - C * (c + 1))
            for s in range(2):
                sp.wait_ge(y_out[s], 16 * (NSTEP - NC))

        def steps(eng, prepare_alone, both, recur_alone):
            prepare_alone(0, 0)
            for c in range(2):
                both(c, c % 2)
            with eng.Fori(1, NSTEP // 2 - 1) as j:
                for s in range(2):
                    both(2 * j + s, s)
            both(NSTEP - 2, 0)
            recur_alone(NSTEP - 1, 1)

        @block.tensor
        def _(pe):
            pe.wait_ge(con_in, 160)
            ident = per["ident"]

            def p_lora(c, s):
                wait(pe, "lora_now", c, 1, 1)
                wait(pe, "tev_a", c - 1, 8, 8)
                wait(pe, "tev_d", c - 1, 8, 8)
                for i, up in ((0, w_up), (1, a_up)):
                    for d in range(2):
                        mm = pe.matmul(B[i][K[d], :], lnow[K[d], i, :], up[K[d], :], start=True, stop=True)
                mm.then_inc(q["lora_sum"], 1)

            def p_cum(c, s):
                wait(pe, "sig_done", c, 1, 1)
                for i in range(2):
                    for d in range(2):
                        mm = pe.matmul(B[2 + i][K[d], :], tri[K[d], i, :], sig[K[d], 0, :], start=True, stop=True)
                for h in range(NH):
                    for d in range(2):
                        mm = pe.matmul(B[0][K[d], h:h + 1], sig[K[d], 0, hd(h)], tot[K[d], :], start=True, stop=True)
                mm.then_inc(q["cum_done"], 1)

            def p_turn(c, s):
                wait(pe, "exp_done", c, 4, 4)
                for n, (src, bank) in enumerate(((alpha, 1), (beta[s], 3), (kap[s], 0), (rho, 2))):
                    wait(pe, "op_done", c, 4, n + 1)
                    for p in range(4):
                        mm = pe.transpose(B[bank][:, p * P:(p + 1) * P], src[:, p * P:(p + 1) * P], ident[:])
                    mm.then_inc(q["turned_up"], 1)

            def r_products(c, s):
                wait(pe, "tev_a", c, 8, 8)
                wait(pe, "tev_d", c, 8, 8)
                wait(pe, "s_added", c - 1, 2, 2)
                wait(pe, "y_copied", c - 1, 2, 2)
                for n, (lhs, g) in enumerate(((bT[s], 0), (bT[s], 1), (kT[s], 0), (kT[s], 1))):
                    for hh in range(H2):
                        for d in range(2):
                            h = g * H2 + hh
                            mm = pe.matmul(B[4 + n][K[d], hh * P:(hh + 1) * P], lhs[K[d], h, :],
                                           arT[s][K[d], h].rearrange("k a t -> k (a t)"), start=True, stop=True)
                    mm.then_inc(q["a_sum"], 1)

            def r_direct(c, s):
                for g in range(2):
                    wait(pe, "a_masked", c, 4, g + 1)
                    for hh in range(H2):
                        for d in range(2):
                            h = g * H2 + hh
                            mm = pe.matmul(B[4 + g][K[d], hd(hh)], arT[s][K[d], h, 0, :], bT[s][K[d], h, :], start=True, stop=True)
                    mm.then_inc(q["adir"], 1)

            def r_level(c, s, l):
                for g in range(2):
                    if l == 1:
                        wait(pe, "d0", c, 2, g + 1)
                        wait(pe, "dt0", c, 2, g + 1)
                        wait(pe, "abi_done", c, 1, 1)
                    else:
                        wait(pe, "d_copied", c, 10, 2 * (l - 2) + g + 1)
                    for hh in range(H2):
                        for d in range(2):
                            h = g * H2 + hh
                            mm = pe.matmul(B[4 + g][K[d], hd(hh)], abi[K[d], h, :], dd[K[d], g, 0, hd(hh)], start=True, stop=True)
                    mm.then_inc(q["z_sum"], 1)
                for g in range(2):
                    wait(pe, "x_done", c, 10, 2 * (l - 1) + g + 1)
                    if l == 1:
                        wait(pe, "a_masked", c, 4, 3 + g)
                    for hh in range(H2):
                        for d in range(2):
                            if l < 5:
                                pe.matmul(B[6 + g][K[d], hd(hh)], dd[K[d], g, 1, hd(hh)], xm[K[d], g, hd(hh)], start=True, stop=True)
                            mm = pe.matmul(B[6 + g][K[d], hd(H2 + hh)], xm[K[d], g, hd(hh)], dd[K[d], g, 1, hd(hh)], start=True, stop=True)
                    mm.then_inc(q["d_sum"], 1)

            def r_state(c, s):
                V = rkv[s][:, 2, :]
                wait(pe, "s_done", c - 1, 2, 2)
                if isinstance(c, int) and c == 0:
                    pe.wait_ge(q["zeroed0"], 1)
                for g in range(2):
                    wait(pe, "x_done", c, 10, 10)
                    for hh in range(H2):
                        for d in range(2):
                            h = g * H2 + hh
                            pe.matmul(B[4 + g][K[d], hd(hh)], arT[s][K[d], h, 0, :], st[K[d], hd(h)], start=True, stop=False)
                            mm = pe.matmul(B[4 + g][K[d], hd(hh)], ak[K[d], h, 0, :], V[K[d], hd(h)], start=False, stop=True)
                    mm.then_inc(q["g_sum"], 1)
                for g in range(2):
                    wait(pe, "g_copied", c, 2, g + 1)
                    wait(pe, "d_copied", c, 10, 9 + g)
                    for hh in range(H2):
                        for d in range(2):
                            h = g * H2 + hh
                            mm = pe.matmul(B[6 + g][K[d], hd(hh)], dd[K[d], g, 1, hd(hh)], gs[K[d], hd(h)], start=True, stop=True)
                    mm.then_inc(q["u_sum"], 1)
                for g in range(2):
                    wait(pe, "u_copied", c, 2, g + 1)
                    for hh in range(H2):
                        for d in range(2):
                            h = g * H2 + hh
                            pe.matmul(B[6 + g][K[d], hd(hh)], beta[s][K[d], hd(h)], us[K[d], hd(h)], start=True, stop=False)
                            mm = pe.matmul(B[6 + g][K[d], hd(hh)], kap[s][K[d], hd(h)], V[K[d], hd(h)], start=False, stop=True)
                    mm.then_inc(q["s_sum"], 1)
                for g in range(2):
                    for hh in range(H2):
                        for d in range(2):
                            h = g * H2 + hh
                            out = B[4 + g][K[d], hd(hh)]
                            pe.matmul(out, arT[s][K[d], h, 1, :], st[K[d], hd(h)], start=True, stop=False)
                            pe.matmul(out, ab[K[d], h, 1, :], us[K[d], hd(h)], start=False, stop=False)
                            mm = pe.matmul(out, ak[K[d], h, 1, :], V[K[d], hd(h)], start=False, stop=True)
                    mm.then_inc(q["y_sum"], 1)

            def prepare(c, s):
                p_lora(c, s)
                p_cum(c, s)
                p_turn(c, s)

            def both(c, s):
                r_products(c, s)
                p_lora(c + 1, 1 - s)
                r_direct(c, s)
                r_level(c, s, 1)
                p_cum(c + 1, 1 - s)
                r_level(c, s, 2)
                r_level(c, s, 3)
                r_level(c, s, 4)
                p_turn(c + 1, 1 - s)
                r_level(c, s, 5)
                r_state(c, s)

            def recur(c, s):
                r_products(c, s)
                r_direct(c, s)
                for l in range(1, 6):
                    r_level(c, s, l)
                r_state(c, s)

            steps(pe, prepare, both, recur)

        @block.scalar
        def _(act):
            act.activation(lora[K[0], :, 0, :], per["wd"][K[0], :].rearrange("r (c t) -> r c t", t=C), ACT.Tanh)
            ins = act.copy(lora[K[0], :, 1, :], per["ad"][K[0], :].rearrange("r (c t) -> r c t", t=C))
            for c in range(NSTEP):
                t = LC - C * (c + 1) if c < LC // C else T + LC - C * (c + 1)
                act.activation(lora[K[1], c, 0, :], per["wd"][K[1], t:t + C], ACT.Tanh)
                ins = act.copy(lora[K[1], c, 1, :], per["ad"][K[1], t:t + C])
            ins.then_inc(q["lora_ready"], 1)
            act.wait_ge(q["lora_ready"], 1)

            def a_lora(c, s):
                wait(act, "lora_sum", c - 1, 1, 1)
                act.copy(lnow[:].rearrange("p a t -> p (a t)"),
                         lora[:, bass.ds(c, 1)].rearrange("p o a t -> p (o a t)")).then_inc(q["lora_now"], 1)

            def a_sig(c, s):
                wait(act, "pre_done", c, 2, 2)
                wait(act, "akk_done", c - 1, 1, 1)
                wait(act, "kd_done", c - 1, 1, 1)
                wait(act, "cum_done", c - 1, 1, 1)
                act.activation(sig[:], pre[:], ACT.Sigmoid).then_inc(q["sig_done"], 1)

            def a_root(c, s):
                wait(act, "clamped", c, 1, 1)
                wait(act, "kk_done", c - 1, 1, 1)
                act.activation(rn[:], ss[:], ACT.Sqrt).then_inc(q["rooted"], 1)

            def a_exp(c, s):
                wait(act, "cum_done", c, 1, 1)
                wait(act, "op_done", c - 1, 4, 4)
                act.activation(e_in[:], B[2][:], ACT.Exp).then_inc(q["exp_done"], 1)
                act.activation(e_ng[:], B[2][:], ACT.Exp, scale=-1.0).then_inc(q["exp_done"], 1)
                act.activation(e_ex[:], B[3][:], ACT.Exp).then_inc(q["exp_done"], 1)
                wait(act, "s_done", c - 2, 2, 2)
                act.activation(dec[s][:], B[0][:, 0:NH], ACT.Exp).then_inc(q["exp_done"], 1)

            def turn_copies(eng, copy, c, s, bank, dst, sem):
                v = B[bank][:].rearrange("p (a d t) -> p a d t", a=4, d=2)
                for par in range(2):
                    for d in range(2):
                        copy(dst(d, par), v[K[par], :, d, :]).then_inc(q[sem], 1)

            def a_turn(c, s):
                wait(act, "y_sum", c - 2, 2, 2)
                wait(act, "turned_up", c, 4, 1)
                turn_copies(act, act.copy, c, s, 1, lambda d, par: arT[s][K[d], par::2, 0, :], "tev_a")
                wait(act, "turned_up", c, 4, 4)
                turn_copies(act, act.copy, c, s, 2, lambda d, par: arT[s][K[d], par::2, 1, :], "tev_a")

            def a_level(c, s, l):
                for g in range(2):
                    wait(act, "d_sum", c, 10, 2 * (l - 1) + g + 1)
                    if l < 5:
                        act.copy(dd[:, g].rearrange("p a x -> p (a x)"), B[6 + g][:]).then_inc(q["d_copied"], 1)
                    else:
                        act.copy(dd[:, g, 1], B[6 + g][:, H2 * C:]).then_inc(q["d_copied"], 1)

            def a_state(c, s):
                for g in range(2):
                    wait(act, "g_sum", c, 2, g + 1)
                    act.copy(half(gs, g), B[4 + g][:, 0:H2 * C]).then_inc(q["g_copied"], 1)
                for g in range(2):
                    wait(act, "u_sum", c, 2, g + 1)
                    act.copy(half(us, g), B[6 + g][:, 0:H2 * C]).then_inc(q["u_copied"], 1)
                y_free(c, s)
                for g in range(2):
                    wait(act, "y_sum", c, 2, g + 1)
                    act.copy(yb[s][:, g * H2 * C:(g + 1) * H2 * C], B[4 + g][:, 0:H2 * C]).then_inc(q["y_copied"], 1)

            def y_free(c, s):
                v = 16 * (c - s - LC // C)
                if not (isinstance(v, int) and v <= 0):
                    act.wait_ge(y_out[s], v)

            def prepare(c, s):
                a_lora(c, s)
                a_sig(c, s)
                a_root(c, s)
                a_exp(c, s)
                a_turn(c, s)

            def both(c, s):
                a_lora(c + 1, 1 - s)
                a_sig(c + 1, 1 - s)
                a_root(c + 1, 1 - s)
                a_level(c, s, 1)
                a_exp(c + 1, 1 - s)
                a_level(c, s, 2)
                a_level(c, s, 3)
                a_level(c, s, 4)
                a_turn(c + 1, 1 - s)
                a_level(c, s, 5)
                a_state(c, s)

            def recur(c, s):
                for l in range(1, 6):
                    a_level(c, s, l)
                a_state(c, s)

            prepare(0, 0)
            for c in range(6):
                both(c, c % 2)
            with act.Fori(3, NSTEP // 2 - 1) as j:
                for s in range(2):
                    both(2 * j + s, s)
            both(NSTEP - 2, 0)
            recur(NSTEP - 1, 1)

        @block.gpsimd
        def _(pool):
            pool.wait_ge(con_in, 160)

            def prepare(c, s):
                pool.wait_ge(rkv_in[s], 32 * (c - s) + 64)
                wait(pool, "kd_done", c - 1, 1, 1)
                wait(pool, "bon_m", c - 1, 1, 1)
                pool.tensor_tensor(kka[:], rkv[s][:, 1, :], rows[:, 1, :], ALU.mult).then_inc(q["pool_k"], 1)
                wait(pool, "pool_k", c, 3, 1)
                pool.tensor_tensor(krest[:], rkv[s][:, 1, :], kka[:], ALU.subtract).then_inc(q["pool_k"], 1)
                pool.tensor_tensor(rrk[:], rkv[s][:, 0, :], rows[:, 2, :], ALU.mult).then_inc(q["pool_k"], 1)
                wait(pool, "pool_k", c, 3, 3)
                wait(pool, "kd_done", c, 1, 1)
                wait(pool, "bon_done", c - 1, 1, 1)
                pool.tensor_tensor(bon[:], rrk[:], kd[:], ALU.mult).then_inc(q["bon_m"], 1)

            def recur(c, s):
                wait(pool, "a_masked", c, 4, 2)
                wait(pool, "z_sum", c - 1, 10, 10)
                wait(pool, "dt0", c - 1, 2, 2)
                pool.tensor_tensor(abi[:], ab[:, :, 0, :], bc(eye[:], 1, NH), ALU.add).then_inc(q["abi_done"], 1)

            def both(c, s):
                recur(c, s)
                prepare(c + 1, 1 - s)

            steps(pool, prepare, both, recur)

        @block.vector
        def _(dve):
            dve.memset(st[:], 0.0).then_inc(q["zeroed0"], 1)
            dve.wait_ge(con_in, 160)
            dve.wait_ge(q["zeroed0"], 1)

            def d_pre(c, s):
                wait(dve, "lora_sum", c, 1, 1)
                wait(dve, "sig_done", c - 1, 1, 1)
                for i in range(2):
                    dve.tensor_tensor(pre[:, i], B[i][:], wa0[:, i], ALU.add).then_inc(q["pre_done"], 1)

            def d_keys(c, s):
                k = rkv[s][:, 1, :]
                dve.wait_ge(rkv_in[s], 32 * (c - s) + 64)
                dve.tensor_tensor(kkr[:], k, rows[:, 0, :], ALU.mult).then_inc(q["raw_k"], 1)
                wait(dve, "raw_k", c, 1, 1)
                dve.tensor_tensor(sq[:], kkr[:], kkr[:], ALU.mult).then_inc(q["sqd"], 1)
                wait(dve, "sqd", c, 1, 1)
                dve.tensor_reduce(ss[:], sq[:].rearrange("p (h k) -> p h k", h=NH), AX_X, ALU.add).then_inc(q["ssd"], 1)
                wait(dve, "ssd", c, 1, 1)
                dve.tensor_scalar(ss[:], ss[:], 1e-24, None, ALU.max).then_inc(q["clamped"], 1)

            def d_unit(c, s):
                wait(dve, "rooted", c, 1, 1)
                dve.reciprocal(rn[:], rn[:]).then_inc(q["rnd"], 1)
                wait(dve, "rnd", c, 1, 1)
                dve.tensor_tensor(kk[:].rearrange("p (h k) -> p h k", h=NH), kkr[:].rearrange("p (h k) -> p h k", h=NH),
                                  bc(rn[:], 2, HD), ALU.mult).then_inc(q["kk_done"], 1)

            def d_rate(c, s):
                wait(dve, "sig_done", c, 1, 1)
                wait(dve, "kk_done", c, 1, 1)
                dve.tensor_tensor(akk[:], sig[:, 1], kk[:], ALU.mult).then_inc(q["akk_done"], 1)
                wait(dve, "pool_k", c, 3, 3)
                wait(dve, "bon_m", c - 1, 1, 1)
                dve.tensor_tensor(kd[:], sig[:, 1], kka[:], ALU.mult).then_inc(q["kd_part"], 1)
                wait(dve, "kd_part", c, 1, 1)
                dve.tensor_tensor(kd[:], kd[:], krest[:], ALU.add).then_inc(q["kd_done"], 1)

            def d_ops(c, s):
                wait(dve, "exp_done", c, 4, 3)
                wait(dve, "turned_up", c - 1, 4, 4)
                wait(dve, "s_sum", c - 2, 2, 2)
                dve.tensor_tensor(alpha[:], kk[:], e_ex[:], ALU.mult).then_inc(q["op_done"], 1)
                wait(dve, "akk_done", c, 1, 1)
                dve.scalar_tensor_tensor(beta[s][:], akk[:], -1.0, e_ng[:], ALU.mult, ALU.mult).then_inc(q["op_done"], 1)
                wait(dve, "kd_done", c, 1, 1)
                dve.tensor_tensor(kap[s][:], kd[:], e_ng[:], ALU.mult).then_inc(q["op_done"], 1)
                dve.tensor_tensor(rho[:], rkv[s][:, 0, :], e_in[:], ALU.mult).then_inc(q["op_done"], 1)

            def d_turn(c, s):
                wait(dve, "s_sum", c - 2, 2, 2)
                for n, bank, dst in ((2, 3, bT), (3, 0, kT)):
                    wait(dve, "turned_up", c, 4, n)
                    v = B[bank][:].rearrange("p (a d t) -> p a d t", a=4, d=2)
                    for par in range(2):
                        for d in range(2):
                            dve.tensor_copy(dst[s][K[d], par::2, :], v[K[par], :, d, :]).then_inc(q["tev_d"], 1)

            def d_bonus(c, s):
                wait(dve, "bon_m", c, 1, 1)
                v = 16 * (c - s - LC // C)
                if not (isinstance(v, int) and v <= 0):
                    dve.wait_ge(y_out[s], v)
                dve.tensor_reduce(yb[s][:, RC:], bon[:].rearrange("p (h k) -> p h k", h=NH), AX_X, ALU.add).then_inc(q["bon_done"], 1)

            def d_masks(c, s):
                mask = bc(causal[:], 1, H2)
                wait(dve, "y_sum", c - 1, 2, 2)
                wait(dve, "abi_done", c - 1, 1, 1)
                for n, dst, g in ((0, ab, 0), (1, ab, 1), (2, ak, 0), (3, ak, 1)):
                    wait(dve, "a_sum", c, 4, n + 1)
                    dve.tensor_tensor(dst[:, g * H2:(g + 1) * H2].rearrange("p h a t -> p h (a t)"),
                                      B[4 + n][:].rearrange("p (h x) -> p h x", h=H2),
                                      bc(causal[:].rearrange("p a t -> p (a t)"), 1, H2), ALU.mult).then_inc(q["a_masked"], 1)

            def d_first(c, s):
                h4 = lambda ap: ap.rearrange("p (h t) -> p h t", h=H2)
                wait(dve, "d_sum", c - 1, 10, 10)
                wait(dve, "u_sum", c - 1, 2, 2)
                for g in range(2):
                    wait(dve, "adir", c, 2, g + 1)
                    dve.tensor_tensor(h4(dd[:, g, 0]), h4(B[4 + g][:, 0:H2 * C]), bc(level[:, 0], 1, H2), ALU.mult).then_inc(q["d_step"], 1)
                for g in range(2):
                    wait(dve, "d_step", c, 2, g + 1)
                    dve.tensor_tensor(h4(dd[:, g, 0]), h4(dd[:, g, 0]), bc(eye[:], 1, H2), ALU.add).then_inc(q["d0"], 1)
                wait(dve, "abi_done", c, 1, 1)
                for g in range(2):
                    dve.tensor_tensor(h4(dd[:, g, 1]), abi[:, g * H2:(g + 1) * H2], bc(level[:, 6], 1, H2), ALU.mult).then_inc(q["dt0"], 1)

            def d_level(c, s, l):
                h4 = lambda ap: ap.rearrange("p (h t) -> p h t", h=H2)
                for g in range(2):
                    wait(dve, "z_sum", c, 10, 2 * (l - 1) + g + 1)
                    if l > 1:
                        wait(dve, "d_sum", c, 10, 2 * (l - 2) + g + 1)
                    dve.tensor_tensor(h4(xm[:, g]), h4(B[4 + g][:, 0:H2 * C]), bc(level[:, l], 1, H2), ALU.mult).then_inc(q["x_done"], 1)

            def d_state(c, s):
                for g in range(2):
                    wait(dve, "s_sum", c, 2, g + 1)
                    dve.tensor_tensor(half(sm, g), half(st, g), B[6 + g][:, 0:H2 * C], ALU.add).then_inc(q["s_added"], 1)
                wait(dve, "y_sum", c, 2, 2)
                for g in range(2):
                    wait(dve, "s_added", c, 2, g + 1)
                    h4 = lambda ap: ap.rearrange("p (h t) -> p h t", h=H2)
                    dve.tensor_tensor(h4(half(st, g)), h4(half(sm, g)), bc(dec[s][:, g * H2:(g + 1) * H2], 2, HD), ALU.mult
                                      ).then_inc(q["s_done"], 1)

            def prepare(c, s):
                d_pre(c, s)
                d_keys(c, s)
                d_unit(c, s)
                d_rate(c, s)
                d_ops(c, s)
                d_turn(c, s)
                d_bonus(c, s)

            def both(c, s):
                d_masks(c, s)
                d_pre(c + 1, 1 - s)
                d_keys(c + 1, 1 - s)
                d_first(c, s)
                d_level(c, s, 1)
                d_unit(c + 1, 1 - s)
                d_level(c, s, 2)
                d_rate(c + 1, 1 - s)
                d_level(c, s, 3)
                d_ops(c + 1, 1 - s)
                d_level(c, s, 4)
                d_turn(c + 1, 1 - s)
                d_level(c, s, 5)
                d_bonus(c + 1, 1 - s)
                d_state(c, s)

            def recur(c, s):
                d_masks(c, s)
                d_first(c, s)
                for l in range(1, 6):
                    d_level(c, s, l)
                d_state(c, s)

            prepare(0, 0)
            for c in range(6):
                both(c, c % 2)
            with dve.Fori(3, NSTEP // 2 - 1) as j:
                for s in range(2):
                    both(2 * j + s, s)
            both(NSTEP - 2, 0)
            recur(NSTEP - 1, 1)


class Chain:

    def __init__(self, eng, sem, per):
        self.eng, self.sem, self.per = eng, sem, per

    def start(self, i):
        self.i, self.k = i, 0

    def do(self, ins):
        ins.then_inc(self.sem, 1)
        self.k += 1
        return self.k

    def wait(self, k=None):
        self.eng.wait_ge(self.sem, self.i * self.per + (self.k if k is None else k))

    def end(self):
        assert self.k == self.per, (self.k, self.per)


def merge(nc, sems, io, per):
    with ExitStack() as ctx:
        m = Mem(nc, ctx, "mg")
        wout = m.sb("wout", [P, KD, D])
        rows = m.sb("mrows", [P, 3 * CH + 2 * CH + 2 * RC])
        lnr = m.sb("lnr", [P, 2, D])
        gup = m.sb("gup", [P, RC])
        wrt = m.sb("wrt", [P, KD, NE])
        ebias = m.sb("ebias", [P, NE])
        wsgu = m.sb("wsgu", [P, KD, 2 * FF])
        wsd = m.sb("wsd", [P, 2, D])
        tri = m.sb("rtri", [P, P])
        ones = m.sb("ones", [P, P])
        iota = m.sb("iota", [P, NE])
        iotap = m.sb("iotap", [P, 1])
        thresh = m.sb("thresh", [P, 8])
        b = m.sb("b", [P, CH])
        cx = m.sb("cx", [P, 3, 2, CH])
        ycat = m.sb("ycat", [P, D])
        yh = m.sb("yh", [P, CH])
        ya = m.sb("ya", [P, CH])
        y01 = m.sb("y01", [P, 2, RC + NH])
        ysum = m.sb("ysum", [P, RC + NH])
        v = m.sb("v", [P, RC])
        z3 = m.sb("z3", [P, 3, CH])
        za = m.sb("za", [P, CH])
        yn = m.sb("yn", [P, RC])
        sqr = m.sb("sqr", [P, RC])
        bonus = m.sb("bonus", [P, RC])
        junk = m.sb("junk", [P, D])
        mean8 = m.sb("mean8", [P, NH])
        var = m.sb("var", [P, 2 + NH])
        rstd = m.sb("rstd", [P, 2 + NH])
        sgd = m.sb("sgd", [P, P])
        ycT = m.sb("ycT", [P, KD, P])
        x = m.sb("x", [P, D])
        t = m.sb("t", [P, D])
        x1 = m.sb("x1", [P, D])
        h2 = m.sb("h2", [P, D])
        base = m.sb("base", [P, D])
        h2T = m.sb("h2T", [P, KD, P])
        stat = m.sb("stat", [P, 4])
        sgm = m.sb("sgm", [P, FF])
        hid = m.sb("hid", [P, FF])
        hidT = m.sb("hidT", [P, 2, P])
        sc = m.sb("sc", [P, NE])
        biased = m.sb("biased", [P, NE])
        top = m.sb("top", [P, 8])
        topi = m.sb("topi", [P, 8], U32)
        topf = m.sb("topf", [P, 8])
        sel3 = m.sb("sel3", [P, TOPK, NE])
        mem = m.sb("mem", [P, NE])
        gsum = m.sb("gsum", [P, 2])
        rank = m.sb("rank", [P, NE])
        carry = m.sb("carry", [P, NE])
        OH = m.sb("OH", [P, NT, TOPK, NE])
        rnk = m.sb("rnk", [P, NT, TOPK])
        gates, slots, slots_i = per["gates"], m.sb("slots", [P, NT, TOPK]), per["slots_i"]
        names = ("G", "T0", "T1", "O0", "O1", "R", "S", "H")
        G, T0, T1, O0, O1, R, S, H = (m.ps(x) for x in names)
        w_in, a_in, x_in = sems("w_in"), sems("a_in"), sems("x_in")
        q = {n: sems(n) for n in (
            "a_free gate_sum gd_sig za2 sq_done vars rooted1 mixed turnedY ycT_done out_sum out_read mean_sum var_sum mu ln_var "
            "rooted2 h2_done turnedH h2T_done logits gu sig_gu hid_done turnedS hidT_done down_sum base_done scored routed "
            "member rank_sum rank_read shifted bon_done gn_sq lnb x_free tail tab "
            "dmix dout pmix h2_st base_st zt tok_in passed passed_pool").split()}
        tiling = ExitStack()
        block = tiling.enter_context(nc.Block())
        MIX, OUT, PMIX = 18, 20, 4

        def wait(eng, name, i, per_tile, k):
            val = i * per_tile + k
            if not (isinstance(val, int) and val <= 0):
                eng.wait_ge(q[name], val)

        def tiles(eng, mix, both, out):
            mix(0)
            both(0)
            with eng.Fori(1, NT - 1) as i:
                both(i)
            out(NT - 1)

        @block.sync
        def _(sp):
            for dst, src in ((rows[:], io["mix_rows"].partition_broadcast(P)), (gup[:], io["g_up"]),
                             (lnr[:].rearrange("p a d -> p (a d)"), io["ln_rows"][0:2 * D].partition_broadcast(P)),
                             (wrt[:], io["w_router"]), (ebias[:], io["e_bias"].partition_broadcast(P)),
                             (wsgu[:], io["w_s_gu"]), (wsd[:], io["w_s_down"]), (tri[:], io["rank_tri"]),
                             (iota[:], io["iota_e"]), (iotap[:], io["iota_p"]), (thresh[:], io["thresh"]), (wout[:], io["w_out"])):
                sp.dma_start(dst, src).then_inc(w_in, 16)

            def load_mix(i):
                wait(sp, "mixed", i - 1, 1, 1)
                wait(sp, "bon_done", i - 1, 1, 1)
                wait(sp, "sq_done", i - 1, 2, 2)
                r0 = LC + i * P
                sp.dma_start(b[:], io["u"][bass.ds(r0, P), 0:CH]).then_inc(a_in, 16)
                for n in range(3):
                    sp.dma_start(cx[:, n], io["u"][bass.ds(r0 + (n - 1) * GRID, P), CH:3 * CH]
                                 .rearrange("t (a c) -> t a c", a=2)).then_inc(a_in, 16)
                sp.dma_start(yh[:], io["yh"][bass.ds(i * P, P)]).then_inc(a_in, 16)
                sp.dma_start(y01[:, 0], io["ys0"][bass.ds(i * P, P)]).then_inc(a_in, 16)
                sp.dma_start(y01[:, 1], io["ys1"][bass.ds(i * P, P)]).then_inc(a_in, 16)
                sp.dma_start(v[:], io["u"][bass.ds(r0, P), UW - RC:UW]).then_inc(a_in, 16)

            def load_out(i):
                wait(sp, "x_free", i - 1, 1, 1)
                sp.dma_start(x[:], io["x"][bass.ds(i * P, P)]).then_inc(x_in, 16)

            def both(i):
                load_mix(i + 1)
                load_out(i)

            tiles(sp, load_mix, both, load_out)

        @block.tensor
        def _(pe):
            ident = per["ident"]
            pe.wait_ge(w_in, 192)

            def mix(i):
                wait(pe, "gd_sig", i, 1, 1)
                wait(pe, "mixed", i - 1, 1, 1)
                pe.matmul(G[:], sgd[:], gup[:], start=True, stop=True).then_inc(q["gate_sum"], 1)
                wait(pe, "mixed", i, 1, 1)
                wait(pe, "h2T_done", i - 2, 2, 2)
                for k in range(KD):
                    bank = (T0, T1)[k // 4]
                    mm = pe.transpose(bank[:, (k % 4) * P:(k % 4 + 1) * P], ycat[:, k * P:(k + 1) * P], ident[:])
                    if k % 4 == 3:
                        mm.then_inc(q["turnedY"], 1)

            def project_out(i):
                wait(pe, "ycT_done", i, 2, 2)
                wait(pe, "base_done", i - 1, 2, 2)
                for n, bank in enumerate((O0, O1)):
                    for k in range(KD):
                        mm = pe.matmul(bank[:], ycT[:, k, :], wout[:, k, n * 512:(n + 1) * 512], start=(k == 0), stop=(k == KD - 1))
                    mm.then_inc(q["out_sum"], 1)

            def after(i, mix_next):
                wait(pe, "h2_done", i, 1, 1)
                if mix_next:
                    wait(pe, "ycT_done", i + 1, 2, 2)
                for k in range(KD):
                    bank = (T0, T1)[k // 4]
                    mm = pe.transpose(bank[:, (k % 4) * P:(k % 4 + 1) * P], h2[:, k * P:(k + 1) * P], ident[:])
                    if k % 4 == 3:
                        mm.then_inc(q["turnedH"], 1)
                wait(pe, "h2T_done", i, 2, 2)
                wait(pe, "rank_read", i - 1, 2, 2)
                for k in range(KD):
                    mm = pe.matmul(R[:, 0:NE], h2T[:, k, :], wrt[:, k, :], start=(k == 0), stop=(k == KD - 1))
                mm.then_inc(q["logits"], 1)
                wait(pe, "hid_done", i - 1, 1, 1)
                for k in range(KD):
                    mm = pe.matmul(S[:], h2T[:, k, :], wsgu[:, k, :], start=(k == 0), stop=(k == KD - 1))
                mm.then_inc(q["gu"], 1)
                wait(pe, "member", i, 1, 1)
                pe.matmul(R[:, 128:128 + NE], tri[:], mem[:], start=True, stop=True)
                pe.matmul(R[:, 256:256 + NE], ones[:], mem[:], start=True, stop=True).then_inc(q["rank_sum"], 1)
                wait(pe, "hid_done", i, 1, 1)
                wait(pe, "hidT_done", i - 1, 1, 1)
                for k in range(2):
                    mm = pe.transpose(H[:, k * P:(k + 1) * P], hid[:, k * P:(k + 1) * P], ident[:])
                mm.then_inc(q["turnedS"], 1)
                wait(pe, "hidT_done", i, 1, 1)
                for n, bank in enumerate((O0, O1)):
                    for k in range(2):
                        mm = pe.matmul(bank[:], hidT[:, k, :], wsd[:, k, n * 512:(n + 1) * 512], start=(k == 0), stop=(k == 1))
                    mm.then_inc(q["down_sum"], 1)

            def both(i):
                project_out(i)
                mix(i + 1)
                wait(pe, "out_read", i, 2, 2)
                after(i, True)

            def out(i):
                project_out(i)
                wait(pe, "out_read", i, 2, 2)
                after(i, False)

            tiles(pe, mix, both, out)

        @block.scalar
        def _(act):
            def mix1(i):
                wait(act, "gate_sum", i - 1, 1, 1)
                act.activation(sgd[:], per["gd"][:, bass.ds(LC + i * P, P)], ACT.Sigmoid).then_inc(q["gd_sig"], 1)

            def mix2(i):
                act.wait_ge(a_in, 128 * i + 128)
                wait(act, "vars", i - 1, 1, 1)
                act.activation(junk[:, 0:CH], yh[:], ACT.Square, accum_out=var[:, 1:2]).then_inc(q["sq_done"], 1)
                wait(act, "za2", i, 1, 1)
                act.activation(junk[:, CH:2 * CH], ya[:], ACT.Square, accum_out=var[:, 0:1]).then_inc(q["sq_done"], 1)
                wait(act, "vars", i, 1, 1)
                act.activation(rstd[:], var[:], ACT.Sqrt).then_inc(q["rooted1"], 1)

            def mix3(i):
                wait(act, "out_sum", i - 1, 2, 2)
                for g, bank in enumerate((T0, T1)):
                    wait(act, "turnedY", i, 2, g + 1)
                    act.copy(ycT[:, 4 * g:4 * g + 4].rearrange("p k t -> p (k t)"), bank[:]).then_inc(q["ycT_done"], 1)

            def norm(i):
                wait(act, "out_read", i, 2, 2)
                wait(act, "shifted", i, 1, 1)
                act.activation(junk[:], t[:], ACT.Identity, accum_out=stat[:, 0:1]).then_inc(q["mean_sum"], 1)
                wait(act, "mu", i, 1, 1)
                wait(act, "mean_sum", i, 1, 1)
                act.activation(junk[:], t[:], ACT.Square, bias=stat[:, 1:2], accum_out=stat[:, 2:3]).then_inc(q["var_sum"], 1)
                wait(act, "ln_var", i, 1, 1)
                act.activation(stat[:, 3:4], stat[:, 2:3], ACT.Sqrt).then_inc(q["rooted2"], 1)

            def after(i):
                wait(act, "down_sum", i - 1, 2, 2)
                for g, bank in enumerate((T0, T1)):
                    wait(act, "turnedH", i, 2, g + 1)
                    act.copy(h2T[:, 4 * g:4 * g + 4].rearrange("p k t -> p (k t)"), bank[:]).then_inc(q["h2T_done"], 1)
                wait(act, "logits", i, 1, 1)
                wait(act, "routed", i - 1, 1, 1)
                act.activation(sc[:], R[:, 0:NE], ACT.Sigmoid).then_inc(q["scored"], 1)
                wait(act, "gu", i, 1, 1)
                wait(act, "hid_done", i - 1, 1, 1)
                act.activation(sgm[:], S[:, 0:FF], ACT.Sigmoid).then_inc(q["sig_gu"], 1)
                wait(act, "turnedS", i, 1, 1)
                act.copy(hidT[:].rearrange("p k t -> p (k t)"), H[:, 0:2 * P]).then_inc(q["hidT_done"], 1)

            def mix(i):
                mix1(i)
                mix2(i)
                mix3(i)

            def both(i):
                mix(i + 1)
                norm(i)
                after(i)

            def out(i):
                norm(i)
                after(i)

            tiles(act, mix, both, out)

        @block.gpsimd
        def _(pool):
            pool.memset(ones[:], 1.0).then_inc(q["tok_in"], 1)
            pool.wait_ge(w_in, 192)
            pool.wait_ge(q["tok_in"], 1)
            ch = Chain(pool, q["pmix"], PMIX)
            v3 = lambda ap: ap.rearrange("p (h k) -> p h k", h=NH)

            def mix(i):
                ch.start(i)
                pool.wait_ge(a_in, 128 * i + 128)
                wait(pool, "za2", i - 1, 1, 1)
                ch.do(pool.tensor_tensor(z3[:], cx[:, :, 0], cx[:, :, 1], ALU.mult))
                ch.wait()
                ch.do(pool.tensor_tensor(z3[:].rearrange("p a c -> p (a c)"), z3[:].rearrange("p a c -> p (a c)"), rows[:, 0:3 * CH], ALU.mult))
                ch.wait()
                wait(pool, "mixed", i - 1, 1, 1)
                ch.do(pool.tensor_tensor(za[:], z3[:, 0], z3[:, 1], ALU.add))
                ch.wait()
                pool.wait_ge(q["dmix"], i * MIX + 1)
                ch.do(pool.tensor_tensor(v3(bonus[:]), bc(ysum[:, RC:], 2, HD), v3(v[:]), ALU.mult))
                ch.wait()
                pool.sem_inc(q["bon_done"], 1)
                ch.end()

            def out(i):
                wait(pool, "h2_done", i, 1, 1)
                pool.sem_inc(q["passed_pool"], 1)
                pool.dma_start(io["h2"][bass.ds(i * P, P)], h2[:]).then_inc(q["h2_st"], 16)
                wait(pool, "base_done", i, 2, 2)
                pool.sem_inc(q["passed_pool"], 1)
                pool.dma_start(io["base"][bass.ds(i * P, P)], base[:]).then_inc(q["base_st"], 16)

            def both(i):
                mix(i + 1)
                out(i)

            tiles(pool, mix, both, out)
            pool.wait_ge(q["h2_st"], 16 * NT)
            pool.wait_ge(q["base_st"], 16 * NT)

        @block.vector
        def _(dve):
            dve.memset(carry[:], 0.0).then_inc(q["zt"], 1)
            dve.wait_ge(w_in, 192)
            dve.wait_ge(q["zt"], 1)
            dve.wait_ge(q["tok_in"], 1)
            cm, co = Chain(dve, q["dmix"], MIX), Chain(dve, q["dout"], OUT)
            v3 = lambda ap: ap.rearrange("p (h k) -> p h k", h=NH)
            o = 3 * CH

            def mix(i):
                c = cm
                c.start(i)
                dve.wait_ge(a_in, 128 * i + 128)
                wait(dve, "bon_done", i - 1, 1, 1)
                c.do(dve.tensor_tensor(ysum[:], y01[:, 0], y01[:, 1], ALU.add))
                c.wait()
                c.do(dve.tensor_reduce(mean8[:], v3(ysum[:, 0:RC]), AX_X, ALU.add))
                c.wait()
                c.do(dve.tensor_scalar(mean8[:], mean8[:], 1.0 / HD, None, ALU.mult))
                c.wait()
                c.do(dve.tensor_tensor(v3(yn[:]), v3(ysum[:, 0:RC]), bc(mean8[:], 2, HD), ALU.subtract))
                c.wait()
                c.do(dve.tensor_tensor(sqr[:], yn[:], yn[:], ALU.mult))
                dve.wait_ge(q["pmix"], i * PMIX + 3)
                c.do(dve.tensor_tensor(za[:], za[:], z3[:, 2], ALU.add))
                c.wait()
                c.do(dve.tensor_tensor(ya[:], za[:], b[:], ALU.mult))
                c.wait()
                dve.sem_inc(q["za2"], 1)
                wait(dve, "rooted1", i - 1, 1, 1)
                c.do(dve.tensor_reduce(var[:, 2:], v3(sqr[:]), AX_X, ALU.add))
                c.wait()
                c.do(dve.tensor_scalar(var[:, 2:], var[:, 2:], 1.0 / HD, GN_EPS, ALU.mult, ALU.add))
                wait(dve, "sq_done", i, 2, 2)
                c.do(dve.tensor_scalar(var[:, 0:2], var[:, 0:2], 1.0 / CH, LN_EPS, ALU.mult, ALU.add))
                c.wait()
                dve.sem_inc(q["vars"], 1)
                wait(dve, "rooted1", i, 1, 1)
                c.do(dve.reciprocal(rstd[:], rstd[:]))
                c.wait()
                wait(dve, "turnedY", i - 1, 2, 2)
                c.do(dve.scalar_tensor_tensor(ycat[:, 0:CH], ya[:], rstd[:, 0:1], rows[:, o:o + CH], ALU.mult, ALU.mult))
                c.do(dve.scalar_tensor_tensor(ycat[:, CH:2 * CH], yh[:], rstd[:, 1:2], rows[:, o + CH:o + 2 * CH], ALU.mult, ALU.mult))
                c.do(dve.tensor_tensor(v3(yn[:]), v3(yn[:]), bc(rstd[:, 2:], 2, HD), ALU.mult))
                c.wait()
                g0 = o + 2 * CH
                c.do(dve.tensor_tensor(yn[:], yn[:], rows[:, g0:g0 + RC], ALU.mult))
                c.wait()
                c.do(dve.tensor_tensor(yn[:], yn[:], rows[:, g0 + RC:g0 + 2 * RC], ALU.add))
                c.wait()
                wait(dve, "bon_done", i, 1, 1)
                c.do(dve.tensor_tensor(yn[:], yn[:], bonus[:], ALU.add))
                c.wait()
                wait(dve, "gate_sum", i, 1, 1)
                c.do(dve.tensor_tensor(ycat[:, 2 * CH:], yn[:], G[:], ALU.mult))
                c.wait()
                dve.sem_inc(q["mixed"], 1)
                c.end()

            def norm(i):
                c = co
                c.start(i)
                dve.wait_ge(x_in, 16 * i + 16)
                g1 = per["rows"][:, 0:D]
                wait(dve, "var_sum", i - 1, 1, 1)
                for n, bank in enumerate((O0, O1)):
                    wait(dve, "out_sum", i, 2, n + 1)
                    dve.tensor_tensor(t[:, n * 512:(n + 1) * 512], bank[:], g1[:, n * 512:(n + 1) * 512], ALU.mult).then_inc(q["out_read"], 1)
                wait(dve, "out_read", i, 2, 2)
                dve.scalar_tensor_tensor(t[:], x[:], ALPHA, t[:], ALU.mult, ALU.add).then_inc(q["shifted"], 1)
                wait(dve, "mean_sum", i, 1, 1)
                dve.sem_inc(q["x_free"], 1)
                c.do(dve.tensor_scalar(stat[:, 1:2], stat[:, 0:1], -1.0 / D, None, ALU.mult))
                c.wait()
                dve.sem_inc(q["mu"], 1)
                wait(dve, "var_sum", i, 1, 1)
                c.do(dve.tensor_scalar(stat[:, 2:3], stat[:, 2:3], 1.0 / D, LN_EPS, ALU.mult, ALU.add))
                c.wait()
                dve.sem_inc(q["ln_var"], 1)
                wait(dve, "rooted2", i, 1, 1)
                c.do(dve.reciprocal(stat[:, 3:4], stat[:, 3:4]))
                c.wait()
                c.do(dve.tensor_scalar(x1[:], t[:], stat[:, 1:2], stat[:, 3:4], ALU.add, ALU.mult))
                c.wait()
                c.do(dve.tensor_tensor(x1[:], x1[:], lnr[:, 0], ALU.mult))
                c.wait()
                c.do(dve.tensor_tensor(x1[:], x1[:], lnr[:, 1], ALU.add))
                c.wait()
                wait(dve, "turnedH", i - 1, 2, 2)
                wait(dve, "h2_st", i - 1, 16, 16)
                c.do(dve.tensor_tensor(h2[:], x1[:], per["rows"][:, 2 * D:3 * D], ALU.mult))
                c.wait()
                dve.tensor_tensor(h2[:], h2[:], per["rows"][:, D:2 * D], ALU.add).then_inc(q["h2_done"], 1)

            def after(i):
                c = co
                wait(dve, "scored", i, 1, 1)
                c.do(dve.tensor_tensor(biased[:], sc[:], ebias[:], ALU.add))
                c.wait()
                dve.sem_inc(q["passed"], 1)
                c.do(dve.max(top[:], biased[:]))
                c.wait()
                dve.sem_inc(q["passed"], 1)
                c.do(dve.max_index(topi[:], top[:], biased[:]))
                c.wait()
                c.do(dve.tensor_copy(topf[:], topi[:]))
                c.wait()
                oh = OH[:, bass.ds(i, 1)].rearrange("p o j e -> p (o j) e")
                c.do(dve.tensor_tensor(oh, bc(iota[:], 1, TOPK), bc(topf[:], 2, NE), ALU.is_equal))
                c.wait()
                dve.sem_inc(q["passed"], 1)
                dve.tensor_reduce(mem[:], oh.rearrange("p j e -> p e j"), AX_X, ALU.add).then_inc(q["member"], 1)
                c.do(dve.tensor_tensor(sel3[:], oh, bc(sc[:], 1, TOPK), ALU.mult))
                c.wait()
                gt = gates[:, bass.ds(i, 1)].rearrange("p o j -> p (o j)")
                c.do(dve.tensor_reduce(gt, sel3[:], AX_X, ALU.add))
                c.wait()
                dve.sem_inc(q["routed"], 1)
                c.do(dve.tensor_reduce(gsum[:, 0:1], gt, AX_X, ALU.add))
                c.wait()
                c.do(dve.reciprocal(gsum[:, 1:2], gsum[:, 0:1]))
                c.wait()
                c.do(dve.tensor_scalar(gt, gt, gsum[:, 1:2], ROUTED, ALU.mult, ALU.mult))
                wait(dve, "sig_gu", i, 1, 1)
                wait(dve, "turnedS", i - 1, 1, 1)
                c.do(dve.tensor_tensor(hid[:], sgm[:], S[:, 0:FF], ALU.mult))
                c.wait()
                dve.tensor_tensor(hid[:], hid[:], S[:, FF:2 * FF], ALU.mult).then_inc(q["hid_done"], 1)
                wait(dve, "rank_sum", i, 1, 1)
                dve.tensor_tensor(rank[:], R[:, 128:128 + NE], carry[:], ALU.add).then_inc(q["rank_read"], 1)
                wait(dve, "rank_read", i, 2, 1)
                dve.tensor_tensor(carry[:], R[:, 256:256 + NE], carry[:], ALU.add).then_inc(q["rank_read"], 1)
                c.do(dve.tensor_tensor(sel3[:], oh, bc(rank[:], 1, TOPK), ALU.mult))
                c.wait()
                c.do(dve.tensor_reduce(rnk[:, bass.ds(i, 1)].rearrange("p o j -> p (o j)"), sel3[:], AX_X, ALU.add))
                c.wait()
                wait(dve, "rank_read", i, 2, 2)
                wait(dve, "base_st", i - 1, 16, 16)
                g2 = per["rows"][:, 3 * D:4 * D]
                for n, bank in enumerate((O0, O1)):
                    wait(dve, "down_sum", i, 2, n + 1)
                    dve.tensor_tensor(base[:, n * 512:(n + 1) * 512], bank[:], g2[:, n * 512:(n + 1) * 512], ALU.mult).then_inc(q["tail"], 1)
                    wait(dve, "tail", i, 2, n + 1)
                    dve.scalar_tensor_tensor(base[:, n * 512:(n + 1) * 512], x1[:, n * 512:(n + 1) * 512], ALPHA,
                                             base[:, n * 512:(n + 1) * 512], ALU.mult, ALU.add).then_inc(q["base_done"], 1)
                wait(dve, "base_done", i, 2, 2)
                c.end()

            def both(i):
                mix(i + 1)
                norm(i)
                after(i)

            def out(i):
                norm(i)
                after(i)

            tiles(dve, mix, both, out)

        tiling.close()

        nb = m.sb("nb", [P, NE])
        ends = [m.sb(f"ends{n}", [P, NE]) for n in range(2)]
        first = m.sb("first", [P, NE])
        be = m.sb("be", [P, 1])
        bei = m.sb("bei", [P, 1], I32)
        tok = m.sb("tok", [P, NT], I32)
        zi = m.sb("zi", [P, P], I32)
        route = sems("route")
        slots_ready, be_ready, zero_ready, tok_ready = (sems(x) for x in ("slots_ready", "be_ready", "zero_ready", "tok_ready"))
        zero_out, be_out, tok_out = sems("zero_out"), sems("be_out"), sems("tok_out")
        tables = ExitStack()
        block = tables.enter_context(nc.Block())

        @block.vector
        def _(dve):
            c = Chain(dve, route, 0)
            c.start(0)

            def do(ins):
                c.do(ins)
                c.wait()

            dve.memset(zi[:], 0).then_inc(zero_ready, 1)
            cmp = sel3[:].rearrange("p j e -> p (j e)").rearrange("p (e n) -> p e n", n=8)
            do(dve.tensor_tensor(cmp, bc(carry[:], 2, 8), bc(thresh[:], 1, NE), ALU.is_gt))
            do(dve.tensor_reduce(nb[:], cmp, AX_X, ALU.add))
            do(dve.tensor_copy(ends[0][:], nb[:]))
            for n in range(6):
                a, z, sh = ends[n % 2], ends[(n + 1) % 2], 2 ** n
                do(dve.tensor_copy(z[:, 0:sh], a[:, 0:sh]))
                do(dve.tensor_tensor(z[:, sh:], a[:, sh:], a[:, 0:NE - sh], ALU.add))
            do(dve.tensor_tensor(first[:], ends[0][:], nb[:], ALU.subtract))
            do(dve.tensor_scalar(first[:], first[:], float(P), None, ALU.mult))
            for i in range(NT):
                do(dve.tensor_tensor(sel3[:], OH[:, i], bc(first[:], 1, TOPK), ALU.mult))
                do(dve.tensor_reduce(slots[:, i], sel3[:], AX_X, ALU.add))
            do(dve.tensor_tensor(slots[:], slots[:], rnk[:], ALU.add))
            dve.tensor_copy(slots_i[:], slots[:]).then_inc(slots_ready, 1)
            do(dve.tensor_tensor(rank[:], ends[0][:], iotap[:].broadcast_to([P, NE]), ALU.is_le))
            do(dve.tensor_reduce(be[:], rank[:], AX_X, ALU.add))
            do(dve.tensor_scalar(be[:], be[:], float(NE - 1), None, ALU.min))
            dve.tensor_copy(bei[:], be[:]).then_inc(be_ready, 1)

        @block.sync
        def _(sp):
            sp.wait_ge(zero_ready, 1)
            sp.dma_start(io["slot_token"].rearrange("(b p) o -> b (p o)", p=P), zi[:]).then_inc(zero_out, 16)
            sp.wait_ge(be_ready, 1)
            sp.dma_start(io["block_expert"].rearrange("o b -> b o"), bei[:]).then_inc(be_out, 16)
            sp.wait_ge(zero_out, 16)
            sp.wait_ge(be_out, 16)

        @block.gpsimd
        def _(pool):
            pool.iota(tok[:], [[P, NT]], base=0, channel_multiplier=1).then_inc(tok_ready, 1)
            pool.wait_ge(tok_ready, 1)
            pool.wait_ge(slots_ready, 1)
            pool.wait_ge(zero_out, 16)
            for i in range(NT):
                for j in range(TOPK):
                    pool.indirect_dma_start(out=io["slot_token"], out_offset=bass.IndirectOffsetOnAxis(ap=slots_i[:, i, j:j + 1], axis=0),
                                            in_=tok[:, i:i + 1], in_offset=None).then_inc(tok_out, 16)
            pool.wait_ge(tok_out, 16 * NT * TOPK)

        tables.close()


def experts(nc, sems, io, per):
    with ExitStack() as ctx:
        m = Mem(nc, ctx, "ex")
        NB = NBLK + 1
        wg = [m.sb(f"wg{s}", [P, KD, FF]) for s in range(2)]
        wu = [m.sb(f"wu{s}", [P, KD, FF]) for s in range(2)]
        wd = [m.sb(f"wd{s}", [P, 2, D]) for s in range(2)]
        xg = [m.sb(f"xg{s}", [P, D]) for s in range(2)]
        xT = [m.sb(f"xT{s}", [P, KD, P]) for s in range(2)]
        y = [m.sb(f"y{s}", [P, D]) for s in range(2)]
        sg = m.sb("sg", [P, FF])
        hid = m.sb("hid", [P, FF])
        hidT = m.sb("hidT", [P, 2, P])
        be = m.sb("be", [1, P], I32)
        idx_b = m.sb("idx_b", [P, P], I32)
        idx_f = m.sb("idx_f", [P, P])
        idx = m.sb("idx", [P, P], I32)
        idx_now = [m.sb(f"idx_now{s}", [P, 1], I32) for s in range(2)]
        T0, T1, H, O0, O1 = (m.ps(x) for x in ("T0", "T1", "H", "O0", "O1"))
        S = [m.ps(f"S{s}") for s in range(2)]
        q = {n: sems(n) for n in ("be_in idx_in idx_conv idx_turned idx_ready turned xT_done gu_sum sig_done hid_part hid_done "
                                  "turnedS hidT_done down_sum y_done idx_copied passed").split()}
        wg_in, wd_in, x_in, y_out = ([sems(f"{x}{s}") for s in range(2)] for x in ("wg_in", "wd_in", "x_in", "y_out"))
        block = ctx.enter_context(nc.Block())

        def wait(eng, name, b, per_block, k):
            v = b * per_block + k
            if not (isinstance(v, int) and v <= 0):
                eng.wait_ge(q[name], v)

        def blocks(eng, body):
            for b in range(2):
                body(b, b)
            with eng.Fori(1, NB // 2) as j:
                for s in range(2):
                    body(2 * j + s, s)

        @block.sync
        def _(sp):
            sp.dma_start(be[:], io["block_expert"]).then_inc(q["be_in"], 16)
            sp.dma_start(idx_b[:], io["slot_token"].rearrange("(b p) o -> b (p o)", p=P)).then_inc(q["idx_in"], 16)
            sp.wait_ge(q["be_in"], 16)

            def load(b, s):
                e = sp.value_load(be[0:1, bass.ds(b, 1)], min_val=0, max_val=NE - 1)
                wait(sp, "gu_sum", b - 2, 1, 1)
                for dst, src in ((wg, "w_e_gate"), (wu, "w_e_up")):
                    sp.dma_start(dst[s][:].rearrange("p k f -> p (k f)"),
                                 io[src][bass.ds(e, 1)].rearrange("o (p k) f -> p (o k f)", p=P)).then_inc(wg_in[s], 16)
                wait(sp, "down_sum", b - 2, 2, 2)
                sp.dma_start(wd[s][:].rearrange("p k f -> p (k f)"),
                             io["w_e_down"][bass.ds(e, 1)].rearrange("o (p k) d -> p (o k d)", p=P)).then_inc(wd_in[s], 16)

            blocks(sp, load)

        @block.gpsimd
        def _(pool):
            pool.wait_ge(q["idx_ready"], 1)

            def gather(b, s):
                wait(pool, "turned", b - 2, 2, 2)
                if isinstance(b, int) and b < 2:
                    pass
                else:
                    pool.wait_ge(x_in[s], 16 * (b - s) // 2 if isinstance(b, int) else 8 * (b - s))
                pool.tensor_copy(idx_now[s][:], idx[:, bass.ds(b, 1)]).then_inc(q["idx_copied"], 1)
                wait(pool, "idx_copied", b, 1, 1)
                pool.sem_inc(q["passed"], 1)
                pool.indirect_dma_start(out=xg[s][:], out_offset=None, in_=io["h2"],
                                        in_offset=bass.IndirectOffsetOnAxis(ap=idx_now[s][:], axis=0)).then_inc(x_in[s], 16)

            blocks(pool, gather)

        @block.tensor
        def _(pe):
            ident = per["ident"]
            pe.wait_ge(q["idx_conv"], 1)
            pe.transpose(H[:, 0:P], idx_f[:], ident[:]).then_inc(q["idx_turned"], 1)
            pe.wait_ge(q["idx_ready"], 1)

            def turn(b, s):
                pe.wait_ge(x_in[s], 8 * (b - s) + 16)
                wait(pe, "xT_done", b - 1, 2, 2)
                for k in range(KD):
                    mm = pe.transpose((T0, T1)[k // 4][:, (k % 4) * P:(k % 4 + 1) * P], xg[s][:, k:D:KD], ident[:])
                    if k % 4 == 3:
                        mm.then_inc(q["turned"], 1)

            def gate_up(b, s):
                pe.wait_ge(wg_in[s], 16 * (b - s) + 32)
                wait(pe, "xT_done", b, 2, 2)
                wait(pe, "hid_done", b - 2, 1, 1)
                for w, c0 in ((wg, 0), (wu, FF)):
                    for k in range(KD):
                        mm = pe.matmul(S[s][:, c0:c0 + FF], xT[s][:, k, :], w[s][:, k, :], start=(k == 0), stop=(k == KD - 1))
                mm.then_inc(q["gu_sum"], 1)

            def down(b, s):
                wait(pe, "hid_done", b, 1, 1)
                wait(pe, "hidT_done", b - 1, 1, 1)
                for k in range(2):
                    mm = pe.transpose(H[:, k * P:(k + 1) * P], hid[:, k:FF:2], ident[:])
                mm.then_inc(q["turnedS"], 1)
                wait(pe, "hidT_done", b, 1, 1)
                pe.wait_ge(wd_in[s], 8 * (b - s) + 16)
                for n, bank in enumerate((O0, O1)):
                    wait(pe, "y_done", b - 1, 2, n + 1)
                    for k in range(2):
                        mm = pe.matmul(bank[:], hidT[:, k, :], wd[s][:, k, n * 512:(n + 1) * 512], start=(k == 0), stop=(k == 1))
                    mm.then_inc(q["down_sum"], 1)

            turn(0, 0)

            def body(b, s):
                gate_up(b, s)
                turn(b + 1, 1 - s)
                down(b, s)

            for b in range(2):
                body(b, b)
            with pe.Fori(1, NB // 2 - 1) as j:
                for s in range(2):
                    body(2 * j + s, s)
            body(NB - 2, 0)
            gate_up(NB - 1, 1)
            down(NB - 1, 1)

        @block.scalar
        def _(act):
            def x_copy(b, s):
                wait(act, "gu_sum", b - 2, 1, 1)
                for n, bank in enumerate((T0, T1)):
                    wait(act, "turned", b, 2, n + 1)
                    act.copy(xT[s][:, 4 * n:4 * n + 4].rearrange("p k t -> p (k t)"), bank[:]).then_inc(q["xT_done"], 1)

            def rest(b, s):
                wait(act, "gu_sum", b, 1, 1)
                wait(act, "hid_part", b - 1, 1, 1)
                act.activation(sg[:], S[s][:, 0:FF], ACT.Sigmoid).then_inc(q["sig_done"], 1)

            def tail(b, s):
                wait(act, "turnedS", b, 1, 1)
                wait(act, "down_sum", b - 1, 2, 2)
                act.copy(hidT[:].rearrange("p k t -> p (k t)"), H[:, 0:2 * P]).then_inc(q["hidT_done"], 1)
                wait(act, "y_done", b, 2, 2)
                act.dma_start(io["eslots"][bass.ds(b * P, P)], y[s][:]).then_inc(y_out[s], 16)

            x_copy(0, 0)

            def body(b, s):
                rest(b, s)
                x_copy(b + 1, 1 - s)
                tail(b, s)

            for b in range(2):
                body(b, b)
            with act.Fori(1, NB // 2 - 1) as j:
                for s in range(2):
                    body(2 * j + s, s)
            body(NB - 2, 0)
            rest(NB - 1, 1)
            tail(NB - 1, 1)
            for s in range(2):
                act.wait_ge(y_out[s], 16 * NB // 2)

        @block.vector
        def _(dve):
            dve.wait_ge(q["idx_in"], 16)
            dve.tensor_copy(idx_f[:], idx_b[:]).then_inc(q["idx_conv"], 1)
            dve.wait_ge(q["idx_turned"], 1)
            dve.tensor_copy(idx[:], H[:, 0:P]).then_inc(q["idx_ready"], 1)

            def body(b, s):
                wait(dve, "sig_done", b, 1, 1)
                wait(dve, "turnedS", b - 1, 1, 1)
                dve.tensor_tensor(hid[:], sg[:], S[s][:, 0:FF], ALU.mult).then_inc(q["hid_part"], 1)
                wait(dve, "hid_part", b, 1, 1)
                dve.tensor_tensor(hid[:], hid[:], S[s][:, FF:2 * FF], ALU.mult).then_inc(q["hid_done"], 1)
                if not (isinstance(b, int) and b < 2):
                    dve.wait_ge(y_out[s], 8 * (b - s))
                for n, bank in enumerate((O0, O1)):
                    wait(dve, "down_sum", b, 2, n + 1)
                    dve.tensor_copy(y[s][:, n * 512:(n + 1) * 512], bank[:]).then_inc(q["y_done"], 1)

            blocks(dve, body)


def combine(nc, sems, io, per):
    with ExitStack() as ctx:
        m = Mem(nc, ctx, "co")
        yg = m.sb("yg", [P, TOPK, D])
        idx_now = m.sb("cidx", [P, TOPK], U32)
        gnow = m.sb("gnow", [P, TOPK])
        base = m.sb("cbase", [P, D])
        acc = m.sb("acc", [P, D])
        lnr = m.sb("clnr", [P, 2, D])
        junk = m.sb("cjunk", [P, D])
        o = m.sb("o", [P, D])
        stat = m.sb("cstat", [P, 4])
        q = {n: sems(n) for n in "ln_in base_in idx_copied added acc_done mean_sum mu var_sum ln_var rooted out_done stored dco passed".split()}
        y_in = [sems(f"y_in{j}") for j in range(TOPK)]
        block = ctx.enter_context(nc.Block())
        OWN = 5

        def wait(eng, name, i, per_tile, k):
            v = i * per_tile + k
            if not (isinstance(v, int) and v <= 0):
                eng.wait_ge(q[name], v)

        def tiles(eng, body):
            body(0)
            with eng.Fori(1, NT) as i:
                body(i)

        @block.sync
        def _(sp):
            sp.dma_start(lnr[:].rearrange("p a d -> p (a d)"), io["ln_rows"][2 * D:4 * D].partition_broadcast(P)).then_inc(q["ln_in"], 16)

            def body(i):
                wait(sp, "acc_done", i - 1, 1, 1)
                sp.dma_start(base[:], io["base"][bass.ds(i * P, P)]).then_inc(q["base_in"], 16)

            tiles(sp, body)

        @block.gpsimd
        def _(pool):
            def body(i):
                for j in range(TOPK):
                    if not (isinstance(i, int) and i == 0):
                        pool.wait_ge(y_in[j], 16 * i)
                pool.tensor_copy(idx_now[:], per["slots_i"][:, bass.ds(i, 1)].rearrange("p o j -> p (o j)")).then_inc(q["idx_copied"], 1)
                wait(pool, "idx_copied", i, 1, 1)
                for j in range(TOPK):
                    wait(pool, "added", i - 1, TOPK, j + 1)
                    pool.sem_inc(q["passed"], 1)
                    pool.indirect_dma_start(out=yg[:, j, :], out_offset=None, in_=io["eslots"],
                                            in_offset=bass.IndirectOffsetOnAxis(ap=idx_now[:, j:j + 1], axis=0)).then_inc(y_in[j], 16)

            tiles(pool, body)

        @block.vector
        def _(dve):
            dve.wait_ge(q["ln_in"], 16)
            c = Chain(dve, q["dco"], OWN)

            def body(i):
                c.start(i)
                c.do(dve.tensor_copy(gnow[:], per["gates"][:, bass.ds(i, 1)].rearrange("p o j -> p (o j)")))
                c.wait()
                wait(dve, "var_sum", i - 1, 1, 1)
                for j in range(TOPK):
                    dve.wait_ge(y_in[j], 16 * i + 16)
                    if j == 0:
                        dve.tensor_scalar(acc[:], yg[:, 0], gnow[:, 0:1], None, ALU.mult).then_inc(q["added"], 1)
                    else:
                        wait(dve, "added", i, TOPK, j)
                        dve.scalar_tensor_tensor(acc[:], yg[:, j], gnow[:, j:j + 1], acc[:], ALU.mult, ALU.add).then_inc(q["added"], 1)
                wait(dve, "added", i, TOPK, TOPK)
                c.do(dve.tensor_tensor(acc[:], acc[:], per["rows"][:, 3 * D:4 * D], ALU.mult))
                c.wait()
                dve.wait_ge(q["base_in"], 16 * i + 16)
                dve.tensor_tensor(acc[:], acc[:], base[:], ALU.add).then_inc(q["acc_done"], 1)
                wait(dve, "mean_sum", i, 1, 1)
                dve.tensor_scalar(stat[:, 1:2], stat[:, 0:1], -1.0 / D, None, ALU.mult).then_inc(q["mu"], 1)
                wait(dve, "var_sum", i, 1, 1)
                dve.tensor_scalar(stat[:, 2:3], stat[:, 2:3], 1.0 / D, LN_EPS, ALU.mult, ALU.add).then_inc(q["ln_var"], 1)
                wait(dve, "rooted", i, 1, 1)
                c.do(dve.reciprocal(stat[:, 3:4], stat[:, 3:4]))
                c.wait()
                if not (isinstance(i, int) and i == 0):
                    dve.wait_ge(q["stored"], 16 * i)
                c.do(dve.tensor_scalar(o[:], acc[:], stat[:, 1:2], stat[:, 3:4], ALU.add, ALU.mult))
                c.wait()
                c.do(dve.tensor_tensor(o[:], o[:], lnr[:, 0], ALU.mult))
                c.wait()
                c.end()
                dve.tensor_tensor(o[:], o[:], lnr[:, 1], ALU.add).then_inc(q["out_done"], 1)

            tiles(dve, body)

        @block.scalar
        def _(act):
            def body(i):
                wait(act, "acc_done", i, 1, 1)
                act.activation(junk[:], acc[:], ACT.Identity, accum_out=stat[:, 0:1]).then_inc(q["mean_sum"], 1)
                wait(act, "mu", i, 1, 1)
                act.activation(junk[:], acc[:], ACT.Square, bias=stat[:, 1:2], accum_out=stat[:, 2:3]).then_inc(q["var_sum"], 1)
                wait(act, "ln_var", i, 1, 1)
                act.activation(stat[:, 3:4], stat[:, 2:3], ACT.Sqrt).then_inc(q["rooted"], 1)
                wait(act, "out_done", i, 1, 1)
                act.dma_start(io["out"][0, bass.ds(i * P, P)], o[:]).then_inc(q["stored"], 16)

            tiles(act, body)
            act.wait_ge(q["stored"], 16 * NT)


def program(nc, io):
    def scratch(name, shape, dt=F32):
        io[name] = nc.dram_tensor(name, shape, dt, kind="Internal").ap()

    scratch("u", [T + PADR, UW])
    scratch("yh", [L, CH])
    scratch("ys0", [L, RC + NH])
    scratch("ys1", [L, RC + NH])
    scratch("h2", [L, D])
    scratch("base", [L, D])
    scratch("block_expert", [1, P], I32)
    scratch("slot_token", [(NBLK + 1) * P, 1], I32)
    scratch("eslots", [(NBLK + 1) * P, D])
    with ExitStack() as ctx:
        def sems(name):
            return ctx.enter_context(nc.semaphore(name))

        keep = Mem(nc, ctx, "keep")
        per = {
            "ident": keep.sb("ident", [P, P]),
            "rows": keep.sb("rows", [P, 4 * D]),
            "cols": keep.sb("cols", [P, 16, 2]),
            "gates": keep.sb("gates", [P, NT, TOPK]),
            "slots_i": keep.sb("slots_i", [P, NT, TOPK], U32),
            "coef_now": keep.sb("coef_now", [P, 4]),
            "wd": keep.sb("wd", [P, T]),
            "ad": keep.sb("ad", [P, T]),
            "gd": keep.sb("gd", [P, T]),
        }
        id_in = sems("id_in")
        with nc.Block() as block:
            @block.sync
            def _(sp):
                sp.dma_start(per["ident"][:], io["ident"]).then_inc(id_in, 16)
                sp.wait_ge(id_in, 16)
        phases = [modulate, project, hyena, scan, merge, experts, combine]
        for phase in phases:
            own = []

            def sems_of_phase(name, own=own, tag=phase.__name__):
                own.append(nc.alloc_semaphore(f"{tag}_{name}"))
                return own[-1]

            phase(nc, sems_of_phase, io, per)
            nc.clear_and_free_semaphores(own)
            nc.all_engine_barrier()


def shape_constants():
    w = (np.arange(L) + 0.5) * np.pi / L
    n = np.arange(L)
    half = np.outer(n + 0.5, w)
    full = np.outer(n, w)
    col = lambda a: np.ascontiguousarray(a.reshape(8, P, 8, P).transpose(2, 1, 0, 3))
    con = {
        "ident": np.eye(P),
        "dft_cos": np.cos(half).reshape(8, P, L).transpose(1, 0, 2),
        "dft_sin": np.sin(half).reshape(8, P, L).transpose(1, 0, 2),
        "fil_cos": col(np.cos(full)),
        "fil_sin": col(-np.sin(full)),
    }
    t = np.linspace(0.0, 1.0, L)
    bands = np.linspace(1e-4, 15, 16)
    ang = (2.0 * np.pi / L) * n[:, None] * bands[None]
    con["posT"] = np.concatenate([t[:, None], np.cos(ang), -np.sin(ang)], 1).T
    deltas = np.abs(np.linspace(math.log(1e-2) / 1.5, math.log(1e-2) / 0.3, CH))
    dec = np.exp(-t[:, None] * deltas[None]) / L
    dec1 = dec.copy()
    dec1[0] = 0.0
    con["window"] = np.concatenate([dec, dec1], 1).reshape(8, P, 2 * CH).transpose(1, 0, 2)
    tri = np.zeros((P, 2, C))
    i = np.arange(C)
    tri[:C, 0] = i[:, None] <= i[None]
    tri[:C, 1] = i[:, None] < i[None]
    tri[C:, 0] = i[:, None] >= i[None]
    tri[C:, 1] = i[:, None] > i[None]
    con["tri"] = tri * LD
    con["tot"] = np.full((P, 1), LD)
    am = np.zeros((P, 2, C))
    am[:, 0] = tri[:, 1]
    am[:, 1] = tri[:, 0]
    con["causal"] = (am != 0)
    lv = np.zeros((P, 7, C))
    for s in range(6):
        same = (i[:, None] // 2 ** (s + 1)) == (i[None] // 2 ** (s + 1))
        off = same & ((i[:, None] // 2 ** s) != (i[None] // 2 ** s))
        diag = (i[:, None] == i[None]) & (s > 0)
        lv[:C, s] = (off & (i[:, None] > i[None])) | diag
        lv[C:, s] = (off & (i[:, None] < i[None])) | diag
    lv[:C, 6] = lv[:C, 0].T + np.eye(C)
    lv[C:, 6] = lv[C:, 0].T + np.eye(C)
    con["level"] = lv
    eye2 = np.zeros((P, C))
    eye2[:C] = np.eye(C)
    eye2[C:] = np.eye(C)
    con["eye2"] = eye2
    con["rank_tri"] = (np.arange(P)[:, None] < np.arange(P)[None])
    con["iota_e"] = np.tile(np.arange(NE), (P, 1))
    con["iota_p"] = np.arange(P)[:, None]
    con["thresh"] = np.tile(np.arange(8) * P, (P, 1))
    return {k: np.ascontiguousarray(v, np.float32) for k, v in con.items()}


def layout(a):
    g = {k: np.asarray(v) for k, v in a.items()}
    v = {k: x[0] for k, x in g.items() if k not in ("c", "c_ctx", "x", "ctx")}
    both = np.concatenate([g["ctx"][0], g["x"][0]], 0)
    cols = lambda r, k: r.reshape(k, P).T
    coef = np.zeros((P, 27, 4), np.float32)
    coef[:, :6, 1] = 1.0
    for j in range(3):
        coef[:, 6:12, j] = cols(v["hy_sconv_w"][j], 6)
    coef[:, 6:12, 3] = cols(v["hy_sconv_b"], 6)
    coef[:, 12:, 0] = cols(v["rw_mu"][0], 15)
    coef[:, 12:, 1] = 1.0
    coef[:, 12:, 2] = cols(v["rw_mu"][1], 15)
    two = lambda a: np.concatenate([np.broadcast_to(a[0], (C, RC)), np.broadcast_to(a[1], (C, RC))], 0)
    out = {
        "c_cols": np.stack([cols(g["c"][0], KD), cols(g["c_ctx"], KD)], 2),
        "w_ada": v["w_ada"],
        "b_cols": cols(v["b_ada"][:2 * D], 16),
        "b_rows": v["b_ada"][2 * D:],
        "hT": both.T.reshape(KD, P, T).transpose(1, 0, 2),
        "x": g["x"][0],
        "w_in": v["w_in"].reshape(KD, P, 27, P).transpose(2, 1, 0, 3),
        "coef": coef,
        "hf_w1": v["hf_w1"], "hf_w2": v["hf_w2"], "hf_w3": v["hf_w3"],
        "hf_b": np.stack([v["hf_b1"], v["hf_b2"], v["hf_b3"], v["hf_freq"]], 1),
        "hf_wout": v["hf_wout"],
        "hf_skip": v["hf_skip"].reshape(-1),
        "w0": two(v["rw_w0"]), "a0": two(v["rw_a0"]),
        "w_up": v["rw_w_up"].reshape(P, RC), "a_up": v["rw_a_up"].reshape(P, RC),
        "g_up": v["rw_g_up"],
        "rw_rows": np.concatenate([v["rw_k_k"], v["rw_k_a"], v["rw_r_k"].reshape(-1)]),
        "mix_rows": np.concatenate([v["conv_a"].reshape(-1), v["mix_norm_g"], v["rw_lnx_g"], v["rw_lnx_b"]]),
        "w_out": v["w_out"].reshape(KD, P, D).transpose(1, 0, 2),
        "ln_rows": np.concatenate([v["ln_g"][0], v["ln_b"][0], v["ln_g"][1], v["ln_b"][1]]),
        "w_router": v["w_router"].reshape(KD, P, NE).transpose(1, 0, 2),
        "e_bias": v["e_bias"],
        "w_e_gate": v["w_e_gate"], "w_e_up": v["w_e_up"], "w_e_down": v["w_e_down"],
        "w_s_gu": np.concatenate([v["w_s_gate"], v["w_s_up"]], 1).reshape(KD, P, 2 * FF).transpose(1, 0, 2),
        "w_s_down": v["w_s_down"].reshape(2, P, D).transpose(1, 0, 2),
    }
    out.update(shape_constants())
    return {k: np.ascontiguousarray(x) for k, x in out.items()}


def kernel(**inputs):
    import concourse.bacc as bacc
    from concourse.bass_utils import run_bass_kernel_spmd

    nc = bacc.Bacc("TRN2", target_bir_lowering=False, num_devices=1)
    arrays = {f"in_{k}": v for k, v in layout(inputs).items()}
    io = {k[3:]: nc.dram_tensor(k, v.shape, mybir.dt.from_np(v.dtype), kind="ExternalInput").ap() for k, v in arrays.items()}
    io["out"] = nc.dram_tensor("out_0", [1, L, D], F32, kind="ExternalOutput").ap()
    program(nc, io)
    r = run_bass_kernel_spmd(nc, [arrays], core_ids=[0])
    return r.results[0]["out_0"]
```

```python
from contextlib import ExitStack

import math

import numpy as np

import concourse.bass as bass
from concourse import mybir

F32 = mybir.dt.float32
I32 = mybir.dt.int32
U32 = mybir.dt.uint32
ALU = mybir.AluOpType
ACT = mybir.ActivationFunctionType
AX_X = mybir.AxisListType.X

P = 128
D = 1024
KD = D // P
L = 1024
LC = 256
T = L + LC
NT = L // P
GRID = 64
NE = 64
TOPK = 8
FF = 256
NBLK = NE + L * TOPK // P - 1
HD = 64
NH = 8
RC = NH * HD
CH = 256
UW = 6 * CH + 3 * RC
PADR = GRID
ALPHA = 2.0 ** 0.25
LN_EPS = 1e-5
GN_EPS = 64e-5
ROUTED = 2.5
C = 64
LD = -math.exp(-0.5)
TWO_PI = 2.0 * math.pi
MAGIC = 1.5 * 2.0 ** 23


class Mem:

    def __init__(self, nc, ctx, tag):
        self.nc, self.ctx, self.tag = nc, ctx, tag

    def sb(self, name, shape, dt=F32):
        return self.ctx.enter_context(self.nc.sbuf_tensor(f"{self.tag}_{name}", shape, dt))

    def ps(self, name, cols=512):
        return self.ctx.enter_context(self.nc.psum_tensor(f"{self.tag}_{name}", [P, cols], F32))


class Count:

    def __init__(self, sem):
        self.sem, self.n = sem, 0

    def inc(self, ins, by=1):
        ins.then_inc(self.sem, by)
        self.n += by
        return self.n


def bc(ap, at, n):
    shape = list(ap.shape)
    u = ap.unsqueeze(at)
    return u.broadcast_to(shape[:at] + [n] + shape[at:])


def modulate(nc, sems, io, per):
    with ExitStack() as ctx:
        m = Mem(nc, ctx, "mod")
        NG = 12
        cc = m.sb("cc", [P, KD, 2])
        sg = m.sb("sg", [P, KD, 2])
        sc = m.sb("sc", [P, KD, 2])
        scb = m.sb("scb", [P, KD, P])
        bcol = m.sb("bcol", [P, 16])
        w = [m.sb(f"w{s}", [P, KD, 512]) for s in range(2)]
        cps = m.ps("cps")
        rps = [m.ps(f"rps{s}") for s in range(2)]
        c_in, w_in, acted, prepared, dve_did = (sems(x) for x in ("c_in", "w_in0", "acted", "prepared", "dve_did"))
        w_in = [w_in, sems("w_in1")]
        used = sems("ada_used")
        b_in = sems("b_in")
        block = ctx.enter_context(nc.Block())

        @block.sync
        def _(sp):
            sp.dma_start(cc[:], io["c_cols"]).then_inc(c_in, 16)
            for g in range(NG):
                if g >= 2:
                    sp.wait_ge(used, g - 1)
                sp.dma_start(w[g % 2][:], io["w_ada"][:, g * 512:(g + 1) * 512]
                             .rearrange("(k p) n -> p k n", p=P)).then_inc(w_in[g % 2], 16)

        @block.scalar
        def _(act):
            act.dma_start(bcol[:], io["b_cols"]).then_inc(b_in, 16)
            act.dma_start(per["rows"][:], io["b_rows"].partition_broadcast(P)).then_inc(b_in, 16)
            act.wait_ge(c_in, 16)
            act.activation(sg[:], cc[:], ACT.Sigmoid).then_inc(acted, 1)

        @block.vector
        def _(dve):
            dve.wait_ge(acted, 1)
            dve.tensor_tensor(sc[:], cc[:], sg[:], ALU.mult).then_inc(dve_did, 1)
            dve.wait_ge(dve_did, 1)
            dve.tensor_copy(scb[:], bc(sc[:, :, 0], 2, P)).then_inc(prepared, 1)
            dve.wait_ge(used, 4)
            dve.wait_ge(b_in, 32)
            dve.tensor_tensor(per["cols"][:], cps[:, 0:32].rearrange("p (m s) -> p m s", s=2),
                              bc(bcol[:], 2, 2), ALU.add).then_inc(dve_did, 1)
            dve.wait_ge(dve_did, 2)
            dve.tensor_scalar(per["cols"][:, 8:16, :], per["cols"][:, 8:16, :], 1.0, None, ALU.add)
            for g in range(4, NG):
                dve.wait_ge(used, g + 1)
                rows = per["rows"][:, (g - 4) * 512:(g - 3) * 512]
                dve.tensor_tensor(rows, rows, rps[g % 2][:], ALU.add).then_inc(dve_did, 1)
            dve.wait_ge(dve_did, 2 + NG - 4)
            dve.tensor_scalar(per["rows"][:, 2048:3072], per["rows"][:, 2048:3072], 1.0, None, ALU.add)

        @block.tensor
        def _(pe):
            pe.wait_ge(prepared, 1)
            for g in range(NG):
                pe.wait_ge(w_in[g % 2], 16 * (g // 2 + 1))
                if g < 4:
                    for q in range(4):
                        for k in range(KD):
                            mm = pe.matmul(cps[:, 2 * (4 * g + q):2 * (4 * g + q) + 2], w[g % 2][:, k, q * P:(q + 1) * P],
                                           sc[:, k, :], start=(k == 0), stop=(k == KD - 1))
                else:
                    if g >= 6:
                        pe.wait_ge(dve_did, 2 + g - 5)
                    for k in range(KD):
                        mm = pe.matmul(rps[g % 2][:], scb[:, k, :], w[g % 2][:, k, :],
                                       start=(k == 0), stop=(k == KD - 1))
                mm.then_inc(used, 1)


def project(nc, sems, io, per):
    with ExitStack() as ctx:
        m = Mem(nc, ctx, "prj")
        hT = m.sb("hT", [P, KD, T])
        w = [m.sb(f"w{s}", [P, KD, P]) for s in range(2)]
        coef = m.sb("coef", [P, 27, 4])
        uw = T + 3
        ub = [m.sb(f"ub{s}", [P, uw]) for s in range(2)]
        cv = [m.sb(f"cv{s}", [P, T]) for s in range(2)]
        ut = [m.sb(f"ut{s}", [P, 10, P]) for s in range(2)]
        zero = m.sb("zero", [GRID, 2 * CH])
        acc = [m.ps(f"acc{s}", 3 * 512) for s in range(2)]
        tp = [m.ps(f"tp{s}") for s in range(2)]
        x_in, coef_in, h_done, coef_done, zeroed, z_out = (
            sems(x) for x in ("x_in", "coef_in", "h_done", "coef_done", "zeroed", "z_out"))
        w_in, summed, copied, convolved, turned, stored = (
            [sems(f"{x}{s}") for s in range(2)] for x in ("pw_in", "summed", "copied", "convolved", "turned", "stored"))
        tp_full = sems("tp_full")
        tp_free = sems("tp_free")
        step = sems("conv_step")
        block = ctx.enter_context(nc.Block())
        LAT = [(LC + 512 * n, 512) for n in range(2)]
        TILES_LAT, TILES = 16, 24

        def parts(ctx_too):
            return ([(0, LC)] if ctx_too else []) + LAT

        def groups(ctx_too):
            return ([(0, 2)] if ctx_too else []) + [(2, 6), (6, 10)]

        def gbase(j, s, ctx_too):
            return 3 * (2 * j + s) - TILES_LAT if ctx_too else 2 * (2 * j + s)

        LOOPS = [(0, TILES_LAT // 2, False), (TILES_LAT // 2, TILES // 2, True)]

        @block.sync
        def _(sp):
            for k in range(KD):
                sp.dma_start(hT[:, k, :], io["hT"][:, k, :]).then_inc(x_in, 16)
            for lo, hi, ctx_too in LOOPS:
                with sp.Fori(lo, hi) as j:
                    for s in range(2):
                        sp.wait_ge(summed[s], j + 1)
                        sp.dma_start(w[s][:], io["w_in"][bass.ds(2 * j + s, 1)].rearrange("o p k n -> p (o k) n")
                                     ).then_inc(w_in[s], 16)
            for n in range(3):
                s = n % 2
                sp.wait_ge(summed[s], 12 + n // 2 + 1)
                sp.dma_start(w[s][:], io["w_in"][24 + n]).then_inc(w_in[s], 16)

        @block.tensor
        def _(pe):
            for s in range(2):
                pe.sem_inc(summed[s], 1)
                pe.sem_inc(turned[s], 1)
            pe.wait_ge(h_done, KD)

            def sums(s, j, ctx_too):
                pe.wait_ge(w_in[s], 16 * (j + 1))
                pe.wait_ge(copied[s], j + 1)
                for n, (t0, tn) in enumerate(parts(ctx_too)):
                    b = 512 * (n if ctx_too else n + 1)
                    for k in range(KD):
                        mm = pe.matmul(acc[s][:, b:b + tn], w[s][:, k, :], hT[:, k, t0:t0 + tn],
                                       start=(k == 0), stop=(k == KD - 1))
                mm.then_inc(summed[s], 1)

            def turns(s, j, ctx_too):
                pe.wait_ge(convolved[s], j + 2)
                for q, (a, b) in enumerate(groups(ctx_too)):
                    g = gbase(j, s, ctx_too) + q
                    pe.wait_ge(tp_free, g + 1)
                    bank = tp[(q + (s if ctx_too else 0)) % 2]
                    for t in range(a, b):
                        mm = pe.transpose(bank[:, (t - a) * P:(t - a + 1) * P], cv[s][:, t * P:(t + 1) * P],
                                          per["ident"][:])
                    mm.then_inc(tp_full, 1)
                pe.wait_ge(tp_full, gbase(j, s, ctx_too) + len(groups(ctx_too)))
                pe.sem_inc(turned[s], 1)

            for lo, hi, ctx_too in LOOPS:
                with pe.Fori(lo, hi) as j:
                    for s in range(2):
                        sums(s, j, ctx_too)
                    for s in range(2):
                        turns(s, j, ctx_too)
            for n, ctx_too in ((0, True), (1, True), (2, False)):
                sums(n % 2, 12 + n // 2, ctx_too)

        @block.scalar
        def _(act):
            act.dma_start(coef[:], io["coef"]).then_inc(coef_in, 16)
            for s in range(2):
                act.sem_inc(copied[s], 1)
            act.sem_inc(tp_free, 2)
            for s in range(2):
                act.sem_inc(stored[s], 16)

            def copy(s, j, ctx_too):
                act.wait_ge(summed[s], j + 2)
                act.wait_ge(convolved[s], j + 1)
                if ctx_too:
                    act.copy(ub[s][:, 1:1 + LC], acc[s][:, 0:LC])
                act.copy(ub[s][:, 2 + LC:2 + LC + L], acc[s][:, 512:512 + L]).then_inc(copied[s], 1)

            def out(s, j, ctx_too):
                a0 = groups(ctx_too)[0][0]
                act.wait_ge(stored[s], 16 * (j + 1))
                for q, (a, b) in enumerate(groups(ctx_too)):
                    g = gbase(j, s, ctx_too) + q
                    act.wait_ge(tp_full, g + 1)
                    act.copy(ut[s][:, a:b, :], tp[(q + (s if ctx_too else 0)) % 2][:, 0:(b - a) * P]
                             .rearrange("p (t c) -> p t c", c=P)).then_inc(tp_free, 1)
                act.wait_ge(tp_free, gbase(j, s, ctx_too) + len(groups(ctx_too)) + 2)
                act.dma_start(io["u"][a0 * P:T, bass.ds((2 * j + s) * P, P)].rearrange("(t p) c -> p t c", p=P),
                              ut[s][:, a0:10, :]).then_inc(stored[s], 16)

            for lo, hi, ctx_too in LOOPS:
                with act.Fori(lo, hi) as j:
                    for s in range(2):
                        copy(s, j, ctx_too)
                    for s in range(2):
                        out(s, j, ctx_too)
            for n, ctx_too in ((0, True), (1, True), (2, False)):
                copy(n % 2, 12 + n // 2, ctx_too)
            for s in range(2):
                act.wait_ge(stored[s], 16 * 13)

        @block.vector
        def _(dve):
            for s in range(2):
                dve.memset(ub[s][:], 0.0)
            dve.memset(zero[:], 0.0).then_inc(zeroed, 1)
            for k in range(KD):
                dve.wait_ge(x_in, 16 * KD)
                for a, b, which in ((0, LC, 1), (LC, T, 0)):
                    ins = dve.tensor_scalar(hT[:, k, a:b], hT[:, k, a:b], per["cols"][:, 8 + k, which:which + 1],
                                            per["cols"][:, k, which:which + 1], ALU.mult, ALU.add)
                ins.then_inc(h_done, 1)
            dve.wait_ge(coef_in, 16)
            dve.tensor_tensor(coef[:, 12:27, 1], coef[:, 12:27, 1], coef[:, 12:27, 0], ALU.subtract).then_inc(coef_done, 1)
            dve.wait_ge(coef_done, 1)
            dve.tensor_tensor(coef[:, 12:27, 1], coef[:, 12:27, 1], coef[:, 12:27, 2], ALU.subtract).then_inc(coef_done, 1)
            dve.wait_ge(coef_done, 2)
            for s in range(2):
                dve.sem_inc(convolved[s], 1)

            cf = m_coef = per["coef_now"]

            def conv(s, j, ctx_too, tile, n_step, out=None):
                dve.wait_ge(copied[s], j + 2)
                if out is None:
                    dve.wait_ge(turned[s], j + 1)
                    out = cv[s]
                dve.tensor_copy(cf[:], coef[:, bass.ds(tile, 1), :].rearrange("p o c -> p (o c)")).then_inc(step, 1)
                dve.wait_ge(step, n_step + 1)
                spans = ([(0, LC, 1)] if ctx_too else []) + [(LC, T, 2)]
                for a, b, sh in spans:
                    ins = dve.tensor_scalar(out[:, a:b], ub[s][:, a + sh:b + sh], cf[:, 1:2], cf[:, 3:4],
                                            ALU.mult, ALU.add)
                ins.then_inc(step, 1)
                dve.wait_ge(step, n_step + 2)
                for a, b, sh in spans:
                    ins = dve.scalar_tensor_tensor(out[:, a:b], ub[s][:, a + sh - 1:b + sh - 1], cf[:, 0:1], out[:, a:b],
                                                   ALU.mult, ALU.add)
                ins.then_inc(step, 1)
                dve.wait_ge(step, n_step + 3)
                for a, b, sh in spans:
                    ins = dve.scalar_tensor_tensor(out[:, a:b], ub[s][:, a + sh + 1:b + sh + 1], cf[:, 2:3], out[:, a:b],
                                                   ALU.mult, ALU.add)
                ins.then_inc(step, 1)
                dve.wait_ge(step, n_step + 4)
                dve.sem_inc(convolved[s], 1)

            for lo, hi, ctx_too in LOOPS:
                with dve.Fori(lo, hi) as j:
                    for s in range(2):
                        conv(s, j, ctx_too, 2 * j + s, 8 * j + 4 * s)
            for n, ctx_too in ((0, True), (1, True), (2, False)):
                conv(n % 2, 12 + n // 2, ctx_too, 24 + n, 4 * (24 + n), per[("wd", "ad", "gd")[n]])

        @block.gpsimd
        def _(pool):
            pool.wait_ge(zeroed, 1)
            pool.dma_start(io["u"][LC - GRID:LC, CH:3 * CH], zero[:]).then_inc(z_out, 16)
            pool.dma_start(io["u"][T:T + PADR, CH:3 * CH], zero[:]).then_inc(z_out, 16)
            pool.wait_ge(z_out, 32)


def hyena(nc, sems, io, per):
    with ExitStack() as ctx:
        m = Mem(nc, ctx, "hy")
        NF = 2 * CH
        z = m.sb("z", [P, NT, CH])
        x12 = m.sb("x12", [P, 2, NT, CH])
        K = m.sb("K", [P, NT, 2, 3, CH])
        tmp = m.sb("tmp", [P, 2, 2, CH])
        skip = m.sb("skip", [P, 2, CH])
        work = m.sb("work", [P, 2, CH])
        banks = [m.ps(f"bank{s}") for s in range(6)]
        v_in, fil_in, pos_in, wout_in, skip_in = (sems(x) for x in ("v_in", "fil_in", "pos_in", "wout_in", "skip_in"))
        dft_in = [sems(f"dft_in{s}") for s in range(2)]
        x_in = sems("x12_in")
        y_out = sems("yh_out")

        with ExitStack() as ctx1:
            m1 = Mem(nc, ctx1, "hf")
            pos = m1.sb("pos", [33, L])
            w1 = m1.sb("w1", [33, 64])
            w23 = m1.sb("w23", [64, 2, 64])
            hb = m1.sb("hb", [64, 4])
            wout = m1.sb("wout", [64, 4 * CH])
            win = m1.sb("win", [P, NT, NF])
            h = [m1.sb(f"h{s}", [64, L]) for s in range(2)]
            q = m1.sb("q", [64, L])
            hw = m1.sb("hw", [P, 2, NF])
            both = m1.sb("both", [P, NT, 2, NF])
            fil = [m1.sb(f"fil{s}", [P, 2, NT, P]) for s in range(2)]
            lin, mapped, stp, out_done, windowed, added, kdone, ktaken = (
                sems(x) for x in ("lin", "mapped", "step", "out_done", "windowed", "added", "kdone", "ktaken"))
            block = ctx1.enter_context(nc.Block())

            @block.sync
            def _(sp):
                for dst, src in ((pos[:], io["posT"]), (w1[:], io["hf_w1"]), (w23[:, 0, :], io["hf_w2"]),
                                 (w23[:, 1, :], io["hf_w3"]), (hb[:], io["hf_b"])):
                    sp.dma_start(dst, src).then_inc(pos_in, 16)
                sp.dma_start(wout[:], io["hf_wout"]).then_inc(wout_in, 16)
                sp.dma_start(win[:], io["window"]).then_inc(wout_in, 16)
                for f in range(NT):
                    if f >= 2:
                        sp.wait_ge(kdone, f - 1)
                    sp.dma_start(fil[f % 2][:, 0], io["fil_cos"][f]).then_inc(dft_in[f % 2], 16)
                    sp.dma_start(fil[f % 2][:, 1], io["fil_sin"][f]).then_inc(dft_in[f % 2], 16)

            @block.tensor
            def _(pe):
                pe.wait_ge(pos_in, 80)
                for layer in range(3):
                    if layer:
                        pe.wait_ge(mapped, layer)
                    for n in range(2):
                        lhsT = w1[:] if layer == 0 else w23[:, layer - 1, :]
                        rhs = pos[:, n * 512:(n + 1) * 512] if layer == 0 else h[(layer - 1) % 2][:, n * 512:(n + 1) * 512]
                        mm = pe.matmul(banks[n][0:64, :], lhsT, rhs, start=True, stop=True)
                    mm.then_inc(lin, 1)
                pe.wait_ge(mapped, 3)
                pe.wait_ge(wout_in, 32)
                for t in range(NT):
                    for o in range(2):
                        n = 2 * t + o
                        if n >= 2:
                            pe.wait_ge(windowed, n - 1)
                        pe.matmul(banks[2 + n % 2][:], h[0][:, t * P:(t + 1) * P], wout[:, o * NF:(o + 1) * NF],
                                  start=True, stop=True).then_inc(out_done, 1)
                pe.wait_ge(added, 4 * NT)
                for f in range(NT):
                    pe.wait_ge(dft_in[f % 2], 32 * (f // 2 + 1))
                    if f >= 2:
                        pe.wait_ge(ktaken, 3 * (f - 1))
                    for part in range(2):
                        for t in range(NT):
                            mm = pe.matmul(banks[2 * (f % 2) + part][:], fil[f % 2][:, part, t, :], both[:, t, part, :],
                                           start=(t == 0), stop=(t == NT - 1))
                    mm.then_inc(kdone, 1)

            @block.vector
            def _(dve):
                st = Count(stp)
                for layer in range(3):
                    dve.wait_ge(lin, layer + 1)
                    src = banks
                    dst = h[layer % 2]
                    for n in range(2):
                        v = st.inc(dve.tensor_scalar(dst[:, n * 512:(n + 1) * 512], src[n][0:64, :], hb[:, layer:layer + 1],
                                                     hb[:, 3:4], ALU.add, ALU.mult))
                    dve.wait_ge(stp, v)
                    dve.wait_ge(stp, st.inc(dve.tensor_scalar(q[:], dst[:], 1.0 / TWO_PI, MAGIC, ALU.mult, ALU.add)))
                    dve.wait_ge(stp, st.inc(dve.tensor_scalar(q[:], q[:], MAGIC, None, ALU.subtract)))
                    dve.wait_ge(stp, st.inc(dve.scalar_tensor_tensor(dst[:], q[:], -6.28125, dst[:], ALU.mult, ALU.add)))
                    dve.wait_ge(stp, st.inc(dve.scalar_tensor_tensor(dst[:], q[:], -(TWO_PI - 6.28125), dst[:], ALU.mult, ALU.add)))
                    st.inc(dve.tensor_scalar(dst[:], dst[:], 3.1415925, -3.1415925, ALU.min, ALU.max))
                dve.wait_ge(wout_in, 32)
                for t in range(NT):
                    for o in range(2):
                        n = 2 * t + o
                        dve.wait_ge(out_done, n + 1)
                        if n >= 2:
                            dve.wait_ge(added, 2 * (n - 1))
                        dve.tensor_tensor(hw[:, n % 2, :], banks[2 + n % 2][:], win[:, t, :], ALU.mult).then_inc(windowed, 1)
                        dve.wait_ge(windowed, n + 1)
                        for part, op in ((0, ALU.add), (1, ALU.subtract)):
                            dve.tensor_tensor(both[:, t, part, o * CH:(o + 1) * CH], hw[:, n % 2, 0:CH], hw[:, n % 2, CH:NF],
                                              op).then_inc(added, 1)

            @block.scalar
            def _(act):
                act.dma_start(z[:], io["u"][LC:T, 3 * CH:4 * CH].rearrange("(t p) c -> p t c", p=P)).then_inc(v_in, 16)
                for o in range(2):
                    act.dma_start(x12[:, o], io["u"][LC:T, (4 + o) * CH:(5 + o) * CH].rearrange("(t p) c -> p t c", p=P)
                                  ).then_inc(x_in, 16)
                act.dma_start(skip[:].rearrange("p o c -> p (o c)"), io["hf_skip"].partition_broadcast(P)).then_inc(skip_in, 16)
                for layer in range(3):
                    act.wait_ge(stp, 7 * layer + 7)
                    act.activation(h[layer % 2][:], h[layer % 2][:], ACT.Sin).then_inc(mapped, 1)
                for f in range(NT):
                    act.wait_ge(kdone, f + 1)
                    for part, kinds in ((0, (0, 2)), (1, (1,))):
                        for kind in kinds:
                            act.copy(K[:, f, :, kind, :], banks[2 * (f % 2) + part][:].rearrange("p (o c) -> p o c", o=2)
                                     ).then_inc(ktaken, 1)
                act.wait_ge(v_in, 16)
                act.wait_ge(x_in, 32)
                act.wait_ge(skip_in, 16)
                act.wait_ge(ktaken, 3 * NT)

        with ExitStack() as ctx2:
            m2 = Mem(nc, ctx2, "hc")
            E = m2.sb("E", [P, NT, CH])
            F = m2.sb("F", [P, NT, CH])
            M = [m2.sb("cos", [P, NT, L]), m2.sb("sin", [P, NT, L])]
            fwd, mixed, inv, gated, stp = (sems(x) for x in ("fwd", "mixed", "inv", "gated", "cstep"))
            tab_in = sems("tab_in")
            block = ctx2.enter_context(nc.Block())

            @block.sync
            def _(sp):
                for t in range(NT):
                    sp.dma_start(M[0][:, t], io["dft_cos"][:, t]).then_inc(tab_in, 16)
                    sp.dma_start(M[1][:, t], io["dft_sin"][:, t]).then_inc(tab_in, 16)
                sp.wait_ge(gated, 2 * NT)
                sp.dma_start(io["yh"].rearrange("(t p) c -> p t c", p=P), z[:]).then_inc(y_out, 16)
                sp.wait_ge(y_out, 16)

            @block.tensor
            def _(pe):
                pe.wait_ge(tab_in, 32 * NT)
                for o in range(2):
                    if o:
                        pe.wait_ge(gated, NT)
                    for f in range(NT):
                        n = NT * o + f
                        if n >= 2:
                            pe.wait_ge(mixed, n - 1)
                        for part in range(2):
                            for t in range(NT):
                                mm = pe.matmul(banks[n % 2][:, part * CH:(part + 1) * CH], M[part][:, t, f * P:(f + 1) * P],
                                               z[:, t, :], start=(t == 0), stop=(t == NT - 1))
                        mm.then_inc(fwd, 1)
                    pe.wait_ge(mixed, NT * (o + 1))
                    for t in range(NT):
                        n = NT * o + t
                        if n >= 2:
                            pe.wait_ge(gated, n - 1)
                        for f in range(NT):
                            for part, src in ((0, E), (1, F)):
                                mm = pe.matmul(banks[2 + n % 2][:, 0:CH], M[part][:, f, t * P:(t + 1) * P], src[:, f, :],
                                               start=(f == 0 and part == 0), stop=(f == NT - 1 and part == 1))
                        mm.then_inc(inv, 1)

            @block.vector
            def _(dve):
                st = Count(stp)
                for o in range(2):
                    for f in range(NT):
                        n = NT * o + f
                        dve.wait_ge(fwd, n + 1)
                        pq = banks[n % 2][:].rearrange("p (a c) -> p a c", a=2)
                        st.inc(dve.tensor_tensor(tmp[:, 0], pq, K[:, f, o, 0:2, :], ALU.mult))
                        v = st.inc(dve.tensor_tensor(tmp[:, 1], pq, K[:, f, o, 1:3, :], ALU.mult))
                        dve.wait_ge(stp, v)
                        st.inc(dve.tensor_tensor(E[:, f, :], tmp[:, 0, 0, :], tmp[:, 0, 1, :], ALU.add))
                        dve.tensor_tensor(F[:, f, :], tmp[:, 1, 1, :], tmp[:, 1, 0, :], ALU.subtract).then_inc(mixed, 1)
                        dve.wait_ge(mixed, n + 1)
                        dve.wait_ge(stp, st.n)
                    for t in range(NT):
                        n = NT * o + t
                        v = st.inc(dve.tensor_tensor(work[:, 0], z[:, t, :], skip[:, o, :], ALU.mult))
                        dve.wait_ge(inv, n + 1)
                        dve.wait_ge(stp, v)
                        dve.wait_ge(stp, st.inc(dve.tensor_tensor(work[:, 1], work[:, 0], banks[2 + n % 2][:, 0:CH], ALU.add)))
                        dve.tensor_tensor(z[:, t, :], work[:, 1], x12[:, o, t, :], ALU.mult).then_inc(gated, 1)
                        dve.wait_ge(gated, n + 1)


NSTEP = T // C


def scan(nc, sems, io, per):
    with ExitStack() as ctx:
        m = Mem(nc, ctx, "sc")
        H2 = NH // 2
        lora = m.sb("lora", [P, NSTEP, 2, C])
        lnow = m.sb("lnow", [P, 2, 2, C])
        w_up = m.sb("w_up", [P, RC])
        a_up = m.sb("a_up", [P, RC])
        wa0 = m.sb("wa0", [P, 2, RC])
        rows = m.sb("rows", [P, 3, RC])
        tri = m.sb("tri", [P, P])
        tot = m.sb("tot", [P, 2])
        causal = m.sb("causal", [P, H2, 2, 2, C])
        level = m.sb("level", [P, 6, C])
        levelbd = m.sb("levelbd", [P, 6, 2, C])
        eye = m.sb("eye", [P, C])
        rkv = [m.sb(f"rkv{s}", [P, 3, RC]) for s in range(2)]
        sig = m.sb("sig", [P, 2, RC])
        e_in, e_ng, e_ex = (m.sb(x, [P, RC]) for x in ("e_in", "e_ng", "e_ex"))
        kkr, sq, kk, kka, krest, rrk, akk, kd = (
            m.sb(x, [P, RC]) for x in ("kkr", "sq", "kk", "kka", "krest", "rrk", "akk", "kd"))
        ss, rn = m.sb("ss", [P, NH]), m.sb("rn", [P, NH])
        alpha, rho = m.sb("alpha", [P, RC]), m.sb("rho", [P, RC])
        beta = [m.sb(f"beta{s}", [P, NH, 2, HD]) for s in range(2)]
        kap = [m.sb(f"kap{s}", [P, NH, 2, HD]) for s in range(2)]
        arT = m.sb("arT", [P, NH, 2, C])
        arb = m.sb("arb", [P, NH, 2, 2, C])
        bT = m.sb("bT", [P, NH, P])
        kT = m.sb("kT", [P, NH, P])
        dec = [m.sb(f"dec{s}", [P, NH]) for s in range(2)]
        ab = [m.sb(f"ab{s}", [P, NH, 2, P]) for s in range(2)]
        ak = [m.sb(f"ak{s}", [P, NH, 2, P]) for s in range(2)]
        abi = m.sb("abi", [P, NH, P])
        dd = m.sb("dd", [P, 2, 2, H2 * C])
        dtb = m.sb("dtb", [P, NH, 2, C])
        xm = m.sb("xm", [P, 2, H2 * C])
        xb = m.sb("xb", [P, NH, 2, C])
        eyebd = per["ident"]
        gs = m.sb("gs", [P, RC])
        us = m.sb("us", [P, RC])
        st = m.sb("st", [P, RC])
        sm = m.sb("sm", [P, RC])
        yb = [m.sb(f"yb{s}", [P, RC + NH]) for s in range(2)]
        B = [m.ps(f"B{n}") for n in range(8)]

        con_in = sems("con_in")
        rk_in, v_in = ([sems(f"{x}{s}") for s in range(2)] for x in ("rk_in", "v_in"))
        names = ("lora_ready lora_now lora_sum pre_done less_done sig_done cum_done exp_done pool_k ssd clamped rooted rnd kk_done akk_done "
                 "kd_done kd_part op_done turned_up tev_a tev_b tev_r tev_k arb_done a_sum a_masked abi_done adir d0 dt0 dtb0 xb_done z_sum x_done d_sum "
                 "d_copied d5_copied g_sum g_copied u_sum u_copied s_sum s_added s_done y_sum y_copied bon_m bon_done zeroed0 zeroed1 zeroed2 passed passed_sp")
        q = {x: sems(x) for x in names.split()}
        y_out = [sems(f"y_out{s}") for s in range(2)]
        block = ctx.enter_context(nc.Block())
        K = (slice(0, 64), slice(64, 128))

        def wait(eng, name, c, per_step, k):
            v = c * per_step + k
            if not (isinstance(v, int) and v <= 0):
                eng.wait_ge(q[name], v)
                if eng is nc.tensor and not isinstance(v, int):
                    eng.sem_inc(q["passed"], 1)

        def hd(h):
            return slice(h * C, (h + 1) * C)

        def half(ap, g):
            return ap[:, g * H2 * C:(g + 1) * H2 * C]

        @block.sync
        def _(sp):
            for dst, src in ((w_up[:], io["w_up"]), (a_up[:], io["a_up"]), (wa0[:, 0], io["w0"]), (wa0[:, 1], io["a0"]),
                             (rows[:].rearrange("p a c -> p (a c)"), io["rw_rows"].partition_broadcast(P)),
                             (tri[:], io["tri"]), (tot[:], io["tot"]), (causal[:], io["causal"]), (level[:], io["level"]), (levelbd[:], io["levelbd"]),
                             (eye[:], io["eye2"])):
                sp.dma_start(dst, src).then_inc(con_in, 16)

            R0 = 6 * CH

            def load_rk(c, s, t_back, context):
                wait(sp, "op_done", c - 2, 6, 6)
                wait(sp, "pool_k", c - 2, 5, 5)
                sp.sem_inc(q["passed_sp"], 1)
                for d, t in ((0, c * C), (1, t_back)):
                    src = io["u"][bass.ds(t, C)]
                    sp.dma_start(rkv[s][K[d], 1, :], src[:, R0 + RC:R0 + 2 * RC]).then_inc(rk_in[s], 16)
                    r = src[:, R0 + RC:R0 + 2 * RC] if context else src[:, R0:R0 + RC]
                    sp.dma_start(rkv[s][K[d], 0, :], r).then_inc(rk_in[s], 16)

            def load_v(c, s, t_back):
                wait(sp, "y_sum", c - 2, 2, 2)
                sp.sem_inc(q["passed_sp"], 1)
                for d, t in ((0, c * C), (1, t_back)):
                    sp.dma_start(rkv[s][K[d], 2, :], io["u"][bass.ds(t, C), R0 + 2 * RC:R0 + 3 * RC]).then_inc(v_in[s], 16)

            def store(c, s, t_back):
                sp.wait_ge(q["y_copied"], 2 * c + 2)
                sp.sem_inc(q["passed_sp"], 1)
                sp.wait_ge(q["bon_done"], c + 1)
                sp.sem_inc(q["passed_sp"], 1)
                sp.dma_start(io["ys0"][bass.ds(c * C - LC, C)], yb[s][K[0], :]).then_inc(y_out[s], 16)
                sp.dma_start(io["ys1"][bass.ds(t_back - LC, C)], yb[s][K[1], :]).then_inc(y_out[s], 16)

            NC = LC // C
            back = lambda c: LC - C * (c + 1) if c < NC else T + LC - C * (c + 1)
            for c in range(2):
                load_rk(c, c, back(c), True)
                load_v(c, c, back(c))

            def turn(c, s):
                t = T + LC - C - C * c
                load_rk(c + 2, s, t - 2 * C, False)
                load_v(c + 1, 1 - s, t - C)
                store(c - 1, 1 - s, t + C)

            for c in range(NC + 2):
                load_rk(c + 2, c % 2, back(c + 2), c + 2 < NC)
                if c > 0:
                    load_v(c + 1, 1 - c % 2, back(c + 1))
                if c > NC:
                    store(c - 1, 1 - c % 2, back(c - 1))
            with sp.Fori(NC // 2 + 1, NSTEP // 2 - 1) as j:
                for s in range(2):
                    turn(2 * j + s, s)
            load_v(NSTEP - 1, 1, back(NSTEP - 1))
            for c in range(NSTEP - 3, NSTEP):
                store(c, c % 2, back(c))
            for s in range(2):
                sp.wait_ge(y_out[s], 16 * (NSTEP - NC))

        def steps(eng, prepare_alone, both, recur_alone):
            prepare_alone(0, 0)
            for c in range(2):
                both(c, c % 2)
            with eng.Fori(1, NSTEP // 2 - 1) as j:
                for s in range(2):
                    both(2 * j + s, s)
            both(NSTEP - 2, 0)
            recur_alone(NSTEP - 1, 1)

        @block.tensor
        def _(pe):
            pe.wait_ge(con_in, 176)
            ident = per["ident"]

            def p_lora(c, s):
                wait(pe, "lora_now", c, 1, 1)
                wait(pe, "a_masked", c - 1, 4, 4)
                for i, up in ((0, w_up), (1, a_up)):
                    mm = pe.matmul(B[i][:], lnow[:, i].rearrange("p d t -> p (d t)"), up[:], start=True, stop=True)
                mm.then_inc(q["lora_sum"], 1)

            def p_cum(c, s):
                wait(pe, "sig_done", c, 1, 1)
                pe.matmul(B[2][:], tri[:], sig[:, 0, :], start=True, stop=True)
                for h in range(NH):
                    mm = pe.matmul(B[0][0:64, 2 * h:2 * h + 2], sig[:, 0, hd(h)], tot[:], start=True, stop=True)
                mm.then_inc(q["cum_done"], 1)

            def p_turn(c, s):
                wait(pe, "exp_done", c, 5, 5)
                wait(pe, "op_done", c, 6, 1)
                for p in range(4):
                    mm = pe.transpose(B[1][:, p * P:(p + 1) * P], alpha[:, p * P:(p + 1) * P], ident[:])
                mm.then_inc(q["turned_up"], 1)
                wait(pe, "op_done", c, 6, 3)
                for h in range(NH):
                    bank = (3, 0)[h // H2]
                    mm = pe.transpose(B[bank][:, (h % H2) * P:(h % H2 + 1) * P], beta[s][:, h].rearrange("p d k -> p (d k)"), ident[:])
                    if h % H2 == H2 - 1:
                        mm.then_inc(q["turned_up"], 1)
                wait(pe, "op_done", c, 6, 6)
                for p in range(4):
                    mm = pe.transpose(B[2][:, p * P:(p + 1) * P], rho[:, p * P:(p + 1) * P], ident[:])
                mm.then_inc(q["turned_up"], 1)
                for h in range(NH):
                    if h == 0:
                        wait(pe, "tev_a", c, 4, 4)
                    if h == H2:
                        wait(pe, "tev_b", c, 2, 1)
                    bank = (1, 3)[h // H2]
                    mm = pe.transpose(B[bank][:, (h % H2) * P:(h % H2 + 1) * P], kap[s][:, h].rearrange("p d k -> p (d k)"), ident[:])
                    if h % H2 == H2 - 1:
                        mm.then_inc(q["turned_up"], 1)

            def r_products(c, lhs, banks):
                wait(pe, "tev_a", c, 4, 4)
                wait(pe, "tev_b", c, 2, 2)
                wait(pe, "tev_r", c, 4, 4)
                wait(pe, "tev_k", c, 2, 2)
                for g, bank in enumerate(banks):
                    for hh in range(H2):
                        h = g * H2 + hh
                        mm = pe.matmul(B[bank][:, hh * P:(hh + 1) * P], lhs[:, h, :], arT[:, h].rearrange("k a t -> k (a t)"),
                                       start=True, stop=True)
                    mm.then_inc(q["a_sum"], 1)

            def r_direct(c, s):
                for g in range(2):
                    wait(pe, "a_masked", c, 4, g + 1)
                    wait(pe, "abi_done", c, 2, g + 1)
                    wait(pe, "s_added", c - 1, 2, g + 1)
                    for hh in range(H2):
                        mm = pe.matmul(B[6 + g][:, hd(hh)], abi[:, g * H2 + hh], eye[:], start=True, stop=True)
                    mm.then_inc(q["adir"], 1)

            def bdm(ap):
                return ap.rearrange("p d t -> p (d t)")

            def r_level(c, s, l):
                for g in range(2):
                    if l == 1:
                        wait(pe, "d0", c, 2, g + 1)
                        wait(pe, "y_copied", c - 1, 2, g + 1)
                    else:
                        wait(pe, "d_copied", c, 24, 3 * (2 * (l - 2) + g) + 1)
                    for hh in range(H2):
                        mm = pe.matmul(B[4 + g][:, hd(hh)], abi[:, g * H2 + hh], dd[:, g, 0, hd(hh)], start=True, stop=True)
                    mm.then_inc(q["z_sum"], 1)
                for g in range(2):
                    if l == 1:
                        wait(pe, "dtb0", c, 2, g + 1)
                        wait(pe, "dt0", c, 4, 2 * g + 2)
                    else:
                        wait(pe, "d_copied", c, 24, 3 * (2 * (l - 2) + g) + 3)
                    if l < 5:
                        wait(pe, "x_done", c, 10, 2 * (l - 1) + g + 1)
                        for hh in range(H2):
                            pe.matmul(B[6 + g][:, hd(hh)], bdm(dtb[:, g * H2 + hh]), xm[:, g, hd(hh)], start=True, stop=True)
                    wait(pe, "xb_done", c, 10, 2 * (l - 1) + g + 1)
                    for hh in range(H2):
                        mm = pe.matmul(B[6 + g][:, hd(H2 + hh)], bdm(xb[:, g * H2 + hh]), dd[:, g, 1, hd(hh)], start=True, stop=True)
                    mm.then_inc(q["d_sum"], 1)

            def r_g(c, s):
                V = rkv[s][:, 2, :]
                wait(pe, "s_done", c - 1, 2, 2)
                wait(pe, "arb_done", c, 2, 2)
                wait(pe, "a_masked", c, 4, 4)
                pe.wait_ge(v_in[s], 16 * (c - s) + 32)
                if isinstance(c, int) and c == 0:
                    pe.wait_ge(q["zeroed0"], 1)
                for g in range(2):
                    wait(pe, "xb_done", c, 10, 9 + g)
                    for hh in range(H2):
                        h = g * H2 + hh
                        pe.matmul(B[4 + g][:, hd(hh)], bdm(arb[:, h, 0]), st[:, hd(h)], start=True, stop=False)
                        mm = pe.matmul(B[4 + g][:, hd(hh)], ak[s][:, h, 0], V[:, hd(h)], start=False, stop=True)
                    mm.then_inc(q["g_sum"], 1)

            def r_u(c, s):
                for g in range(2):
                    wait(pe, "g_copied", c, 2, g + 1)
                    wait(pe, "d5_copied", c, 4, 2 * g + 2)
                    for hh in range(H2):
                        h = g * H2 + hh
                        mm = pe.matmul(B[6 + g][:, hd(hh)], bdm(dtb[:, h]), gs[:, hd(h)], start=True, stop=True)
                    mm.then_inc(q["u_sum"], 1)

            def r_s(c, s):
                V = rkv[s][:, 2, :]
                for g in range(2):
                    wait(pe, "u_copied", c, 2, g + 1)
                    for hh in range(H2):
                        h = g * H2 + hh
                        pe.matmul(B[6 + g][:, hd(hh)], bdm(beta[s][:, h]), us[:, hd(h)], start=True, stop=False)
                        mm = pe.matmul(B[6 + g][:, hd(hh)], bdm(kap[s][:, h]), V[:, hd(h)], start=False, stop=True)
                    mm.then_inc(q["s_sum"], 1)

            def r_y(c, s):
                V = rkv[s][:, 2, :]
                for g in range(2):
                    wait(pe, "u_copied", c, 2, g + 1)
                    for hh in range(H2):
                        h = g * H2 + hh
                        out = B[4 + g][:, hd(hh)]
                        pe.matmul(out, bdm(arb[:, h, 1]), st[:, hd(h)], start=True, stop=False)
                        pe.matmul(out, ab[s][:, h, 1], us[:, hd(h)], start=False, stop=False)
                        mm = pe.matmul(out, ak[s][:, h, 1], V[:, hd(h)], start=False, stop=True)
                    mm.then_inc(q["y_sum"], 1)

            def prepare(c, s):
                p_lora(c, s)
                p_cum(c, s)
                p_turn(c, s)
                r_products(c, bT, (2, 3))
                r_products(c, kT, (0, 1))

            def both(c, s):
                r_direct(c, s)
                p_lora(c + 1, 1 - s)
                r_level(c, s, 1)
                r_level(c, s, 2)
                r_level(c, s, 3)
                p_cum(c + 1, 1 - s)
                r_level(c, s, 4)
                r_level(c, s, 5)
                r_g(c, s)
                p_turn(c + 1, 1 - s)
                r_u(c, s)
                r_s(c, s)
                r_products(c + 1, bT, (2, 3))
                r_products(c + 1, kT, (0, 1))
                r_y(c, s)

            def recur(c, s):
                r_direct(c, s)
                for l in range(1, 6):
                    r_level(c, s, l)
                r_g(c, s)
                r_u(c, s)
                r_y(c, s)

            steps(pe, prepare, both, recur)

        @block.scalar
        def _(act):
            act.activation(lora[K[0], :, 0, :], per["wd"][K[0], :].rearrange("r (c t) -> r c t", t=C), ACT.Tanh)
            ins = act.copy(lora[K[0], :, 1, :], per["ad"][K[0], :].rearrange("r (c t) -> r c t", t=C))
            for c in range(NSTEP):
                t = LC - C * (c + 1) if c < LC // C else T + LC - C * (c + 1)
                act.activation(lora[K[1], c, 0, :], per["wd"][K[1], t:t + C], ACT.Tanh)
                ins = act.copy(lora[K[1], c, 1, :], per["ad"][K[1], t:t + C])
            ins.then_inc(q["lora_ready"], 1)
            act.wait_ge(q["lora_ready"], 1)

            def a_lora(c, s):
                wait(act, "lora_sum", c - 1, 1, 1)
                for d in range(2):
                    ins = act.copy(lnow[K[d], :, d, :], lora[K[d], bass.ds(c, 1)].rearrange("p o a t -> p (o a) t"))
                ins.then_inc(q["lora_now"], 1)

            def a_sig(c, s):
                wait(act, "pre_done", c, 2, 2)
                act.activation(sig[:], sig[:], ACT.Sigmoid).then_inc(q["sig_done"], 1)

            def a_root(c, s):
                wait(act, "clamped", c, 1, 1)
                wait(act, "kk_done", c - 1, 1, 1)
                act.activation(rn[:], ss[:], ACT.Sqrt).then_inc(q["rooted"], 1)

            def a_exp(c, s):
                wait(act, "cum_done", c, 1, 1)
                wait(act, "op_done", c - 1, 6, 6)
                wait(act, "less_done", c, 1, 1)
                act.activation(e_in[:], B[2][:], ACT.Exp).then_inc(q["exp_done"], 1)
                act.activation(e_ng[:], B[2][:], ACT.Exp, scale=-1.0).then_inc(q["exp_done"], 1)
                act.activation(e_ex[:], e_ex[:], ACT.Exp).then_inc(q["exp_done"], 1)
                wait(act, "s_done", c - 2, 2, 2)
                for d in range(2):
                    act.activation(dec[s][K[d], :], B[0][0:64, 0:2 * NH].rearrange("k (h d) -> k h d", d=2)[:, :, d], ACT.Exp
                                   ).then_inc(q["exp_done"], 1)

            def turn_copies(eng, copy, c, s, bank, dst, sem):
                v = B[bank][:].rearrange("p (a d t) -> p a d t", a=4, d=2)
                for par in range(2):
                    for d in range(2):
                        copy(dst(d, par), v[K[par], :, d, :]).then_inc(q[sem], 1)

            def a_turn(c, s):
                wait(act, "arb_done", c - 1, 2, 2)
                wait(act, "turned_up", c, 6, 1)
                turn_copies(act, act.copy, c, s, 1, lambda d, par: arT[K[d], par::2, 0, :], "tev_a")
                wait(act, "turned_up", c, 6, 4)
                turn_copies(act, act.copy, c, s, 2, lambda d, par: arT[K[d], par::2, 1, :], "tev_r")

            def a_arb(c, s):
                wait(act, "y_sum", c - 1, 2, 2)
                wait(act, "tev_r", c, 4, 4)
                for d in range(2):
                    act.copy(arb[K[d], :, :, d, :].rearrange("p h a t -> p (h a) t"), arT[K[d]].rearrange("p h a t -> p (h a) t")
                             ).then_inc(q["arb_done"], 1)

            def a_level(c, s, l):
                for g in range(2):
                    wait(act, "d_sum", c, 10, 2 * (l - 1) + g + 1)
                    if l < 5:
                        act.copy(dd[:, g].rearrange("p a x -> p (a x)"), B[6 + g][:]).then_inc(q["d_copied"], 1)
                    for d in range(2):
                        act.copy(dtb[K[d], g * H2:(g + 1) * H2, d, :], B[6 + g][K[d], H2 * C:].rearrange("p (h t) -> p h t", h=H2)
                                 ).then_inc(q["d_copied" if l < 5 else "d5_copied"], 1)

            def a_g(c, s):
                for g in range(2):
                    wait(act, "g_sum", c, 2, g + 1)
                    act.copy(half(gs, g), B[4 + g][:, 0:H2 * C]).then_inc(q["g_copied"], 1)

            def a_state(c, s):
                for g in range(2):
                    wait(act, "u_sum", c, 2, g + 1)
                    act.copy(half(us, g), B[6 + g][:, 0:H2 * C]).then_inc(q["u_copied"], 1)
                y_free(c, s)
                for g in range(2):
                    wait(act, "y_sum", c, 2, g + 1)
                    act.copy(yb[s][:, g * H2 * C:(g + 1) * H2 * C], B[4 + g][:, 0:H2 * C]).then_inc(q["y_copied"], 1)

            def y_free(c, s):
                v = 16 * (c - s - LC // C)
                if not (isinstance(v, int) and v <= 0):
                    act.wait_ge(y_out[s], v)

            def prepare(c, s):
                a_lora(c, s)
                a_sig(c, s)
                a_root(c, s)
                a_exp(c, s)
                a_turn(c, s)

            def both(c, s):
                a_lora(c + 1, 1 - s)
                a_arb(c, s)
                a_level(c, s, 1)
                a_sig(c + 1, 1 - s)
                a_root(c + 1, 1 - s)
                a_level(c, s, 2)
                a_level(c, s, 3)
                a_exp(c + 1, 1 - s)
                a_level(c, s, 4)
                a_level(c, s, 5)
                a_g(c, s)
                a_turn(c + 1, 1 - s)
                a_state(c, s)

            def recur(c, s):
                a_arb(c, s)
                for l in range(1, 6):
                    a_level(c, s, l)
                a_g(c, s)
                a_state(c, s)

            act.wait_ge(q["zeroed1"], 2)
            act.wait_ge(q["zeroed2"], 5)
            prepare(0, 0)
            for c in range(6):
                both(c, c % 2)
            with act.Fori(3, NSTEP // 2 - 1) as j:
                for s in range(2):
                    both(2 * j + s, s)
            both(NSTEP - 2, 0)
            recur(NSTEP - 1, 1)

        @block.gpsimd
        def _(pool):
            pool.memset(lnow[:], 0.0).then_inc(q["zeroed1"], 1)
            pool.memset(dtb[:], 0.0).then_inc(q["zeroed1"], 1)
            pool.memset(arb[:], 0.0).then_inc(q["zeroed2"], 1)
            for s in range(2):
                pool.memset(beta[s][:], 0.0).then_inc(q["zeroed2"], 1)
                pool.memset(kap[s][:], 0.0).then_inc(q["zeroed2"], 1)
            pool.wait_ge(q["zeroed2"], 5)
            pool.wait_ge(con_in, 176)

            def keys(c, s):
                k = rkv[s][:, 1, :]
                pool.wait_ge(rk_in[s], 32 * (c - s) + 64)
                wait(pool, "kk_done", c - 1, 1, 1)
                pool.tensor_tensor(kkr[:], k, rows[:, 0, :], ALU.mult).then_inc(q["pool_k"], 1)
                wait(pool, "pool_k", c, 5, 1)
                wait(pool, "ssd", c - 1, 1, 1)
                pool.tensor_tensor(sq[:], kkr[:], kkr[:], ALU.mult).then_inc(q["pool_k"], 1)
                wait(pool, "kd_done", c - 1, 1, 1)
                pool.tensor_tensor(kka[:], k, rows[:, 1, :], ALU.mult).then_inc(q["pool_k"], 1)
                wait(pool, "pool_k", c, 5, 3)
                pool.tensor_tensor(krest[:], k, kka[:], ALU.subtract).then_inc(q["pool_k"], 1)
                wait(pool, "bon_done", c - 1, 1, 1)
                pool.tensor_tensor(rrk[:], rkv[s][:, 0, :], rows[:, 2, :], ALU.mult).then_inc(q["pool_k"], 1)

            def rate(c, s):
                wait(pool, "sig_done", c, 1, 1)
                wait(pool, "kk_done", c, 1, 1)
                wait(pool, "op_done", c - 1, 6, 3)
                pool.tensor_tensor(akk[:], sig[:, 1], kk[:], ALU.mult).then_inc(q["akk_done"], 1)
                wait(pool, "pool_k", c, 5, 5)
                wait(pool, "kd_done", c, 1, 1)
                pool.tensor_tensor(rrk[:], rrk[:], kd[:], ALU.mult).then_inc(q["bon_m"], 1)

            def first(c, s):
                for g in range(2):
                    hs = slice(g * H2, (g + 1) * H2)
                    wait(pool, "a_masked", c, 4, g + 1)
                    if g == 0:
                        wait(pool, "z_sum", c - 1, 10, 10)
                        wait(pool, "dt0", c - 1, 4, 4)
                        wait(pool, "dtb0", c - 1, 2, 2)
                    pool.tensor_tensor(abi[:, hs], ab[s][:, hs, 0], bc(eyebd[:], 1, H2), ALU.add).then_inc(q["abi_done"], 1)
                for g in range(2):
                    hs = slice(g * H2, (g + 1) * H2)
                    wait(pool, "abi_done", c, 2, g + 1)
                    if g == 0:
                        wait(pool, "u_sum", c - 1, 2, 2)
                    pool.tensor_tensor(bdm(dtb[:, hs].rearrange("p h d t -> p (h d) t")).rearrange("p (h x) -> p h x", h=H2), abi[:, hs],
                                       bc(levelbd[:, 0].rearrange("p d t -> p (d t)"), 1, H2), ALU.mult).then_inc(q["dtb0"], 1)

            def prepare(c, s):
                keys(c, s)
                rate(c, s)
                first(c, s)

            def bdm(ap):
                return ap.rearrange("p x t -> p (x t)")

            def both(c, s):
                prepare(c + 1, 1 - s)

            steps(pool, prepare, both, lambda c, s: None)

        @block.vector
        def _(dve):
            dve.memset(st[:], 0.0).then_inc(q["zeroed0"], 1)
            dve.wait_ge(con_in, 176)
            dve.wait_ge(q["zeroed0"], 1)
            dve.wait_ge(q["zeroed2"], 5)

            def d_pre(c, s):
                wait(dve, "lora_sum", c, 1, 1)
                wait(dve, "cum_done", c - 1, 1, 1)
                wait(dve, "less_done", c - 1, 1, 1)
                wait(dve, "akk_done", c - 1, 1, 1)
                wait(dve, "kd_done", c - 1, 1, 1)
                for i in range(2):
                    dve.tensor_tensor(sig[:, i], B[i][:], wa0[:, i], ALU.add).then_inc(q["pre_done"], 1)

            def d_keys(c, s):
                wait(dve, "pool_k", c, 5, 2)
                wait(dve, "rooted", c - 1, 1, 1)
                dve.tensor_reduce(ss[:], sq[:].rearrange("p (h k) -> p h k", h=NH), AX_X, ALU.add).then_inc(q["ssd"], 1)
                wait(dve, "ssd", c, 1, 1)
                dve.tensor_scalar(ss[:], ss[:], 1e-24, None, ALU.max).then_inc(q["clamped"], 1)

            def d_unit(c, s):
                wait(dve, "rooted", c, 1, 1)
                dve.reciprocal(rn[:], rn[:]).then_inc(q["rnd"], 1)
                wait(dve, "rnd", c, 1, 1)
                wait(dve, "akk_done", c - 1, 1, 1)
                dve.tensor_tensor(kk[:].rearrange("p (h k) -> p h k", h=NH), kkr[:].rearrange("p (h k) -> p h k", h=NH),
                                  bc(rn[:], 2, HD), ALU.mult).then_inc(q["kk_done"], 1)

            def d_rate(c, s):
                wait(dve, "sig_done", c, 1, 1)
                wait(dve, "pool_k", c, 5, 4)
                wait(dve, "bon_m", c - 1, 1, 1)
                dve.tensor_tensor(kd[:], sig[:, 1], kka[:], ALU.mult).then_inc(q["kd_part"], 1)
                wait(dve, "kd_part", c, 1, 1)
                dve.tensor_tensor(kd[:], kd[:], krest[:], ALU.add).then_inc(q["kd_done"], 1)

            def d_less(c, s):
                wait(dve, "cum_done", c, 1, 1)
                wait(dve, "exp_done", c - 1, 5, 5)
                dve.scalar_tensor_tensor(e_ex[:], sig[:, 0], -LD, B[2][:], ALU.mult, ALU.add).then_inc(q["less_done"], 1)

            def d_ops(c, s):
                v3 = lambda ap: ap.rearrange("p (h k) -> p h k", h=NH)
                wait(dve, "exp_done", c, 5, 3)
                wait(dve, "turned_up", c - 1, 6, 6)
                wait(dve, "s_sum", c - 2, 2, 2)
                dve.tensor_tensor(alpha[:], kk[:], e_ex[:], ALU.mult).then_inc(q["op_done"], 1)
                wait(dve, "akk_done", c, 1, 1)
                for d in range(2):
                    dve.scalar_tensor_tensor(beta[s][K[d], :, d, :], v3(akk[K[d], :]), -1.0, v3(e_ng[K[d], :]), ALU.mult, ALU.mult
                                             ).then_inc(q["op_done"], 1)
                wait(dve, "kd_done", c, 1, 1)
                for d in range(2):
                    dve.tensor_tensor(kap[s][K[d], :, d, :], v3(kd[K[d], :]), v3(e_ng[K[d], :]), ALU.mult).then_inc(q["op_done"], 1)
                dve.tensor_tensor(rho[:], rkv[s][:, 0, :], e_in[:], ALU.mult).then_inc(q["op_done"], 1)

            def d_turn(c, s):
                wait(dve, "a_sum", c - 1, 4, 4)
                for n, bank, dst, g, name in ((2, 3, bT, 0, "tev_b"), (3, 0, bT, 1, "tev_b"), (5, 1, kT, 0, "tev_k"), (6, 3, kT, 1, "tev_k")):
                    wait(dve, "turned_up", c, 6, n)
                    dve.tensor_copy(dst[:, g * H2:(g + 1) * H2].rearrange("p h x -> p (h x)"), B[bank][:]).then_inc(q[name], 1)

            def d_bonus(c, s):
                wait(dve, "bon_m", c, 1, 1)
                v = 16 * (c - s - LC // C)
                if not (isinstance(v, int) and v <= 0):
                    dve.wait_ge(y_out[s], v)
                dve.tensor_reduce(yb[s][:, RC:], rrk[:].rearrange("p (h k) -> p h k", h=NH), AX_X, ALU.add).then_inc(q["bon_done"], 1)

            def d_masks(c, s):
                wait(dve, "y_sum", c - 2, 2, 2)
                wait(dve, "abi_done", c - 2, 2, 2)
                for n, dst, g, bank in ((0, ab[s], 0, 2), (1, ab[s], 1, 3), (2, ak[s], 0, 0), (3, ak[s], 1, 1)):
                    wait(dve, "a_sum", c, 4, n + 1)
                    dve.tensor_tensor(dst[:, g * H2:(g + 1) * H2].rearrange("p h a (d t) -> p (h a) d t", d=2),
                                      bc(B[bank][:].rearrange("p (x t) -> p x t", t=C), 2, 2),
                                      causal[:].rearrange("p h a d t -> p (h a) d t"), ALU.mult).then_inc(q["a_masked"], 1)

            def d_first(c, s):
                h4 = lambda ap: ap.rearrange("p (h t) -> p h t", h=H2)
                wait(dve, "d_sum", c - 1, 10, 10)
                for g in range(2):
                    wait(dve, "abi_done", c, 2, g + 1)
                    for d in range(2):
                        dve.tensor_tensor(h4(dd[K[d], g, 1]), abi[K[d], g * H2:(g + 1) * H2, d * C:(d + 1) * C],
                                          bc(levelbd[K[d], 0, d], 1, H2), ALU.mult).then_inc(q["dt0"], 1)
                for g in range(2):
                    wait(dve, "adir", c, 2, g + 1)
                    dve.tensor_tensor(h4(dd[:, g, 0]), h4(B[6 + g][:, 0:H2 * C]), bc(level[:, 0], 1, H2), ALU.mult).then_inc(q["d0"], 1)

            def d_level(c, s, l):
                h4 = lambda ap: ap.rearrange("p (h t) -> p h t", h=H2)
                for g in range(2):
                    wait(dve, "z_sum", c, 10, 2 * (l - 1) + g + 1)
                    if l > 1:
                        wait(dve, "d_sum", c, 10, 2 * (l - 2) + g + 1)
                    z = h4(B[4 + g][:, 0:H2 * C])
                    if l < 5:
                        dve.tensor_tensor(h4(xm[:, g]), z, bc(level[:, l], 1, H2), ALU.mult).then_inc(q["x_done"], 1)
                    else:
                        dve.sem_inc(q["x_done"], 1)
                    dve.tensor_tensor(xb[:, g * H2:(g + 1) * H2], bc(z, 2, 2), bc(levelbd[:, l], 1, H2), ALU.mult).then_inc(q["xb_done"], 1)

            def d_added(c, s):
                for g in range(2):
                    wait(dve, "s_sum", c, 2, g + 1)
                    if g == 0:
                        wait(dve, "s_done", c - 1, 2, 2)
                    dve.tensor_tensor(half(sm, g), half(st, g), B[6 + g][:, 0:H2 * C], ALU.add).then_inc(q["s_added"], 1)

            def d_decay(c, s):
                h4 = lambda ap: ap.rearrange("p (h t) -> p h t", h=H2)
                if isinstance(c, int) and c < 0:
                    return
                wait(dve, "exp_done", c, 5, 5)
                wait(dve, "y_sum", c, 2, 2)
                for g in range(2):
                    wait(dve, "s_added", c, 2, g + 1)
                    dve.tensor_tensor(h4(half(st, g)), h4(half(sm, g)), bc(dec[s][:, g * H2:(g + 1) * H2], 2, HD), ALU.mult
                                      ).then_inc(q["s_done"], 1)

            def prepare(c, s):
                d_pre(c, s)
                d_keys(c, s)
                d_unit(c, s)
                d_rate(c, s)
                d_less(c, s)
                d_ops(c, s)
                d_turn(c, s)
                d_masks(c, s)
                d_bonus(c, s)

            def both(c, s):
                d_first(c, s)
                d_decay(c - 1, 1 - s)
                d_keys(c + 1, 1 - s)
                d_level(c, s, 1)
                d_pre(c + 1, 1 - s)
                d_level(c, s, 2)
                d_unit(c + 1, 1 - s)
                d_level(c, s, 3)
                d_rate(c + 1, 1 - s)
                d_less(c + 1, 1 - s)
                d_level(c, s, 4)
                d_level(c, s, 5)
                d_ops(c + 1, 1 - s)
                d_turn(c + 1, 1 - s)
                d_added(c, s)
                d_masks(c + 1, 1 - s)
                d_bonus(c + 1, 1 - s)

            def recur(c, s):
                d_first(c, s)
                d_decay(c - 1, 1 - s)
                for l in range(1, 6):
                    d_level(c, s, l)

            prepare(0, 0)
            for c in range(6):
                both(c, c % 2)
            with dve.Fori(3, NSTEP // 2 - 1) as j:
                for s in range(2):
                    both(2 * j + s, s)
            both(NSTEP - 2, 0)
            recur(NSTEP - 1, 1)


class Chain:

    def __init__(self, eng, sem, per):
        self.eng, self.sem, self.per = eng, sem, per

    def start(self, i):
        self.i, self.k = i, 0

    def do(self, ins):
        ins.then_inc(self.sem, 1)
        self.k += 1
        return self.k

    def wait(self, k=None):
        self.eng.wait_ge(self.sem, self.i * self.per + (self.k if k is None else k))

    def end(self):
        assert self.k == self.per, (self.k, self.per)


def merge(nc, sems, io, per):
    with ExitStack() as ctx:
        m = Mem(nc, ctx, "mg")
        wout = m.sb("wout", [P, KD, D])
        rows = m.sb("mrows", [P, 3 * CH + 2 * CH + 2 * RC])
        lnr = m.sb("lnr", [P, 2, D])
        gup = m.sb("gup", [P, RC])
        wrt = m.sb("wrt", [P, KD, NE])
        ebias = m.sb("ebias", [P, NE])
        wsgu = m.sb("wsgu", [P, KD, 2 * FF])
        wsd = m.sb("wsd", [P, 2, D])
        tri = m.sb("rtri", [P, P])
        ones = m.sb("ones", [P, P])
        iota = m.sb("iota", [P, NE])
        iotap = m.sb("iotap", [P, 1])
        thresh = m.sb("thresh", [P, 8])
        b = m.sb("b", [P, CH])
        cx = m.sb("cx", [P, 3, 2, CH])
        ycat = m.sb("ycat", [P, D])
        yh = m.sb("yh", [P, CH])
        ya = m.sb("ya", [P, CH])
        y01 = m.sb("y01", [P, 2, RC + NH])
        ysum = m.sb("ysum", [P, RC + NH])
        v = m.sb("v", [P, RC])
        z3 = m.sb("z3", [P, 3, CH])
        za = m.sb("za", [P, CH])
        yn = m.sb("yn", [P, RC])
        sqr = m.sb("sqr", [P, RC])
        bonus = m.sb("bonus", [P, RC])
        junk = m.sb("junk", [P, D])
        mean8 = m.sb("mean8", [P, NH])
        var = m.sb("var", [P, 2 + NH])
        rstd = m.sb("rstd", [P, 2 + NH])
        sgd = m.sb("sgd", [P, P])
        ycT = m.sb("ycT", [P, KD, P])
        x = m.sb("x", [P, D])
        t = m.sb("t", [P, D])
        x1 = m.sb("x1", [P, D])
        h2 = m.sb("h2", [P, D])
        base = m.sb("base", [P, D])
        h2T = m.sb("h2T", [P, KD, P])
        stat = m.sb("stat", [P, 4])
        sgm = m.sb("sgm", [P, FF])
        hid = m.sb("hid", [P, FF])
        hidT = m.sb("hidT", [P, 2, P])
        sc = m.sb("sc", [P, NE])
        biased = m.sb("biased", [P, NE])
        top = m.sb("top", [P, 8])
        topi = m.sb("topi", [P, 8], U32)
        topf = m.sb("topf", [P, 8])
        sel3 = m.sb("sel3", [P, TOPK, NE])
        mem = m.sb("mem", [P, NE])
        gsum = m.sb("gsum", [P, 2])
        rank = m.sb("rank", [P, NE])
        carry = m.sb("carry", [P, NE])
        OH = m.sb("OH", [P, NT, TOPK, NE])
        rnk = m.sb("rnk", [P, NT, TOPK])
        gates, slots, slots_i = per["gates"], m.sb("slots", [P, NT, TOPK]), per["slots_i"]
        names = ("G", "T0", "T1", "O0", "O1", "R", "S", "H")
        G, T0, T1, O0, O1, R, S, H = (m.ps(x) for x in names)
        w_in, a_in, x_in = sems("w_in"), sems("a_in"), sems("x_in")
        q = {n: sems(n) for n in (
            "a_free gate_sum gd_sig za2 sq_done vars rooted1 mixed turnedY ycT_done out_sum out_read mean_sum var_sum mu ln_var "
            "rooted2 h2_done turnedH h2T_done logits gu sig_gu hid_done turnedS hidT_done down_sum base_done scored routed "
            "member rank_sum rank_read shifted bon_done gn_sq lnb x_free tail tab "
            "dmix dout pmix h2_st base_st zt tok_in passed passed_pool").split()}
        tiling = ExitStack()
        block = tiling.enter_context(nc.Block())
        MIX, OUT, PMIX = 18, 20, 4

        def wait(eng, name, i, per_tile, k):
            val = i * per_tile + k
            if not (isinstance(val, int) and val <= 0):
                eng.wait_ge(q[name], val)

        def tiles(eng, mix, both, out):
            mix(0)
            both(0)
            with eng.Fori(1, NT - 1) as i:
                both(i)
            out(NT - 1)

        @block.sync
        def _(sp):
            for dst, src in ((rows[:], io["mix_rows"].partition_broadcast(P)), (gup[:], io["g_up"]),
                             (lnr[:].rearrange("p a d -> p (a d)"), io["ln_rows"][0:2 * D].partition_broadcast(P)),
                             (wrt[:], io["w_router"]), (ebias[:], io["e_bias"].partition_broadcast(P)),
                             (wsgu[:], io["w_s_gu"]), (wsd[:], io["w_s_down"]), (tri[:], io["rank_tri"]),
                             (iota[:], io["iota_e"]), (iotap[:], io["iota_p"]), (thresh[:], io["thresh"]), (wout[:], io["w_out"])):
                sp.dma_start(dst, src).then_inc(w_in, 16)

            def load_mix(i):
                wait(sp, "mixed", i - 1, 1, 1)
                wait(sp, "bon_done", i - 1, 1, 1)
                wait(sp, "sq_done", i - 1, 2, 2)
                r0 = LC + i * P
                sp.dma_start(b[:], io["u"][bass.ds(r0, P), 0:CH]).then_inc(a_in, 16)
                for n in range(3):
                    sp.dma_start(cx[:, n], io["u"][bass.ds(r0 + (n - 1) * GRID, P), CH:3 * CH]
                                 .rearrange("t (a c) -> t a c", a=2)).then_inc(a_in, 16)
                sp.dma_start(yh[:], io["yh"][bass.ds(i * P, P)]).then_inc(a_in, 16)
                sp.dma_start(y01[:, 0], io["ys0"][bass.ds(i * P, P)]).then_inc(a_in, 16)
                sp.dma_start(y01[:, 1], io["ys1"][bass.ds(i * P, P)]).then_inc(a_in, 16)
                sp.dma_start(v[:], io["u"][bass.ds(r0, P), UW - RC:UW]).then_inc(a_in, 16)

            def load_out(i):
                wait(sp, "x_free", i - 1, 1, 1)
                sp.dma_start(x[:], io["x"][bass.ds(i * P, P)]).then_inc(x_in, 16)

            def both(i):
                load_mix(i + 1)
                load_out(i)

            tiles(sp, load_mix, both, load_out)

        @block.tensor
        def _(pe):
            ident = per["ident"]
            pe.wait_ge(w_in, 192)

            def mix(i):
                wait(pe, "gd_sig", i, 1, 1)
                wait(pe, "mixed", i - 1, 1, 1)
                pe.matmul(G[:], sgd[:], gup[:], start=True, stop=True).then_inc(q["gate_sum"], 1)
                wait(pe, "mixed", i, 1, 1)
                wait(pe, "h2T_done", i - 2, 2, 2)
                for k in range(KD):
                    bank = (T0, T1)[k // 4]
                    mm = pe.transpose(bank[:, (k % 4) * P:(k % 4 + 1) * P], ycat[:, k * P:(k + 1) * P], ident[:])
                    if k % 4 == 3:
                        mm.then_inc(q["turnedY"], 1)

            def project_out(i):
                wait(pe, "ycT_done", i, 2, 2)
                wait(pe, "base_done", i - 1, 2, 2)
                for n, bank in enumerate((O0, O1)):
                    for k in range(KD):
                        mm = pe.matmul(bank[:], ycT[:, k, :], wout[:, k, n * 512:(n + 1) * 512], start=(k == 0), stop=(k == KD - 1))
                    mm.then_inc(q["out_sum"], 1)

            def after(i, mix_next):
                wait(pe, "h2_done", i, 1, 1)
                if mix_next:
                    wait(pe, "ycT_done", i + 1, 2, 2)
                for k in range(KD):
                    bank = (T0, T1)[k // 4]
                    mm = pe.transpose(bank[:, (k % 4) * P:(k % 4 + 1) * P], h2[:, k * P:(k + 1) * P], ident[:])
                    if k % 4 == 3:
                        mm.then_inc(q["turnedH"], 1)
                wait(pe, "h2T_done", i, 2, 2)
                wait(pe, "rank_read", i - 1, 2, 2)
                for k in range(KD):
                    mm = pe.matmul(R[:, 0:NE], h2T[:, k, :], wrt[:, k, :], start=(k == 0), stop=(k == KD - 1))
                mm.then_inc(q["logits"], 1)
                wait(pe, "hid_done", i - 1, 1, 1)
                for k in range(KD):
                    mm = pe.matmul(S[:], h2T[:, k, :], wsgu[:, k, :], start=(k == 0), stop=(k == KD - 1))
                mm.then_inc(q["gu"], 1)
                wait(pe, "member", i, 1, 1)
                pe.matmul(R[:, 128:128 + NE], tri[:], mem[:], start=True, stop=True)
                pe.matmul(R[:, 256:256 + NE], ones[:], mem[:], start=True, stop=True).then_inc(q["rank_sum"], 1)
                wait(pe, "hid_done", i, 1, 1)
                wait(pe, "hidT_done", i - 1, 1, 1)
                for k in range(2):
                    mm = pe.transpose(H[:, k * P:(k + 1) * P], hid[:, k * P:(k + 1) * P], ident[:])
                mm.then_inc(q["turnedS"], 1)
                wait(pe, "hidT_done", i, 1, 1)
                for n, bank in enumerate((O0, O1)):
                    for k in range(2):
                        mm = pe.matmul(bank[:], hidT[:, k, :], wsd[:, k, n * 512:(n + 1) * 512], start=(k == 0), stop=(k == 1))
                    mm.then_inc(q["down_sum"], 1)

            def both(i):
                project_out(i)
                mix(i + 1)
                wait(pe, "out_read", i, 2, 2)
                after(i, True)

            def out(i):
                project_out(i)
                wait(pe, "out_read", i, 2, 2)
                after(i, False)

            tiles(pe, mix, both, out)

        @block.scalar
        def _(act):
            def mix1(i):
                wait(act, "gate_sum", i - 1, 1, 1)
                act.activation(sgd[:], per["gd"][:, bass.ds(LC + i * P, P)], ACT.Sigmoid).then_inc(q["gd_sig"], 1)

            def mix2(i):
                act.wait_ge(a_in, 128 * i + 128)
                wait(act, "vars", i - 1, 1, 1)
                act.activation(junk[:, 0:CH], yh[:], ACT.Square, accum_out=var[:, 1:2]).then_inc(q["sq_done"], 1)
                wait(act, "za2", i, 1, 1)
                act.activation(junk[:, CH:2 * CH], ya[:], ACT.Square, accum_out=var[:, 0:1]).then_inc(q["sq_done"], 1)
                wait(act, "vars", i, 1, 1)
                act.activation(rstd[:], var[:], ACT.Sqrt).then_inc(q["rooted1"], 1)

            def mix3(i):
                wait(act, "out_sum", i - 1, 2, 2)
                for g, bank in enumerate((T0, T1)):
                    wait(act, "turnedY", i, 2, g + 1)
                    act.copy(ycT[:, 4 * g:4 * g + 4].rearrange("p k t -> p (k t)"), bank[:]).then_inc(q["ycT_done"], 1)

            def norm(i):
                wait(act, "out_read", i, 2, 2)
                wait(act, "shifted", i, 1, 1)
                act.activation(junk[:], t[:], ACT.Identity, accum_out=stat[:, 0:1]).then_inc(q["mean_sum"], 1)
                wait(act, "mu", i, 1, 1)
                wait(act, "mean_sum", i, 1, 1)
                act.activation(junk[:], t[:], ACT.Square, bias=stat[:, 1:2], accum_out=stat[:, 2:3]).then_inc(q["var_sum"], 1)
                wait(act, "ln_var", i, 1, 1)
                act.activation(stat[:, 3:4], stat[:, 2:3], ACT.Sqrt).then_inc(q["rooted2"], 1)

            def after(i):
                wait(act, "down_sum", i - 1, 2, 2)
                for g, bank in enumerate((T0, T1)):
                    wait(act, "turnedH", i, 2, g + 1)
                    act.copy(h2T[:, 4 * g:4 * g + 4].rearrange("p k t -> p (k t)"), bank[:]).then_inc(q["h2T_done"], 1)
                wait(act, "logits", i, 1, 1)
                wait(act, "routed", i - 1, 1, 1)
                act.activation(sc[:], R[:, 0:NE], ACT.Sigmoid).then_inc(q["scored"], 1)
                wait(act, "gu", i, 1, 1)
                wait(act, "hid_done", i - 1, 1, 1)
                act.activation(sgm[:], S[:, 0:FF], ACT.Sigmoid).then_inc(q["sig_gu"], 1)
                wait(act, "turnedS", i, 1, 1)
                act.copy(hidT[:].rearrange("p k t -> p (k t)"), H[:, 0:2 * P]).then_inc(q["hidT_done"], 1)

            def mix(i):
                mix1(i)
                mix2(i)
                mix3(i)

            def both(i):
                mix(i + 1)
                norm(i)
                after(i)

            def out(i):
                norm(i)
                after(i)

            tiles(act, mix, both, out)

        @block.gpsimd
        def _(pool):
            pool.memset(ones[:], 1.0).then_inc(q["tok_in"], 1)
            pool.wait_ge(w_in, 192)
            pool.wait_ge(q["tok_in"], 1)
            ch = Chain(pool, q["pmix"], PMIX)
            v3 = lambda ap: ap.rearrange("p (h k) -> p h k", h=NH)

            def mix(i):
                ch.start(i)
                pool.wait_ge(a_in, 128 * i + 128)
                wait(pool, "za2", i - 1, 1, 1)
                ch.do(pool.tensor_tensor(z3[:], cx[:, :, 0], cx[:, :, 1], ALU.mult))
                ch.wait()
                ch.do(pool.tensor_tensor(z3[:].rearrange("p a c -> p (a c)"), z3[:].rearrange("p a c -> p (a c)"), rows[:, 0:3 * CH], ALU.mult))
                ch.wait()
                wait(pool, "mixed", i - 1, 1, 1)
                ch.do(pool.tensor_tensor(za[:], z3[:, 0], z3[:, 1], ALU.add))
                ch.wait()
                pool.wait_ge(q["dmix"], i * MIX + 1)
                ch.do(pool.tensor_tensor(v3(bonus[:]), bc(ysum[:, RC:], 2, HD), v3(v[:]), ALU.mult))
                ch.wait()
                pool.sem_inc(q["bon_done"], 1)
                ch.end()

            def out(i):
                wait(pool, "h2_done", i, 1, 1)
                pool.sem_inc(q["passed_pool"], 1)
                pool.dma_start(io["h2"][bass.ds(i * P, P)], h2[:]).then_inc(q["h2_st"], 16)
                wait(pool, "base_done", i, 2, 2)
                pool.sem_inc(q["passed_pool"], 1)
                pool.dma_start(io["base"][bass.ds(i * P, P)], base[:]).then_inc(q["base_st"], 16)

            def both(i):
                mix(i + 1)
                out(i)

            tiles(pool, mix, both, out)
            pool.wait_ge(q["h2_st"], 16 * NT)
            pool.wait_ge(q["base_st"], 16 * NT)

        @block.vector
        def _(dve):
            dve.memset(carry[:], 0.0).then_inc(q["zt"], 1)
            dve.wait_ge(w_in, 192)
            dve.wait_ge(q["zt"], 1)
            dve.wait_ge(q["tok_in"], 1)
            cm, co = Chain(dve, q["dmix"], MIX), Chain(dve, q["dout"], OUT)
            v3 = lambda ap: ap.rearrange("p (h k) -> p h k", h=NH)
            o = 3 * CH

            def mix(i):
                c = cm
                c.start(i)
                dve.wait_ge(a_in, 128 * i + 128)
                wait(dve, "bon_done", i - 1, 1, 1)
                c.do(dve.tensor_tensor(ysum[:], y01[:, 0], y01[:, 1], ALU.add))
                c.wait()
                c.do(dve.tensor_reduce(mean8[:], v3(ysum[:, 0:RC]), AX_X, ALU.add))
                c.wait()
                c.do(dve.tensor_scalar(mean8[:], mean8[:], 1.0 / HD, None, ALU.mult))
                c.wait()
                c.do(dve.tensor_tensor(v3(yn[:]), v3(ysum[:, 0:RC]), bc(mean8[:], 2, HD), ALU.subtract))
                c.wait()
                c.do(dve.tensor_tensor(sqr[:], yn[:], yn[:], ALU.mult))
                dve.wait_ge(q["pmix"], i * PMIX + 3)
                c.do(dve.tensor_tensor(za[:], za[:], z3[:, 2], ALU.add))
                c.wait()
                c.do(dve.tensor_tensor(ya[:], za[:], b[:], ALU.mult))
                c.wait()
                dve.sem_inc(q["za2"], 1)
                wait(dve, "rooted1", i - 1, 1, 1)
                c.do(dve.tensor_reduce(var[:, 2:], v3(sqr[:]), AX_X, ALU.add))
                c.wait()
                c.do(dve.tensor_scalar(var[:, 2:], var[:, 2:], 1.0 / HD, GN_EPS, ALU.mult, ALU.add))
                wait(dve, "sq_done", i, 2, 2)
                c.do(dve.tensor_scalar(var[:, 0:2], var[:, 0:2], 1.0 / CH, LN_EPS, ALU.mult, ALU.add))
                c.wait()
                dve.sem_inc(q["vars"], 1)
                wait(dve, "rooted1", i, 1, 1)
                c.do(dve.reciprocal(rstd[:], rstd[:]))
                c.wait()
                wait(dve, "turnedY", i - 1, 2, 2)
                c.do(dve.scalar_tensor_tensor(ycat[:, 0:CH], ya[:], rstd[:, 0:1], rows[:, o:o + CH], ALU.mult, ALU.mult))
                c.do(dve.scalar_tensor_tensor(ycat[:, CH:2 * CH], yh[:], rstd[:, 1:2], rows[:, o + CH:o + 2 * CH], ALU.mult, ALU.mult))
                c.do(dve.tensor_tensor(v3(yn[:]), v3(yn[:]), bc(rstd[:, 2:], 2, HD), ALU.mult))
                c.wait()
                g0 = o + 2 * CH
                c.do(dve.tensor_tensor(yn[:], yn[:], rows[:, g0:g0 + RC], ALU.mult))
                c.wait()
                c.do(dve.tensor_tensor(yn[:], yn[:], rows[:, g0 + RC:g0 + 2 * RC], ALU.add))
                c.wait()
                wait(dve, "bon_done", i, 1, 1)
                c.do(dve.tensor_tensor(yn[:], yn[:], bonus[:], ALU.add))
                c.wait()
                wait(dve, "gate_sum", i, 1, 1)
                c.do(dve.tensor_tensor(ycat[:, 2 * CH:], yn[:], G[:], ALU.mult))
                c.wait()
                dve.sem_inc(q["mixed"], 1)
                c.end()

            def norm(i):
                c = co
                c.start(i)
                dve.wait_ge(x_in, 16 * i + 16)
                g1 = per["rows"][:, 0:D]
                wait(dve, "var_sum", i - 1, 1, 1)
                for n, bank in enumerate((O0, O1)):
                    wait(dve, "out_sum", i, 2, n + 1)
                    dve.tensor_tensor(t[:, n * 512:(n + 1) * 512], bank[:], g1[:, n * 512:(n + 1) * 512], ALU.mult).then_inc(q["out_read"], 1)
                wait(dve, "out_read", i, 2, 2)
                dve.scalar_tensor_tensor(t[:], x[:], ALPHA, t[:], ALU.mult, ALU.add).then_inc(q["shifted"], 1)
                wait(dve, "mean_sum", i, 1, 1)
                dve.sem_inc(q["x_free"], 1)
                c.do(dve.tensor_scalar(stat[:, 1:2], stat[:, 0:1], -1.0 / D, None, ALU.mult))
                c.wait()
                dve.sem_inc(q["mu"], 1)
                wait(dve, "var_sum", i, 1, 1)
                c.do(dve.tensor_scalar(stat[:, 2:3], stat[:, 2:3], 1.0 / D, LN_EPS, ALU.mult, ALU.add))
                c.wait()
                dve.sem_inc(q["ln_var"], 1)
                wait(dve, "rooted2", i, 1, 1)
                c.do(dve.reciprocal(stat[:, 3:4], stat[:, 3:4]))
                c.wait()
                c.do(dve.tensor_scalar(x1[:], t[:], stat[:, 1:2], stat[:, 3:4], ALU.add, ALU.mult))
                c.wait()
                c.do(dve.tensor_tensor(x1[:], x1[:], lnr[:, 0], ALU.mult))
                c.wait()
                c.do(dve.tensor_tensor(x1[:], x1[:], lnr[:, 1], ALU.add))
                c.wait()
                wait(dve, "turnedH", i - 1, 2, 2)
                wait(dve, "h2_st", i - 1, 16, 16)
                c.do(dve.tensor_tensor(h2[:], x1[:], per["rows"][:, 2 * D:3 * D], ALU.mult))
                c.wait()
                dve.tensor_tensor(h2[:], h2[:], per["rows"][:, D:2 * D], ALU.add).then_inc(q["h2_done"], 1)

            def after(i):
                c = co
                wait(dve, "scored", i, 1, 1)
                c.do(dve.tensor_tensor(biased[:], sc[:], ebias[:], ALU.add))
                c.wait()
                dve.sem_inc(q["passed"], 1)
                c.do(dve.max(top[:], biased[:]))
                c.wait()
                dve.sem_inc(q["passed"], 1)
                c.do(dve.max_index(topi[:], top[:], biased[:]))
                c.wait()
                c.do(dve.tensor_copy(topf[:], topi[:]))
                c.wait()
                oh = OH[:, bass.ds(i, 1)].rearrange("p o j e -> p (o j) e")
                c.do(dve.tensor_tensor(oh, bc(iota[:], 1, TOPK), bc(topf[:], 2, NE), ALU.is_equal))
                c.wait()
                dve.sem_inc(q["passed"], 1)
                dve.tensor_reduce(mem[:], oh.rearrange("p j e -> p e j"), AX_X, ALU.add).then_inc(q["member"], 1)
                c.do(dve.tensor_tensor(sel3[:], oh, bc(sc[:], 1, TOPK), ALU.mult))
                c.wait()
                gt = gates[:, bass.ds(i, 1)].rearrange("p o j -> p (o j)")
                c.do(dve.tensor_reduce(gt, sel3[:], AX_X, ALU.add))
                c.wait()
                dve.sem_inc(q["routed"], 1)
                c.do(dve.tensor_reduce(gsum[:, 0:1], gt, AX_X, ALU.add))
                c.wait()
                c.do(dve.reciprocal(gsum[:, 1:2], gsum[:, 0:1]))
                c.wait()
                c.do(dve.tensor_scalar(gt, gt, gsum[:, 1:2], ROUTED, ALU.mult, ALU.mult))
                wait(dve, "sig_gu", i, 1, 1)
                wait(dve, "turnedS", i - 1, 1, 1)
                c.do(dve.tensor_tensor(hid[:], sgm[:], S[:, 0:FF], ALU.mult))
                c.wait()
                dve.tensor_tensor(hid[:], hid[:], S[:, FF:2 * FF], ALU.mult).then_inc(q["hid_done"], 1)
                wait(dve, "rank_sum", i, 1, 1)
                dve.tensor_tensor(rank[:], R[:, 128:128 + NE], carry[:], ALU.add).then_inc(q["rank_read"], 1)
                wait(dve, "rank_read", i, 2, 1)
                dve.tensor_tensor(carry[:], R[:, 256:256 + NE], carry[:], ALU.add).then_inc(q["rank_read"], 1)
                c.do(dve.tensor_tensor(sel3[:], oh, bc(rank[:], 1, TOPK), ALU.mult))
                c.wait()
                c.do(dve.tensor_reduce(rnk[:, bass.ds(i, 1)].rearrange("p o j -> p (o j)"), sel3[:], AX_X, ALU.add))
                c.wait()
                wait(dve, "rank_read", i, 2, 2)
                wait(dve, "base_st", i - 1, 16, 16)
                g2 = per["rows"][:, 3 * D:4 * D]
                for n, bank in enumerate((O0, O1)):
                    wait(dve, "down_sum", i, 2, n + 1)
                    dve.tensor_tensor(base[:, n * 512:(n + 1) * 512], bank[:], g2[:, n * 512:(n + 1) * 512], ALU.mult).then_inc(q["tail"], 1)
                    wait(dve, "tail", i, 2, n + 1)
                    dve.scalar_tensor_tensor(base[:, n * 512:(n + 1) * 512], x1[:, n * 512:(n + 1) * 512], ALPHA,
                                             base[:, n * 512:(n + 1) * 512], ALU.mult, ALU.add).then_inc(q["base_done"], 1)
                wait(dve, "base_done", i, 2, 2)
                c.end()

            def both(i):
                mix(i + 1)
                norm(i)
                after(i)

            def out(i):
                norm(i)
                after(i)

            tiles(dve, mix, both, out)

        tiling.close()

        nb = m.sb("nb", [P, NE])
        ends = [m.sb(f"ends{n}", [P, NE]) for n in range(2)]
        first = m.sb("first", [P, NE])
        be = m.sb("be", [P, 1])
        bei = m.sb("bei", [P, 1], I32)
        tok = m.sb("tok", [P, NT], I32)
        zi = m.sb("zi", [P, P], I32)
        route = sems("route")
        slots_ready, be_ready, zero_ready, tok_ready = (sems(x) for x in ("slots_ready", "be_ready", "zero_ready", "tok_ready"))
        zero_out, be_out, tok_out = sems("zero_out"), sems("be_out"), sems("tok_out")
        tables = ExitStack()
        block = tables.enter_context(nc.Block())

        @block.vector
        def _(dve):
            c = Chain(dve, route, 0)
            c.start(0)

            def do(ins):
                c.do(ins)
                c.wait()

            dve.memset(zi[:], 0).then_inc(zero_ready, 1)
            cmp = sel3[:].rearrange("p j e -> p (j e)").rearrange("p (e n) -> p e n", n=8)
            do(dve.tensor_tensor(cmp, bc(carry[:], 2, 8), bc(thresh[:], 1, NE), ALU.is_gt))
            do(dve.tensor_reduce(nb[:], cmp, AX_X, ALU.add))
            do(dve.tensor_copy(ends[0][:], nb[:]))
            for n in range(6):
                a, z, sh = ends[n % 2], ends[(n + 1) % 2], 2 ** n
                do(dve.tensor_copy(z[:, 0:sh], a[:, 0:sh]))
                do(dve.tensor_tensor(z[:, sh:], a[:, sh:], a[:, 0:NE - sh], ALU.add))
            do(dve.tensor_tensor(first[:], ends[0][:], nb[:], ALU.subtract))
            do(dve.tensor_scalar(first[:], first[:], float(P), None, ALU.mult))
            for i in range(NT):
                do(dve.tensor_tensor(sel3[:], OH[:, i], bc(first[:], 1, TOPK), ALU.mult))
                do(dve.tensor_reduce(slots[:, i], sel3[:], AX_X, ALU.add))
            do(dve.tensor_tensor(slots[:], slots[:], rnk[:], ALU.add))
            dve.tensor_copy(slots_i[:], slots[:]).then_inc(slots_ready, 1)
            do(dve.tensor_tensor(rank[:], ends[0][:], iotap[:].broadcast_to([P, NE]), ALU.is_le))
            do(dve.tensor_reduce(be[:], rank[:], AX_X, ALU.add))
            do(dve.tensor_scalar(be[:], be[:], float(NE - 1), None, ALU.min))
            dve.tensor_copy(bei[:], be[:]).then_inc(be_ready, 1)

        @block.sync
        def _(sp):
            sp.wait_ge(zero_ready, 1)
            sp.dma_start(io["slot_token"].rearrange("(b p) o -> b (p o)", p=P), zi[:]).then_inc(zero_out, 16)
            sp.wait_ge(be_ready, 1)
            sp.dma_start(io["block_expert"].rearrange("o b -> b o"), bei[:]).then_inc(be_out, 16)
            sp.wait_ge(zero_out, 16)
            sp.wait_ge(be_out, 16)

        @block.gpsimd
        def _(pool):
            pool.iota(tok[:], [[P, NT]], base=0, channel_multiplier=1).then_inc(tok_ready, 1)
            pool.wait_ge(tok_ready, 1)
            pool.wait_ge(slots_ready, 1)
            pool.wait_ge(zero_out, 16)
            for i in range(NT):
                for j in range(TOPK):
                    pool.indirect_dma_start(out=io["slot_token"], out_offset=bass.IndirectOffsetOnAxis(ap=slots_i[:, i, j:j + 1], axis=0),
                                            in_=tok[:, i:i + 1], in_offset=None).then_inc(tok_out, 16)
            pool.wait_ge(tok_out, 16 * NT * TOPK)

        tables.close()


def experts(nc, sems, io, per):
    with ExitStack() as ctx:
        m = Mem(nc, ctx, "ex")
        NB = NBLK + 1
        wg = [m.sb(f"wg{s}", [P, KD, FF]) for s in range(2)]
        wu = [m.sb(f"wu{s}", [P, KD, FF]) for s in range(2)]
        wd = [m.sb(f"wd{s}", [P, 2, D]) for s in range(2)]
        xg = [m.sb(f"xg{s}", [P, D]) for s in range(2)]
        xT = [m.sb(f"xT{s}", [P, KD, P]) for s in range(2)]
        y = [m.sb(f"y{s}", [P, D]) for s in range(2)]
        sg = m.sb("sg", [P, FF])
        hid = m.sb("hid", [P, FF])
        hidT = m.sb("hidT", [P, 2, P])
        be = m.sb("be", [1, P], I32)
        idx_b = m.sb("idx_b", [P, P], I32)
        idx_f = m.sb("idx_f", [P, P])
        idx = m.sb("idx", [P, P], I32)
        idx_now = [m.sb(f"idx_now{s}", [P, 1], I32) for s in range(2)]
        T0, T1, H, O0, O1 = (m.ps(x) for x in ("T0", "T1", "H", "O0", "O1"))
        S = [m.ps(f"S{s}") for s in range(2)]
        q = {n: sems(n) for n in ("be_in idx_in idx_conv idx_turned idx_ready turned xT_done gu_sum sig_done hid_part hid_done "
                                  "turnedS hidT_done down_sum y_done idx_copied passed").split()}
        wg_in, wd_in, x_in, y_out = ([sems(f"{x}{s}") for s in range(2)] for x in ("wg_in", "wd_in", "x_in", "y_out"))
        block = ctx.enter_context(nc.Block())

        def wait(eng, name, b, per_block, k):
            v = b * per_block + k
            if not (isinstance(v, int) and v <= 0):
                eng.wait_ge(q[name], v)

        def blocks(eng, body):
            for b in range(2):
                body(b, b)
            with eng.Fori(1, NB // 2) as j:
                for s in range(2):
                    body(2 * j + s, s)

        @block.sync
        def _(sp):
            sp.dma_start(be[:], io["block_expert"]).then_inc(q["be_in"], 16)
            sp.dma_start(idx_b[:], io["slot_token"].rearrange("(b p) o -> b (p o)", p=P)).then_inc(q["idx_in"], 16)
            sp.wait_ge(q["be_in"], 16)

            def load(b, s):
                e = sp.value_load(be[0:1, bass.ds(b, 1)], min_val=0, max_val=NE - 1)
                wait(sp, "gu_sum", b - 2, 1, 1)
                for dst, src in ((wg, "w_e_gate"), (wu, "w_e_up")):
                    sp.dma_start(dst[s][:].rearrange("p k f -> p (k f)"),
                                 io[src][bass.ds(e, 1)].rearrange("o (p k) f -> p (o k f)", p=P)).then_inc(wg_in[s], 16)
                wait(sp, "down_sum", b - 2, 2, 2)
                sp.dma_start(wd[s][:].rearrange("p k f -> p (k f)"),
                             io["w_e_down"][bass.ds(e, 1)].rearrange("o (p k) d -> p (o k d)", p=P)).then_inc(wd_in[s], 16)

            blocks(sp, load)

        @block.gpsimd
        def _(pool):
            pool.wait_ge(q["idx_ready"], 1)

            def gather(b, s):
                wait(pool, "turned", b - 2, 2, 2)
                if isinstance(b, int) and b < 2:
                    pass
                else:
                    pool.wait_ge(x_in[s], 16 * (b - s) // 2 if isinstance(b, int) else 8 * (b - s))
                pool.tensor_copy(idx_now[s][:], idx[:, bass.ds(b, 1)]).then_inc(q["idx_copied"], 1)
                wait(pool, "idx_copied", b, 1, 1)
                pool.sem_inc(q["passed"], 1)
                pool.indirect_dma_start(out=xg[s][:], out_offset=None, in_=io["h2"],
                                        in_offset=bass.IndirectOffsetOnAxis(ap=idx_now[s][:], axis=0)).then_inc(x_in[s], 16)

            blocks(pool, gather)

        @block.tensor
        def _(pe):
            ident = per["ident"]
            pe.wait_ge(q["idx_conv"], 1)
            pe.transpose(H[:, 0:P], idx_f[:], ident[:]).then_inc(q["idx_turned"], 1)
            pe.wait_ge(q["idx_ready"], 1)

            def turn(b, s):
                pe.wait_ge(x_in[s], 8 * (b - s) + 16)
                wait(pe, "xT_done", b - 1, 2, 2)
                for k in range(KD):
                    mm = pe.transpose((T0, T1)[k // 4][:, (k % 4) * P:(k % 4 + 1) * P], xg[s][:, k:D:KD], ident[:])
                    if k % 4 == 3:
                        mm.then_inc(q["turned"], 1)

            def gate_up(b, s):
                pe.wait_ge(wg_in[s], 16 * (b - s) + 32)
                wait(pe, "xT_done", b, 2, 2)
                wait(pe, "hid_done", b - 2, 1, 1)
                for w, c0 in ((wg, 0), (wu, FF)):
                    for k in range(KD):
                        mm = pe.matmul(S[s][:, c0:c0 + FF], xT[s][:, k, :], w[s][:, k, :], start=(k == 0), stop=(k == KD - 1))
                mm.then_inc(q["gu_sum"], 1)

            def down(b, s):
                wait(pe, "hid_done", b, 1, 1)
                wait(pe, "hidT_done", b - 1, 1, 1)
                for k in range(2):
                    mm = pe.transpose(H[:, k * P:(k + 1) * P], hid[:, k:FF:2], ident[:])
                mm.then_inc(q["turnedS"], 1)
                wait(pe, "hidT_done", b, 1, 1)
                pe.wait_ge(wd_in[s], 8 * (b - s) + 16)
                for n, bank in enumerate((O0, O1)):
                    wait(pe, "y_done", b - 1, 2, n + 1)
                    for k in range(2):
                        mm = pe.matmul(bank[:], hidT[:, k, :], wd[s][:, k, n * 512:(n + 1) * 512], start=(k == 0), stop=(k == 1))
                    mm.then_inc(q["down_sum"], 1)

            turn(0, 0)

            def body(b, s):
                gate_up(b, s)
                turn(b + 1, 1 - s)
                down(b, s)

            for b in range(2):
                body(b, b)
            with pe.Fori(1, NB // 2 - 1) as j:
                for s in range(2):
                    body(2 * j + s, s)
            body(NB - 2, 0)
            gate_up(NB - 1, 1)
            down(NB - 1, 1)

        @block.scalar
        def _(act):
            def x_copy(b, s):
                wait(act, "gu_sum", b - 2, 1, 1)
                for n, bank in enumerate((T0, T1)):
                    wait(act, "turned", b, 2, n + 1)
                    act.copy(xT[s][:, 4 * n:4 * n + 4].rearrange("p k t -> p (k t)"), bank[:]).then_inc(q["xT_done"], 1)

            def rest(b, s):
                wait(act, "gu_sum", b, 1, 1)
                wait(act, "hid_part", b - 1, 1, 1)
                act.activation(sg[:], S[s][:, 0:FF], ACT.Sigmoid).then_inc(q["sig_done"], 1)

            def tail(b, s):
                wait(act, "turnedS", b, 1, 1)
                wait(act, "down_sum", b - 1, 2, 2)
                act.copy(hidT[:].rearrange("p k t -> p (k t)"), H[:, 0:2 * P]).then_inc(q["hidT_done"], 1)
                wait(act, "y_done", b, 2, 2)
                act.dma_start(io["eslots"][bass.ds(b * P, P)], y[s][:]).then_inc(y_out[s], 16)

            x_copy(0, 0)

            def body(b, s):
                rest(b, s)
                x_copy(b + 1, 1 - s)
                tail(b, s)

            for b in range(2):
                body(b, b)
            with act.Fori(1, NB // 2 - 1) as j:
                for s in range(2):
                    body(2 * j + s, s)
            body(NB - 2, 0)
            rest(NB - 1, 1)
            tail(NB - 1, 1)
            for s in range(2):
                act.wait_ge(y_out[s], 16 * NB // 2)

        @block.vector
        def _(dve):
            dve.wait_ge(q["idx_in"], 16)
            dve.tensor_copy(idx_f[:], idx_b[:]).then_inc(q["idx_conv"], 1)
            dve.wait_ge(q["idx_turned"], 1)
            dve.tensor_copy(idx[:], H[:, 0:P]).then_inc(q["idx_ready"], 1)

            def body(b, s):
                wait(dve, "sig_done", b, 1, 1)
                wait(dve, "turnedS", b - 1, 1, 1)
                dve.tensor_tensor(hid[:], sg[:], S[s][:, 0:FF], ALU.mult).then_inc(q["hid_part"], 1)
                wait(dve, "hid_part", b, 1, 1)
                dve.tensor_tensor(hid[:], hid[:], S[s][:, FF:2 * FF], ALU.mult).then_inc(q["hid_done"], 1)
                if not (isinstance(b, int) and b < 2):
                    dve.wait_ge(y_out[s], 8 * (b - s))
                for n, bank in enumerate((O0, O1)):
                    wait(dve, "down_sum", b, 2, n + 1)
                    dve.tensor_copy(y[s][:, n * 512:(n + 1) * 512], bank[:]).then_inc(q["y_done"], 1)

            blocks(dve, body)


def combine(nc, sems, io, per):
    with ExitStack() as ctx:
        m = Mem(nc, ctx, "co")
        yg = m.sb("yg", [P, TOPK, D])
        idx_now = m.sb("cidx", [P, TOPK], U32)
        gnow = m.sb("gnow", [P, TOPK])
        base = m.sb("cbase", [P, D])
        acc = m.sb("acc", [P, D])
        lnr = m.sb("clnr", [P, 2, D])
        junk = m.sb("cjunk", [P, D])
        o = m.sb("o", [P, D])
        stat = m.sb("cstat", [P, 4])
        q = {n: sems(n) for n in "ln_in base_in idx_copied added acc_done mean_sum mu var_sum ln_var rooted out_done stored dco passed".split()}
        y_in = [sems(f"y_in{j}") for j in range(TOPK)]
        block = ctx.enter_context(nc.Block())
        OWN = 5

        def wait(eng, name, i, per_tile, k):
            v = i * per_tile + k
            if not (isinstance(v, int) and v <= 0):
                eng.wait_ge(q[name], v)

        def tiles(eng, body):
            body(0)
            with eng.Fori(1, NT) as i:
                body(i)

        @block.sync
        def _(sp):
            sp.dma_start(lnr[:].rearrange("p a d -> p (a d)"), io["ln_rows"][2 * D:4 * D].partition_broadcast(P)).then_inc(q["ln_in"], 16)

            def body(i):
                wait(sp, "acc_done", i - 1, 1, 1)
                sp.dma_start(base[:], io["base"][bass.ds(i * P, P)]).then_inc(q["base_in"], 16)

            tiles(sp, body)

        @block.gpsimd
        def _(pool):
            def body(i):
                for j in range(TOPK):
                    if not (isinstance(i, int) and i == 0):
                        pool.wait_ge(y_in[j], 16 * i)
                pool.tensor_copy(idx_now[:], per["slots_i"][:, bass.ds(i, 1)].rearrange("p o j -> p (o j)")).then_inc(q["idx_copied"], 1)
                wait(pool, "idx_copied", i, 1, 1)
                for j in range(TOPK):
                    wait(pool, "added", i - 1, TOPK, j + 1)
                    pool.sem_inc(q["passed"], 1)
                    pool.indirect_dma_start(out=yg[:, j, :], out_offset=None, in_=io["eslots"],
                                            in_offset=bass.IndirectOffsetOnAxis(ap=idx_now[:, j:j + 1], axis=0)).then_inc(y_in[j], 16)

            tiles(pool, body)

        @block.vector
        def _(dve):
            dve.wait_ge(q["ln_in"], 16)
            c = Chain(dve, q["dco"], OWN)

            def body(i):
                c.start(i)
                c.do(dve.tensor_copy(gnow[:], per["gates"][:, bass.ds(i, 1)].rearrange("p o j -> p (o j)")))
                c.wait()
                wait(dve, "var_sum", i - 1, 1, 1)
                for j in range(TOPK):
                    dve.wait_ge(y_in[j], 16 * i + 16)
                    if j == 0:
                        dve.tensor_scalar(acc[:], yg[:, 0], gnow[:, 0:1], None, ALU.mult).then_inc(q["added"], 1)
                    else:
                        wait(dve, "added", i, TOPK, j)
                        dve.scalar_tensor_tensor(acc[:], yg[:, j], gnow[:, j:j + 1], acc[:], ALU.mult, ALU.add).then_inc(q["added"], 1)
                wait(dve, "added", i, TOPK, TOPK)
                c.do(dve.tensor_tensor(acc[:], acc[:], per["rows"][:, 3 * D:4 * D], ALU.mult))
                c.wait()
                dve.wait_ge(q["base_in"], 16 * i + 16)
                dve.tensor_tensor(acc[:], acc[:], base[:], ALU.add).then_inc(q["acc_done"], 1)
                wait(dve, "mean_sum", i, 1, 1)
                dve.tensor_scalar(stat[:, 1:2], stat[:, 0:1], -1.0 / D, None, ALU.mult).then_inc(q["mu"], 1)
                wait(dve, "var_sum", i, 1, 1)
                dve.tensor_scalar(stat[:, 2:3], stat[:, 2:3], 1.0 / D, LN_EPS, ALU.mult, ALU.add).then_inc(q["ln_var"], 1)
                wait(dve, "rooted", i, 1, 1)
                c.do(dve.reciprocal(stat[:, 3:4], stat[:, 3:4]))
                c.wait()
                if not (isinstance(i, int) and i == 0):
                    dve.wait_ge(q["stored"], 16 * i)
                c.do(dve.tensor_scalar(o[:], acc[:], stat[:, 1:2], stat[:, 3:4], ALU.add, ALU.mult))
                c.wait()
                c.do(dve.tensor_tensor(o[:], o[:], lnr[:, 0], ALU.mult))
                c.wait()
                c.end()
                dve.tensor_tensor(o[:], o[:], lnr[:, 1], ALU.add).then_inc(q["out_done"], 1)

            tiles(dve, body)

        @block.scalar
        def _(act):
            def body(i):
                wait(act, "acc_done", i, 1, 1)
                act.activation(junk[:], acc[:], ACT.Identity, accum_out=stat[:, 0:1]).then_inc(q["mean_sum"], 1)
                wait(act, "mu", i, 1, 1)
                act.activation(junk[:], acc[:], ACT.Square, bias=stat[:, 1:2], accum_out=stat[:, 2:3]).then_inc(q["var_sum"], 1)
                wait(act, "ln_var", i, 1, 1)
                act.activation(stat[:, 3:4], stat[:, 2:3], ACT.Sqrt).then_inc(q["rooted"], 1)
                wait(act, "out_done", i, 1, 1)
                act.dma_start(io["out"][0, bass.ds(i * P, P)], o[:]).then_inc(q["stored"], 16)

            tiles(act, body)
            act.wait_ge(q["stored"], 16 * NT)


def program(nc, io):
    def scratch(name, shape, dt=F32):
        io[name] = nc.dram_tensor(name, shape, dt, kind="Internal").ap()

    scratch("u", [T + PADR, UW])
    scratch("yh", [L, CH])
    scratch("ys0", [L, RC + NH])
    scratch("ys1", [L, RC + NH])
    scratch("h2", [L, D])
    scratch("base", [L, D])
    scratch("block_expert", [1, P], I32)
    scratch("slot_token", [(NBLK + 1) * P, 1], I32)
    scratch("eslots", [(NBLK + 1) * P, D])
    with ExitStack() as ctx:
        def sems(name):
            return ctx.enter_context(nc.semaphore(name))

        keep = Mem(nc, ctx, "keep")
        per = {
            "ident": keep.sb("ident", [P, P]),
            "rows": keep.sb("rows", [P, 4 * D]),
            "cols": keep.sb("cols", [P, 16, 2]),
            "gates": keep.sb("gates", [P, NT, TOPK]),
            "slots_i": keep.sb("slots_i", [P, NT, TOPK], U32),
            "coef_now": keep.sb("coef_now", [P, 4]),
            "wd": keep.sb("wd", [P, T]),
            "ad": keep.sb("ad", [P, T]),
            "gd": keep.sb("gd", [P, T]),
        }
        id_in = sems("id_in")
        with nc.Block() as block:
            @block.sync
            def _(sp):
                sp.dma_start(per["ident"][:], io["ident"]).then_inc(id_in, 16)
                sp.wait_ge(id_in, 16)
        phases = [modulate, project, hyena, scan, merge, experts, combine]
        for phase in phases:
            own = []

            def sems_of_phase(name, own=own, tag=phase.__name__):
                own.append(nc.alloc_semaphore(f"{tag}_{name}"))
                return own[-1]

            phase(nc, sems_of_phase, io, per)
            nc.clear_and_free_semaphores(own)
            nc.all_engine_barrier()


def shape_constants():
    w = (np.arange(L) + 0.5) * np.pi / L
    n = np.arange(L)
    half = np.outer(n + 0.5, w)
    full = np.outer(n, w)
    col = lambda a: np.ascontiguousarray(a.reshape(8, P, 8, P).transpose(2, 1, 0, 3))
    con = {
        "ident": np.eye(P),
        "dft_cos": np.cos(half).reshape(8, P, L).transpose(1, 0, 2),
        "dft_sin": np.sin(half).reshape(8, P, L).transpose(1, 0, 2),
        "fil_cos": col(np.cos(full)),
        "fil_sin": col(-np.sin(full)),
    }
    t = np.linspace(0.0, 1.0, L)
    bands = np.linspace(1e-4, 15, 16)
    ang = (2.0 * np.pi / L) * n[:, None] * bands[None]
    con["posT"] = np.concatenate([t[:, None], np.cos(ang), -np.sin(ang)], 1).T
    deltas = np.abs(np.linspace(math.log(1e-2) / 1.5, math.log(1e-2) / 0.3, CH))
    dec = np.exp(-t[:, None] * deltas[None]) / L
    dec1 = dec.copy()
    dec1[0] = 0.0
    con["window"] = np.concatenate([dec, dec1], 1).reshape(8, P, 2 * CH).transpose(1, 0, 2)
    tri = np.zeros((P, 2, C))
    i = np.arange(C)
    tri[:C, 0] = i[:, None] <= i[None]
    tri[:C, 1] = i[:, None] < i[None]
    tri[C:, 0] = i[:, None] >= i[None]
    tri[C:, 1] = i[:, None] > i[None]
    both = lambda a: np.concatenate([np.where(np.arange(P)[:, None] < C, a, 0), np.where(np.arange(P)[:, None] < C, 0, a)], 1)
    bd = lambda a: np.stack([both(a[:, n]) for n in range(a.shape[1])], 1)
    con["tri"] = bd(tri)[:, 0] * LD
    con["tot"] = both(np.full((P, 1), LD))
    con["causal"] = np.tile(bd(tri[:, ::-1]).reshape(P, 1, 2, P), (1, 4, 1, 1))
    lv = np.zeros((P, 7, C))
    for s in range(6):
        same = (i[:, None] // 2 ** (s + 1)) == (i[None] // 2 ** (s + 1))
        off = same & ((i[:, None] // 2 ** s) != (i[None] // 2 ** s))
        lv[:C, s] = (off & (i[:, None] > i[None])) | (i[:, None] == i[None])
        lv[C:, s] = (off & (i[:, None] < i[None])) | (i[:, None] == i[None])
    lv[:C, 6] = lv[:C, 0].T
    lv[C:, 6] = lv[C:, 0].T
    con["level"] = lv[:, :6]
    con["levelbd"] = bd(lv[:, [6, 1, 2, 3, 4, 5]]).reshape(P, 6, 2, C)
    con["eye2"] = np.concatenate([np.eye(C), np.eye(C)], 0)
    con["rank_tri"] = (np.arange(P)[:, None] < np.arange(P)[None])
    con["iota_e"] = np.tile(np.arange(NE), (P, 1))
    con["iota_p"] = np.arange(P)[:, None]
    con["thresh"] = np.tile(np.arange(8) * P, (P, 1))
    con["causal"] = con["causal"].reshape(P, 4, 2, 2, C)
    return {k: np.ascontiguousarray(v, np.float32) for k, v in con.items()}


def layout(a):
    g = {k: np.asarray(v) for k, v in a.items()}
    v = {k: x[0] for k, x in g.items() if k not in ("c", "c_ctx", "x", "ctx")}
    both = np.concatenate([g["ctx"][0], g["x"][0]], 0)
    cols = lambda r, k: r.reshape(k, P).T
    coef = np.zeros((P, 27, 4), np.float32)
    coef[:, :6, 1] = 1.0
    for j in range(3):
        coef[:, 6:12, j] = cols(v["hy_sconv_w"][j], 6)
    coef[:, 6:12, 3] = cols(v["hy_sconv_b"], 6)
    coef[:, 12:, 0] = cols(v["rw_mu"][0], 15)
    coef[:, 12:, 1] = 1.0
    coef[:, 12:, 2] = cols(v["rw_mu"][1], 15)
    two = lambda a: np.concatenate([np.broadcast_to(a[0], (C, RC)), np.broadcast_to(a[1], (C, RC))], 0)
    out = {
        "c_cols": np.stack([cols(g["c"][0], KD), cols(g["c_ctx"], KD)], 2),
        "w_ada": v["w_ada"],
        "b_cols": cols(v["b_ada"][:2 * D], 16),
        "b_rows": v["b_ada"][2 * D:],
        "hT": both.T.reshape(KD, P, T).transpose(1, 0, 2),
        "x": g["x"][0],
        "w_in": v["w_in"].reshape(KD, P, 27, P).transpose(2, 1, 0, 3),
        "coef": coef,
        "hf_w1": v["hf_w1"], "hf_w2": v["hf_w2"], "hf_w3": v["hf_w3"],
        "hf_b": np.stack([v["hf_b1"], v["hf_b2"], v["hf_b3"], v["hf_freq"]], 1),
        "hf_wout": v["hf_wout"],
        "hf_skip": v["hf_skip"].reshape(-1),
        "w0": two(v["rw_w0"]), "a0": two(v["rw_a0"]),
        "w_up": v["rw_w_up"].reshape(P, RC), "a_up": v["rw_a_up"].reshape(P, RC),
        "g_up": v["rw_g_up"],
        "rw_rows": np.concatenate([v["rw_k_k"], v["rw_k_a"], v["rw_r_k"].reshape(-1)]),
        "mix_rows": np.concatenate([v["conv_a"].reshape(-1), v["mix_norm_g"], v["rw_lnx_g"], v["rw_lnx_b"]]),
        "w_out": v["w_out"].reshape(KD, P, D).transpose(1, 0, 2),
        "ln_rows": np.concatenate([v["ln_g"][0], v["ln_b"][0], v["ln_g"][1], v["ln_b"][1]]),
        "w_router": v["w_router"].reshape(KD, P, NE).transpose(1, 0, 2),
        "e_bias": v["e_bias"],
        "w_e_gate": v["w_e_gate"], "w_e_up": v["w_e_up"], "w_e_down": v["w_e_down"],
        "w_s_gu": np.concatenate([v["w_s_gate"], v["w_s_up"]], 1).reshape(KD, P, 2 * FF).transpose(1, 0, 2),
        "w_s_down": v["w_s_down"].reshape(2, P, D).transpose(1, 0, 2),
    }
    out.update(shape_constants())
    return {k: np.ascontiguousarray(x) for k, x in out.items()}


def kernel(**inputs):
    import concourse.bacc as bacc
    from concourse.bass_utils import run_bass_kernel_spmd

    nc = bacc.Bacc("TRN2", target_bir_lowering=False, num_devices=1)
    arrays = {f"in_{k}": v for k, v in layout(inputs).items()}
    io = {k[3:]: nc.dram_tensor(k, v.shape, mybir.dt.from_np(v.dtype), kind="ExternalInput").ap() for k, v in arrays.items()}
    io["out"] = nc.dram_tensor("out_0", [1, L, D], F32, kind="ExternalOutput").ap()
    program(nc, io)
    r = run_bass_kernel_spmd(nc, [arrays], core_ids=[0])
    return r.results[0]["out_0"]
```

```python
from contextlib import ExitStack

import math

import numpy as np

import concourse.bass as bass
from concourse import mybir

F32 = mybir.dt.float32
I32 = mybir.dt.int32
U32 = mybir.dt.uint32
ALU = mybir.AluOpType
ACT = mybir.ActivationFunctionType
AX_X = mybir.AxisListType.X

P = 128
D = 1024
KD = D // P
L = 1024
LC = 256
T = L + LC
NT = L // P
GRID = 64
NE = 64
TOPK = 8
FF = 256
NBLK = NE + L * TOPK // P - 1
TAB = 4
HD = 64
NH = 8
RC = NH * HD
CH = 256
UW = 6 * CH + 3 * RC
PADR = GRID
ALPHA = 2.0 ** 0.25
LN_EPS = 1e-5
GN_EPS = 64e-5
ROUTED = 2.5
C = 64
LD = -math.exp(-0.5)
TWO_PI = 2.0 * math.pi
MAGIC = 1.5 * 2.0 ** 23


class Mem:

    def __init__(self, nc, ctx, tag):
        self.nc, self.ctx, self.tag = nc, ctx, tag

    def sb(self, name, shape, dt=F32):
        return self.ctx.enter_context(self.nc.sbuf_tensor(f"{self.tag}_{name}", shape, dt))

    def ps(self, name, cols=512):
        return self.ctx.enter_context(self.nc.psum_tensor(f"{self.tag}_{name}", [P, cols], F32))


class Count:

    def __init__(self, sem):
        self.sem, self.n = sem, 0

    def inc(self, ins, by=1):
        ins.then_inc(self.sem, by)
        self.n += by
        return self.n


def bc(ap, at, n):
    shape = list(ap.shape)
    u = ap.unsqueeze(at)
    return u.broadcast_to(shape[:at] + [n] + shape[at:])


def modulate(nc, sems, io, per):
    with ExitStack() as ctx:
        m = Mem(nc, ctx, "mod")
        NG = 12
        cc = m.sb("cc", [P, KD, 2])
        sg = m.sb("sg", [P, KD, 2])
        sc = m.sb("sc", [P, KD, 2])
        scb = m.sb("scb", [P, KD, P])
        bcol = m.sb("bcol", [P, 16])
        NS = 3
        w = [m.sb(f"w{s}", [P, KD, 512]) for s in range(NS)]
        two = m.sb("two", [2, 2 * D])
        cps = m.ps("cps")
        rps = [m.ps(f"rps{s}") for s in range(2)]
        c_in, w_in, acted, prepared, dve_did = (sems(x) for x in ("c_in", "w_in0", "acted", "prepared", "dve_did"))
        w_in = [w_in, sems("w_in1"), sems("w_in2")]
        x_in = sems("hT_in")
        NF = 2 * CH
        pos = m.sb("pos", [33, L])
        w1 = m.sb("hw1", [33, 64])
        w23 = m.sb("hw23", [64, 2, 64])
        hb = m.sb("hb", [64, 4])
        wout = m.sb("hwout", [64, 4 * CH])
        win = m.sb("win", [P, NT, NF])
        h = [m.sb(f"h{s}", [64, L]) for s in range(2)]
        q = m.sb("q", [64, L])
        hw = m.sb("hw", [P, 2, NF])
        both = per["filters"]
        banks = [m.ps(f"bank{s}") for s in range(4)]
        pos_in, wout_in, lin, mapped, stp, out_done, windowed, added = (
            sems(x) for x in ("pos_in", "wout_in", "lin", "mapped", "step", "out_done", "windowed", "added"))
        used = sems("ada_used")
        b_in = sems("b_in")
        two_taken, columns = sems("two_taken"), sems("columns")
        block = ctx.enter_context(nc.Block())

        @block.sync
        def _(sp):
            sp.dma_start(cc[:], io["c_cols"]).then_inc(c_in, 16)
            for dst, src in ((pos[:], io["posT"]), (w1[:], io["hf_w1"]), (w23[:, 0, :], io["hf_w2"]),
                             (w23[:, 1, :], io["hf_w3"]), (hb[:], io["hf_b"])):
                sp.dma_start(dst, src).then_inc(pos_in, 16)
            for g in range(NG):
                if g == NS:
                    sp.dma_start(wout[:], io["hf_wout"]).then_inc(wout_in, 16)
                    sp.dma_start(win[:], io["window"]).then_inc(wout_in, 16)
                if g >= NS:
                    sp.wait_ge(used, g - NS + 1)
                sp.dma_start(w[g % NS][:], io["w_ada"][:, g * 512:(g + 1) * 512]
                             .rearrange("(k p) n -> p k n", p=P)).then_inc(w_in[g % NS], 16)
            for k in range(KD):
                sp.dma_start(per["hT"][:, k, :], io["hT"][:, k, :]).then_inc(x_in, 16)
            sp.wait_ge(x_in, 16 * KD)

        @block.scalar
        def _(act):
            act.dma_start(bcol[:], io["b_cols"]).then_inc(b_in, 16)
            act.dma_start(per["rows"][:], io["b_rows"].partition_broadcast(P)).then_inc(b_in, 16)
            act.wait_ge(c_in, 16)
            act.activation(sg[:], cc[:], ACT.Sigmoid).then_inc(acted, 1)
            for layer in range(3):
                act.wait_ge(stp, 7 * layer + 7)
                act.activation(h[layer % 2][:], h[layer % 2][:], ACT.Sin).then_inc(mapped, 1)

        @block.vector
        def _(dve):
            dve.wait_ge(acted, 1)
            dve.tensor_tensor(sc[:], cc[:], sg[:], ALU.mult).then_inc(dve_did, 1)
            dve.wait_ge(dve_did, 1)
            dve.tensor_copy(scb[:], bc(sc[:, :, 0], 2, P)).then_inc(prepared, 1)
            st = Count(stp)

            def layer_argument(layer):
                dve.wait_ge(lin, layer + 1)
                dst = h[layer % 2]
                for n in range(2):
                    v = st.inc(dve.tensor_scalar(dst[:, n * 512:(n + 1) * 512], banks[n][0:64, :], hb[:, layer:layer + 1],
                                                 hb[:, 3:4], ALU.add, ALU.mult))
                dve.wait_ge(stp, v)
                dve.wait_ge(stp, st.inc(dve.tensor_scalar(q[:], dst[:], 1.0 / TWO_PI, MAGIC, ALU.mult, ALU.add)))
                dve.wait_ge(stp, st.inc(dve.tensor_scalar(q[:], q[:], MAGIC, None, ALU.subtract)))
                dve.wait_ge(stp, st.inc(dve.scalar_tensor_tensor(dst[:], q[:], -6.28125, dst[:], ALU.mult, ALU.add)))
                dve.wait_ge(stp, st.inc(dve.scalar_tensor_tensor(dst[:], q[:], -(TWO_PI - 6.28125), dst[:], ALU.mult, ALU.add)))
                st.inc(dve.tensor_scalar(dst[:], dst[:], 3.1415925, -3.1415925, ALU.min, ALU.max))

            def window(t):
                for o in range(2):
                    n = 2 * t + o
                    dve.wait_ge(out_done, n + 1)
                    if n >= 2:
                        dve.wait_ge(added, 2 * (n - 1))
                    dve.tensor_tensor(hw[:, n % 2, :], banks[2 + n % 2][:], win[:, t, :], ALU.mult).then_inc(windowed, 1)
                    dve.wait_ge(windowed, n + 1)
                    for part, op in ((0, ALU.add), (1, ALU.subtract)):
                        dve.tensor_tensor(both[:, t, part, o * CH:(o + 1) * CH], hw[:, n % 2, 0:CH], hw[:, n % 2, CH:NF],
                                          op).then_inc(added, 1)

            for g in range(4):
                dve.wait_ge(used, g + 1)
                dve.tensor_copy(two[:, g * 512:(g + 1) * 512], rps[g % 2][0:2, :]).then_inc(two_taken, 1)
                if g < 3:
                    layer_argument(g)
            dve.wait_ge(columns, 1)
            dve.wait_ge(b_in, 32)
            dve.tensor_tensor(per["cols"][:], cps[:, 0:32].rearrange("p (m s) -> p m s", s=2),
                              bc(bcol[:], 2, 2), ALU.add).then_inc(dve_did, 1)
            dve.wait_ge(dve_did, 2)
            dve.tensor_scalar(per["cols"][:, 8:16, :], per["cols"][:, 8:16, :], 1.0, None, ALU.add)
            for g in range(4, NG):
                dve.wait_ge(used, g + 1)
                rows = per["rows"][:, (g - 4) * 512:(g - 3) * 512]
                dve.tensor_tensor(rows, rows, rps[g % 2][:], ALU.add).then_inc(dve_did, 1)
                if 5 <= g < 9:
                    if g == 5:
                        dve.wait_ge(wout_in, 32)
                    window(2 * (g - 5))
                    window(2 * (g - 5) + 1)
            dve.wait_ge(dve_did, 2 + NG - 4)
            dve.tensor_scalar(per["rows"][:, 2048:3072], per["rows"][:, 2048:3072], 1.0, None, ALU.add)

        @block.tensor
        def _(pe):
            def layer_product(layer):
                if layer:
                    pe.wait_ge(mapped, layer)
                else:
                    pe.wait_ge(pos_in, 80)
                for n in range(2):
                    lhsT = w1[:] if layer == 0 else w23[:, layer - 1, :]
                    rhs = pos[:, n * 512:(n + 1) * 512] if layer == 0 else h[(layer - 1) % 2][:, n * 512:(n + 1) * 512]
                    mm = pe.matmul(banks[n][0:64, :], lhsT, rhs, start=True, stop=True)
                mm.then_inc(lin, 1)

            def filters(t):
                for o in range(2):
                    n = 2 * t + o
                    if n >= 2:
                        pe.wait_ge(windowed, n - 1)
                    pe.matmul(banks[2 + n % 2][:], h[0][:, t * P:(t + 1) * P], wout[:, o * NF:(o + 1) * NF],
                              start=True, stop=True).then_inc(out_done, 1)

            pe.wait_ge(prepared, 1)
            for g in range(NG):
                pe.wait_ge(w_in[g % NS], 16 * (g // NS + 1))
                if g < 4:
                    if g >= 2:
                        pe.wait_ge(two_taken, g - 1)
                    for k in range(KD):
                        mm = pe.matmul(rps[g % 2][0:2, :], sc[:, k, :], w[g % NS][:, k, :],
                                       start=(k == 0), stop=(k == KD - 1))
                else:
                    if g < 6:
                        pe.wait_ge(two_taken, g - 1)
                    if g == 5:
                        for q in range(16):
                            mm = pe.transpose(cps[:, 2 * q:2 * q + 2], two[:, q * P:(q + 1) * P], per["ident"][0:2, 0:2])
                        mm.then_inc(columns, 1)
                    if g >= 6:
                        pe.wait_ge(dve_did, 2 + g - 5)
                    for k in range(KD):
                        mm = pe.matmul(rps[g % 2][:], scb[:, k, :], w[g % NS][:, k, :],
                                       start=(k == 0), stop=(k == KD - 1))
                mm.then_inc(used, 1)
                if g < 3:
                    layer_product(g)
                if 5 <= g < 9:
                    if g == 5:
                        pe.wait_ge(mapped, 3)
                        pe.wait_ge(wout_in, 32)
                    filters(2 * (g - 5))
                    filters(2 * (g - 5) + 1)


def project(nc, sems, io, per):
    with ExitStack() as ctx:
        m = Mem(nc, ctx, "prj")
        hT = per["hT"]
        w = [m.sb(f"w{s}", [P, KD, P]) for s in range(2)]
        coef = m.sb("coef", [P, 27, 4])
        uw = T + 3
        ub = [m.sb(f"ub{s}", [P, uw]) for s in range(2)]
        cv = [m.sb(f"cv{s}", [P, T]) for s in range(2)]
        ut = [m.sb(f"ut{s}", [P, 10, P]) for s in range(2)]
        zero = m.sb("zero", [GRID, 2 * CH])
        acc = [m.ps(f"acc{s}", 3 * 512) for s in range(2)]
        tp = [m.ps(f"tp{s}") for s in range(2)]
        coef_in, h_done, coef_done, zeroed, z_out = (
            sems(x) for x in ("coef_in", "h_done", "coef_done", "zeroed", "z_out"))
        w_in, summed, copied, convolved, stored = (
            [sems(f"{x}{s}") for s in range(2)] for x in ("pw_in", "summed", "copied", "convolved", "stored"))
        tp_full = sems("tp_full")
        tp_free = sems("tp_free")
        step = sems("conv_step")
        block = ctx.enter_context(nc.Block())
        LAT = [(LC + 512 * n, 512) for n in range(2)]
        TILES_LAT, TILES = 16, 24

        def parts(ctx_too):
            return ([(0, LC)] if ctx_too else []) + LAT

        def groups(ctx_too):
            return ([(0, 2)] if ctx_too else []) + [(2, 6), (6, 10)]

        def gbase(j, s, ctx_too):
            return 3 * (2 * j + s) - TILES_LAT if ctx_too else 2 * (2 * j + s)

        LAT_END, END = TILES_LAT // 2, TILES // 2
        LOOPS = [(0, LAT_END, False), (LAT_END, END, True)]

        @block.sync
        def _(sp):
            for lo, hi, ctx_too in LOOPS:
                with sp.Fori(lo, hi) as j:
                    for s in range(2):
                        sp.wait_ge(summed[s], j + 1)
                        sp.dma_start(w[s][:], io["w_in"][bass.ds(2 * j + s, 1)].rearrange("o p k n -> p (o k) n")
                                     ).then_inc(w_in[s], 16)
            for n in range(3):
                s = n % 2
                sp.wait_ge(summed[s], 12 + n // 2 + 1)
                sp.dma_start(w[s][:], io["w_in"][24 + n]).then_inc(w_in[s], 16)

        @block.tensor
        def _(pe):
            for s in range(2):
                pe.sem_inc(summed[s], 1)
            pe.wait_ge(h_done, KD)

            def sums(s, j, ctx_too):
                pe.wait_ge(w_in[s], 16 * (j + 1))
                pe.wait_ge(copied[s], j + 1)
                for n, (t0, tn) in enumerate(parts(ctx_too)):
                    b = 512 * (n if ctx_too else n + 1)
                    for k in range(KD):
                        mm = pe.matmul(acc[s][:, b:b + tn], w[s][:, k, :], hT[:, k, t0:t0 + tn],
                                       start=(k == 0), stop=(k == KD - 1))
                mm.then_inc(summed[s], 1)

            def turns(s, j, ctx_too):
                pe.wait_ge(convolved[s], j + 2)
                for q, (a, b) in enumerate(groups(ctx_too)):
                    g = gbase(j, s, ctx_too) + q
                    pe.wait_ge(tp_free, g + 1)
                    bank = tp[(q + (s if ctx_too else 0)) % 2]
                    for t in range(a, b):
                        mm = pe.transpose(bank[:, (t - a) * P:(t - a + 1) * P], cv[s][:, t * P:(t + 1) * P],
                                          per["ident"][:])
                    mm.then_inc(tp_full, 1)

            sums(0, 0, False)
            sums(1, 0, False)
            turns(0, 0, False)
            with pe.Fori(1, LAT_END) as j:
                sums(0, j, False)
                turns(1, j - 1, False)
                sums(1, j, False)
                turns(0, j, False)
            sums(0, LAT_END, True)
            turns(1, LAT_END - 1, False)
            sums(1, LAT_END, True)
            turns(0, LAT_END, True)
            with pe.Fori(LAT_END + 1, END) as j:
                sums(0, j, True)
                turns(1, j - 1, True)
                sums(1, j, True)
                turns(0, j, True)
            sums(0, END, True)
            turns(1, END - 1, True)
            sums(1, END, True)
            sums(0, END + 1, False)

        @block.scalar
        def _(act):
            act.dma_start(coef[:], io["coef"]).then_inc(coef_in, 16)
            for k in range(1, KD, 2):
                for a, b, which in ((0, LC, 1), (LC, T, 0)):
                    ins = act.activation(hT[:, k, a:b], hT[:, k, a:b], ACT.Identity, bias=per["cols"][:, k, which:which + 1],
                                         scale=per["cols"][:, 8 + k, which:which + 1])
                ins.then_inc(h_done, 1)
            for s in range(2):
                act.sem_inc(copied[s], 1)
            act.sem_inc(tp_free, 2)
            for s in range(2):
                act.sem_inc(stored[s], 16)

            def copy(s, j, ctx_too):
                act.wait_ge(summed[s], j + 2)
                act.wait_ge(convolved[s], j + 1)
                if ctx_too:
                    act.copy(ub[s][:, 1:1 + LC], acc[s][:, 0:LC])
                act.copy(ub[s][:, 2 + LC:2 + LC + L], acc[s][:, 512:512 + L]).then_inc(copied[s], 1)

            def out(s, j, ctx_too):
                a0 = groups(ctx_too)[0][0]
                act.wait_ge(stored[s], 16 * (j + 1))
                for q, (a, b) in enumerate(groups(ctx_too)):
                    g = gbase(j, s, ctx_too) + q
                    act.wait_ge(tp_full, g + 1)
                    act.copy(ut[s][:, a:b, :], tp[(q + (s if ctx_too else 0)) % 2][:, 0:(b - a) * P]
                             .rearrange("p (t c) -> p t c", c=P)).then_inc(tp_free, 1)
                act.wait_ge(tp_free, gbase(j, s, ctx_too) + len(groups(ctx_too)) + 2)
                act.dma_start(io["u"][a0 * P:T, bass.ds((2 * j + s) * P, P)].rearrange("(t p) c -> p t c", p=P),
                              ut[s][:, a0:10, :]).then_inc(stored[s], 16)

            copy(0, 0, False)
            copy(1, 0, False)
            out(0, 0, False)
            with act.Fori(1, LAT_END) as j:
                copy(0, j, False)
                out(1, j - 1, False)
                copy(1, j, False)
                out(0, j, False)
            copy(0, LAT_END, True)
            out(1, LAT_END - 1, False)
            copy(1, LAT_END, True)
            out(0, LAT_END, True)
            with act.Fori(LAT_END + 1, END) as j:
                copy(0, j, True)
                out(1, j - 1, True)
                copy(1, j, True)
                out(0, j, True)
            copy(0, END, True)
            out(1, END - 1, True)
            copy(1, END, True)
            copy(0, END + 1, False)
            for s in range(2):
                act.wait_ge(stored[s], 16 * 13)

        @block.vector
        def _(dve):
            for s in range(2):
                dve.memset(ub[s][:], 0.0)
            dve.memset(zero[:], 0.0).then_inc(zeroed, 1)
            for k in range(0, KD, 2):
                for a, b, which in ((0, LC, 1), (LC, T, 0)):
                    ins = dve.tensor_scalar(hT[:, k, a:b], hT[:, k, a:b], per["cols"][:, 8 + k, which:which + 1],
                                            per["cols"][:, k, which:which + 1], ALU.mult, ALU.add)
                ins.then_inc(h_done, 1)
            dve.wait_ge(coef_in, 16)
            dve.tensor_tensor(coef[:, 12:27, 1], coef[:, 12:27, 1], coef[:, 12:27, 0], ALU.subtract).then_inc(coef_done, 1)
            dve.wait_ge(coef_done, 1)
            dve.tensor_tensor(coef[:, 12:27, 1], coef[:, 12:27, 1], coef[:, 12:27, 2], ALU.subtract).then_inc(coef_done, 1)
            dve.wait_ge(coef_done, 2)
            for s in range(2):
                dve.sem_inc(convolved[s], 1)

            cf = per["coef_now"]

            def conv(s, j, ctx_too, tile, n_step, last_ctx, out=None):
                dve.wait_ge(copied[s], j + 2)
                if out is None:
                    if not (isinstance(j, int) and j == 0):
                        dve.wait_ge(tp_full, gbase(j - 1, s, last_ctx) + len(groups(last_ctx)))
                    out = cv[s]
                dve.tensor_copy(cf[:], coef[:, bass.ds(tile, 1), :].rearrange("p o c -> p (o c)")).then_inc(step, 1)
                dve.wait_ge(step, n_step + 1)
                spans = ([(0, LC, 1)] if ctx_too else []) + [(LC, T, 2)]
                for a, b, sh in spans:
                    ins = dve.tensor_scalar(out[:, a:b], ub[s][:, a + sh:b + sh], cf[:, 1:2], cf[:, 3:4],
                                            ALU.mult, ALU.add)
                ins.then_inc(step, 1)
                dve.wait_ge(step, n_step + 2)
                for a, b, sh in spans:
                    ins = dve.scalar_tensor_tensor(out[:, a:b], ub[s][:, a + sh - 1:b + sh - 1], cf[:, 0:1], out[:, a:b],
                                                   ALU.mult, ALU.add)
                ins.then_inc(step, 1)
                dve.wait_ge(step, n_step + 3)
                for a, b, sh in spans:
                    ins = dve.scalar_tensor_tensor(out[:, a:b], ub[s][:, a + sh + 1:b + sh + 1], cf[:, 2:3], out[:, a:b],
                                                   ALU.mult, ALU.add)
                ins.then_inc(step, 1)
                dve.wait_ge(step, n_step + 4)
                dve.sem_inc(convolved[s], 1)

            for lo, hi, ctx_too in LOOPS:
                for s in range(2):
                    conv(s, lo, ctx_too, 2 * lo + s, 8 * lo + 4 * s, False)
                with dve.Fori(lo + 1, hi) as j:
                    for s in range(2):
                        conv(s, j, ctx_too, 2 * j + s, 8 * j + 4 * s, ctx_too)
            for n, ctx_too in ((0, True), (1, True), (2, False)):
                conv(n % 2, END + n // 2, ctx_too, TILES + n, 4 * (TILES + n), True, per[("wd", "ad", "gd")[n]])

        @block.gpsimd
        def _(pool):
            pool.wait_ge(zeroed, 1)
            pool.dma_start(io["u"][LC - GRID:LC, CH:3 * CH], zero[:]).then_inc(z_out, 16)
            pool.dma_start(io["u"][T:T + PADR, CH:3 * CH], zero[:]).then_inc(z_out, 16)
            pool.wait_ge(z_out, 32)


def hyena(nc, sems, io, per):
    with ExitStack() as ctx:
        m = Mem(nc, ctx, "hy")
        NF = 2 * CH
        z = m.sb("z", [P, NT, CH])
        x12 = m.sb("x12", [P, 2, NT, CH])
        K = m.sb("K", [P, NT, 2, 3, CH])
        skip = m.sb("skip", [P, 2, CH])
        work = m.sb("work", [P, 2, CH])
        banks = [m.ps(f"bank{s}") for s in range(6)]
        v_in, skip_in = sems("v_in"), sems("skip_in")
        dft_in = [sems(f"dft_in{s}") for s in range(2)]
        x_in = sems("x12_in")
        y_out = sems("yh_out")

        with ExitStack() as ctx1:
            m1 = Mem(nc, ctx1, "hf")
            fil = [m1.sb(f"fil{s}", [P, 2, NT, P]) for s in range(2)]
            kdone, ktaken = sems("kdone"), sems("ktaken")
            both = per["filters"]
            block = ctx1.enter_context(nc.Block())

            @block.sync
            def _(sp):
                for f in range(NT):
                    if f >= 2:
                        sp.wait_ge(kdone, f - 1)
                    sp.dma_start(fil[f % 2][:, 0], io["fil_cos"][f]).then_inc(dft_in[f % 2], 16)
                    sp.dma_start(fil[f % 2][:, 1], io["fil_sin"][f]).then_inc(dft_in[f % 2], 16)

            @block.tensor
            def _(pe):
                for f in range(NT):
                    pe.wait_ge(dft_in[f % 2], 32 * (f // 2 + 1))
                    if f >= 2:
                        pe.wait_ge(ktaken, 3 * (f - 1))
                    for part in range(2):
                        for t in range(NT):
                            mm = pe.matmul(banks[2 * (f % 2) + part][:], fil[f % 2][:, part, t, :], both[:, t, part, :],
                                           start=(t == 0), stop=(t == NT - 1))
                    mm.then_inc(kdone, 1)

            @block.scalar
            def _(act):
                act.dma_start(z[:], io["u"][LC:T, 3 * CH:4 * CH].rearrange("(t p) c -> p t c", p=P)).then_inc(v_in, 16)
                for o in range(2):
                    act.dma_start(x12[:, o], io["u"][LC:T, (4 + o) * CH:(5 + o) * CH].rearrange("(t p) c -> p t c", p=P)
                                  ).then_inc(x_in, 16)
                act.dma_start(skip[:].rearrange("p o c -> p (o c)"), io["hf_skip"].partition_broadcast(P)).then_inc(skip_in, 16)
                for f in range(NT):
                    act.wait_ge(kdone, f + 1)
                    for part, kinds in ((0, (0, 2)), (1, (1,))):
                        for kind in kinds:
                            act.copy(K[:, f, :, kind, :], banks[2 * (f % 2) + part][:].rearrange("p (o c) -> p o c", o=2)
                                     ).then_inc(ktaken, 1)
                act.wait_ge(v_in, 16)
                act.wait_ge(x_in, 32)
                act.wait_ge(skip_in, 16)
                act.wait_ge(ktaken, 3 * NT)

        with ExitStack() as ctx2:
            m2 = Mem(nc, ctx2, "hc")
            E = per["filters"][:, :, 0, 0:CH]
            F = per["filters"][:, :, 0, CH:NF]
            tmp = per["filters"][:, 0:2, 1, :].rearrange("p a (b c) -> p a b c", b=2)
            M = [m2.sb("cos", [P, NT, L]), m2.sb("sin", [P, NT, L])]
            fwd, mixed, inv, gated, stp = (sems(x) for x in ("fwd", "mixed", "inv", "gated", "cstep"))
            tab_in = [sems(f"tab_in{f}") for f in range(NT)]
            block = ctx2.enter_context(nc.Block())

            @block.sync
            def _(sp):
                for f in range(NT):
                    for part, name in ((0, "dft_cos"), (1, "dft_sin")):
                        sp.dma_start(M[part][:, :, f * P:(f + 1) * P], io[name][:, :, f * P:(f + 1) * P]).then_inc(tab_in[f], 16)
                sp.wait_ge(gated, 2 * NT)
                sp.dma_start(io["yh"].rearrange("(t p) c -> p t c", p=P), z[:]).then_inc(y_out, 16)
                sp.wait_ge(y_out, 16)

            @block.tensor
            def _(pe):
                for o in range(2):
                    if o:
                        pe.wait_ge(gated, NT)
                    for f in range(NT):
                        n = NT * o + f
                        if not o:
                            pe.wait_ge(tab_in[f], 32)
                        if n >= 2:
                            pe.wait_ge(mixed, n - 1)
                        for part in range(2):
                            for t in range(NT):
                                mm = pe.matmul(banks[n % 2][:, part * CH:(part + 1) * CH], M[part][:, t, f * P:(f + 1) * P],
                                               z[:, t, :], start=(t == 0), stop=(t == NT - 1))
                        mm.then_inc(fwd, 1)
                    pe.wait_ge(mixed, NT * (o + 1))
                    for t in range(NT):
                        n = NT * o + t
                        if n >= 2:
                            pe.wait_ge(gated, n - 1)
                        for f in range(NT):
                            for part, src in ((0, E), (1, F)):
                                mm = pe.matmul(banks[2 + n % 2][:, 0:CH], M[part][:, f, t * P:(t + 1) * P], src[:, f, :],
                                               start=(f == 0 and part == 0), stop=(f == NT - 1 and part == 1))
                        mm.then_inc(inv, 1)

            @block.vector
            def _(dve):
                st = Count(stp)
                for o in range(2):
                    for f in range(NT):
                        n = NT * o + f
                        dve.wait_ge(fwd, n + 1)
                        pq = banks[n % 2][:].rearrange("p (a c) -> p a c", a=2)
                        st.inc(dve.tensor_tensor(tmp[:, 0], pq, K[:, f, o, 0:2, :], ALU.mult))
                        v = st.inc(dve.tensor_tensor(tmp[:, 1], pq, K[:, f, o, 1:3, :], ALU.mult))
                        dve.wait_ge(stp, v)
                        st.inc(dve.tensor_tensor(E[:, f, :], tmp[:, 0, 0, :], tmp[:, 0, 1, :], ALU.add))
                        dve.tensor_tensor(F[:, f, :], tmp[:, 1, 1, :], tmp[:, 1, 0, :], ALU.subtract).then_inc(mixed, 1)
                        dve.wait_ge(mixed, n + 1)
                        dve.wait_ge(stp, st.n)
                    for t in range(NT):
                        n = NT * o + t
                        v = st.inc(dve.tensor_tensor(work[:, 0], z[:, t, :], skip[:, o, :], ALU.mult))
                        dve.wait_ge(inv, n + 1)
                        dve.wait_ge(stp, v)
                        dve.wait_ge(stp, st.inc(dve.tensor_tensor(work[:, 1], work[:, 0], banks[2 + n % 2][:, 0:CH], ALU.add)))
                        dve.tensor_tensor(z[:, t, :], work[:, 1], x12[:, o, t, :], ALU.mult).then_inc(gated, 1)
                        dve.wait_ge(gated, n + 1)


NSTEP = T // C


def scan(nc, sems, io, per):
    with ExitStack() as ctx:
        m = Mem(nc, ctx, "sc")
        H2 = NH // 2
        lora = m.sb("lora", [P, NSTEP, 2, C])
        lnow = m.sb("lnow", [P, 2, 2, C])
        w_up = m.sb("w_up", [P, RC])
        a_up = m.sb("a_up", [P, RC])
        wa0 = m.sb("wa0", [P, 2, RC])
        rows = m.sb("rows", [P, 3, RC])
        tri = m.sb("tri", [P, P])
        tot = m.sb("tot", [P, 2])
        causal = m.sb("causal", [P, H2, 2, 2, C])
        level = m.sb("level", [P, 6, C])
        levelbd = m.sb("levelbd", [P, 6, 2, C])
        eye = m.sb("eye", [P, C])
        rkv = [m.sb(f"rkv{s}", [P, 3, RC]) for s in range(2)]
        sig = m.sb("sig", [P, 2, RC])
        e_in, e_ng, e_ex = (m.sb(x, [P, RC]) for x in ("e_in", "e_ng", "e_ex"))
        kkr, sq, kk, kka, krest, rrk, akk, kd = (
            m.sb(x, [P, RC]) for x in ("kkr", "sq", "kk", "kka", "krest", "rrk", "akk", "kd"))
        ss, rn = m.sb("ss", [P, NH]), m.sb("rn", [P, NH])
        alpha, rho = m.sb("alpha", [P, RC]), m.sb("rho", [P, RC])
        beta = [m.sb(f"beta{s}", [P, NH, 2, HD]) for s in range(2)]
        kap = [m.sb(f"kap{s}", [P, NH, 2, HD]) for s in range(2)]
        arT = m.sb("arT", [P, NH, 2, C])
        arb = m.sb("arb", [P, NH, 2, 2, C])
        bT = m.sb("bT", [P, NH, P])
        kT = m.sb("kT", [P, NH, P])
        dec = [m.sb(f"dec{s}", [P, NH]) for s in range(2)]
        ab = [m.sb(f"ab{s}", [P, NH, 2, P]) for s in range(2)]
        ak = [m.sb(f"ak{s}", [P, NH, 2, P]) for s in range(2)]
        abi = m.sb("abi", [P, NH, P])
        dd = m.sb("dd", [P, 2, 2, H2 * C])
        dtb = m.sb("dtb", [P, NH, 2, C])
        xm = m.sb("xm", [P, 2, H2 * C])
        xb = m.sb("xb", [P, NH, 2, C])
        eyebd = per["ident"]
        gs = m.sb("gs", [P, RC])
        us = m.sb("us", [P, RC])
        st = m.sb("st", [P, RC])
        sm = m.sb("sm", [P, RC])
        yb = [m.sb(f"yb{s}", [P, RC + NH]) for s in range(2)]
        B = [m.ps(f"B{n}") for n in range(8)]

        con_in = sems("con_in")
        rk_in, v_in = ([sems(f"{x}{s}") for s in range(2)] for x in ("rk_in", "v_in"))
        names = ("lora_ready lora_now lora_sum pre_done less_done sig_done cum_done exp_done pool_k ssd clamped rooted rnd kk_done akk_done "
                 "kd_done kd_part op_done turned_up tev_a tev_b tev_r tev_k arb_done a_sum a_masked abi_done adir d0 dt0 dtb0 xb_done z_sum x_done d_sum "
                 "d_copied d5_copied g_sum g_copied u_sum u_copied s_sum s_added s_done y_sum y_copied bon_m bon_done zeroed0 zeroed1 zeroed2 passed_sp")
        q = {x: sems(x) for x in names.split()}
        y_out = [sems(f"y_out{s}") for s in range(2)]
        block = ctx.enter_context(nc.Block())
        K = (slice(0, 64), slice(64, 128))

        def wait(eng, name, c, per_step, k):
            v = c * per_step + k
            if not (isinstance(v, int) and v <= 0):
                eng.wait_ge(q[name], v)

        def hd(h):
            return slice(h * C, (h + 1) * C)

        def half(ap, g):
            return ap[:, g * H2 * C:(g + 1) * H2 * C]

        @block.sync
        def _(sp):
            for dst, src in ((w_up[:], io["w_up"]), (a_up[:], io["a_up"]), (wa0[:, 0], io["w0"]), (wa0[:, 1], io["a0"]),
                             (rows[:].rearrange("p a c -> p (a c)"), io["rw_rows"].partition_broadcast(P)),
                             (tri[:], io["tri"]), (tot[:], io["tot"]), (causal[:], io["causal"]), (level[:], io["level"]), (levelbd[:], io["levelbd"]),
                             (eye[:], io["eye2"])):
                sp.dma_start(dst, src).then_inc(con_in, 16)

            R0 = 6 * CH

            def load_rk(c, s, t_back, context):
                wait(sp, "op_done", c - 2, 6, 6)
                wait(sp, "pool_k", c - 2, 5, 5)
                sp.sem_inc(q["passed_sp"], 1)
                for d, t in ((0, c * C), (1, t_back)):
                    src = io["u"][bass.ds(t, C)]
                    sp.dma_start(rkv[s][K[d], 1, :], src[:, R0 + RC:R0 + 2 * RC]).then_inc(rk_in[s], 16)
                    r = src[:, R0 + RC:R0 + 2 * RC] if context else src[:, R0:R0 + RC]
                    sp.dma_start(rkv[s][K[d], 0, :], r).then_inc(rk_in[s], 16)

            def load_v(c, s, t_back):
                wait(sp, "y_sum", c - 2, 2, 2)
                sp.sem_inc(q["passed_sp"], 1)
                for d, t in ((0, c * C), (1, t_back)):
                    sp.dma_start(rkv[s][K[d], 2, :], io["u"][bass.ds(t, C), R0 + 2 * RC:R0 + 3 * RC]).then_inc(v_in[s], 16)

            def store(c, s, t_back):
                sp.wait_ge(q["y_copied"], 2 * c + 2)
                sp.sem_inc(q["passed_sp"], 1)
                sp.wait_ge(q["bon_done"], c + 1)
                sp.sem_inc(q["passed_sp"], 1)
                sp.dma_start(io["ys0"][bass.ds(c * C - LC, C)], yb[s][K[0], :]).then_inc(y_out[s], 16)
                sp.dma_start(io["ys1"][bass.ds(t_back - LC, C)], yb[s][K[1], :]).then_inc(y_out[s], 16)

            NC = LC // C
            back = lambda c: LC - C * (c + 1) if c < NC else T + LC - C * (c + 1)
            for c in range(2):
                load_rk(c, c, back(c), True)
                load_v(c, c, back(c))

            def turn(c, s):
                t = T + LC - C - C * c
                load_rk(c + 2, s, t - 2 * C, False)
                load_v(c + 1, 1 - s, t - C)
                store(c - 1, 1 - s, t + C)

            for c in range(NC + 2):
                load_rk(c + 2, c % 2, back(c + 2), c + 2 < NC)
                if c > 0:
                    load_v(c + 1, 1 - c % 2, back(c + 1))
                if c > NC:
                    store(c - 1, 1 - c % 2, back(c - 1))
            with sp.Fori(NC // 2 + 1, NSTEP // 2 - 1) as j:
                for s in range(2):
                    turn(2 * j + s, s)
            load_v(NSTEP - 1, 1, back(NSTEP - 1))
            for c in range(NSTEP - 3, NSTEP):
                store(c, c % 2, back(c))
            for s in range(2):
                sp.wait_ge(y_out[s], 16 * (NSTEP - NC))

        def steps(eng, prepare_alone, both, recur_alone):
            prepare_alone(0, 0)
            for c in range(2):
                both(c, c % 2)
            with eng.Fori(1, NSTEP // 2 - 1) as j:
                for s in range(2):
                    both(2 * j + s, s)
            both(NSTEP - 2, 0)
            recur_alone(NSTEP - 1, 1)

        @block.tensor
        def _(pe):
            pe.wait_ge(con_in, 176)
            ident = per["ident"]

            def p_lora(c, s):
                wait(pe, "lora_now", c, 1, 1)
                wait(pe, "a_masked", c - 1, 4, 4)
                for i, up in ((0, w_up), (1, a_up)):
                    mm = pe.matmul(B[i][:], lnow[:, i].rearrange("p d t -> p (d t)"), up[:], start=True, stop=True)
                mm.then_inc(q["lora_sum"], 1)

            def p_cum(c, s):
                wait(pe, "sig_done", c, 1, 1)
                pe.matmul(B[2][:], tri[:], sig[:, 0, :], start=True, stop=True)
                for h in range(NH):
                    mm = pe.matmul(B[0][0:64, 2 * h:2 * h + 2], sig[:, 0, hd(h)], tot[:], start=True, stop=True)
                mm.then_inc(q["cum_done"], 1)

            def p_turn(c, s):
                wait(pe, "exp_done", c, 5, 5)
                wait(pe, "op_done", c, 6, 1)
                for p in range(4):
                    mm = pe.transpose(B[1][:, p * P:(p + 1) * P], alpha[:, p * P:(p + 1) * P], ident[:])
                mm.then_inc(q["turned_up"], 1)
                wait(pe, "op_done", c, 6, 3)
                for h in range(NH):
                    bank = (3, 0)[h // H2]
                    mm = pe.transpose(B[bank][:, (h % H2) * P:(h % H2 + 1) * P], beta[s][:, h].rearrange("p d k -> p (d k)"), ident[:])
                    if h % H2 == H2 - 1:
                        mm.then_inc(q["turned_up"], 1)
                wait(pe, "op_done", c, 6, 6)
                for p in range(4):
                    mm = pe.transpose(B[2][:, p * P:(p + 1) * P], rho[:, p * P:(p + 1) * P], ident[:])
                mm.then_inc(q["turned_up"], 1)
                for h in range(NH):
                    if h == 0:
                        wait(pe, "tev_a", c, 4, 4)
                    if h == H2:
                        wait(pe, "tev_b", c, 2, 1)
                    bank = (1, 3)[h // H2]
                    mm = pe.transpose(B[bank][:, (h % H2) * P:(h % H2 + 1) * P], kap[s][:, h].rearrange("p d k -> p (d k)"), ident[:])
                    if h % H2 == H2 - 1:
                        mm.then_inc(q["turned_up"], 1)

            def r_products(c, lhs, banks):
                wait(pe, "tev_a", c, 4, 4)
                wait(pe, "tev_b", c, 2, 2)
                wait(pe, "tev_r", c, 4, 4)
                wait(pe, "tev_k", c, 2, 2)
                for g, bank in enumerate(banks):
                    for hh in range(H2):
                        h = g * H2 + hh
                        mm = pe.matmul(B[bank][:, hh * P:(hh + 1) * P], lhs[:, h, :], arT[:, h].rearrange("k a t -> k (a t)"),
                                       start=True, stop=True)
                    mm.then_inc(q["a_sum"], 1)

            def r_direct(c, s):
                for g in range(2):
                    wait(pe, "a_masked", c, 4, g + 1)
                    wait(pe, "abi_done", c, 2, g + 1)
                    wait(pe, "s_added", c - 1, 2, g + 1)
                    for hh in range(H2):
                        mm = pe.matmul(B[6 + g][:, hd(hh)], abi[:, g * H2 + hh], eye[:], start=True, stop=True)
                    mm.then_inc(q["adir"], 1)

            def bdm(ap):
                return ap.rearrange("p d t -> p (d t)")

            def r_level(c, s, l):
                for g in range(2):
                    if l == 1:
                        wait(pe, "d0", c, 2, g + 1)
                        wait(pe, "y_copied", c - 1, 2, g + 1)
                    else:
                        wait(pe, "d_copied", c, 24, 3 * (2 * (l - 2) + g) + 1)
                    for hh in range(H2):
                        mm = pe.matmul(B[4 + g][:, hd(hh)], abi[:, g * H2 + hh], dd[:, g, 0, hd(hh)], start=True, stop=True)
                    mm.then_inc(q["z_sum"], 1)
                for g in range(2):
                    if l == 1:
                        wait(pe, "dtb0", c, 2, g + 1)
                        wait(pe, "dt0", c, 4, 2 * g + 2)
                    else:
                        wait(pe, "d_copied", c, 24, 3 * (2 * (l - 2) + g) + 3)
                    if l < 5:
                        wait(pe, "x_done", c, 10, 2 * (l - 1) + g + 1)
                        for hh in range(H2):
                            pe.matmul(B[6 + g][:, hd(hh)], bdm(dtb[:, g * H2 + hh]), xm[:, g, hd(hh)], start=True, stop=True)
                    wait(pe, "xb_done", c, 10, 2 * (l - 1) + g + 1)
                    for hh in range(H2):
                        mm = pe.matmul(B[6 + g][:, hd(H2 + hh)], bdm(xb[:, g * H2 + hh]), dd[:, g, 1, hd(hh)], start=True, stop=True)
                    mm.then_inc(q["d_sum"], 1)

            def r_g(c, s):
                V = rkv[s][:, 2, :]
                wait(pe, "s_done", c - 1, 2, 2)
                wait(pe, "arb_done", c, 2, 2)
                wait(pe, "a_masked", c, 4, 4)
                pe.wait_ge(v_in[s], 16 * (c - s) + 32)
                if isinstance(c, int) and c == 0:
                    pe.wait_ge(q["zeroed0"], 1)
                for g in range(2):
                    wait(pe, "xb_done", c, 10, 9 + g)
                    for hh in range(H2):
                        h = g * H2 + hh
                        pe.matmul(B[4 + g][:, hd(hh)], bdm(arb[:, h, 0]), st[:, hd(h)], start=True, stop=False)
                        mm = pe.matmul(B[4 + g][:, hd(hh)], ak[s][:, h, 0], V[:, hd(h)], start=False, stop=True)
                    mm.then_inc(q["g_sum"], 1)

            def r_u(c, s):
                for g in range(2):
                    wait(pe, "g_copied", c, 2, g + 1)
                    wait(pe, "d5_copied", c, 4, 2 * g + 2)
                    for hh in range(H2):
                        h = g * H2 + hh
                        mm = pe.matmul(B[6 + g][:, hd(hh)], bdm(dtb[:, h]), gs[:, hd(h)], start=True, stop=True)
                    mm.then_inc(q["u_sum"], 1)

            def r_s(c, s):
                V = rkv[s][:, 2, :]
                for g in range(2):
                    wait(pe, "u_copied", c, 2, g + 1)
                    for hh in range(H2):
                        h = g * H2 + hh
                        pe.matmul(B[6 + g][:, hd(hh)], bdm(beta[s][:, h]), us[:, hd(h)], start=True, stop=False)
                        mm = pe.matmul(B[6 + g][:, hd(hh)], bdm(kap[s][:, h]), V[:, hd(h)], start=False, stop=True)
                    mm.then_inc(q["s_sum"], 1)

            def r_y(c, s):
                V = rkv[s][:, 2, :]
                for g in range(2):
                    wait(pe, "u_copied", c, 2, g + 1)
                    for hh in range(H2):
                        h = g * H2 + hh
                        out = B[4 + g][:, hd(hh)]
                        pe.matmul(out, bdm(arb[:, h, 1]), st[:, hd(h)], start=True, stop=False)
                        pe.matmul(out, ab[s][:, h, 1], us[:, hd(h)], start=False, stop=False)
                        mm = pe.matmul(out, ak[s][:, h, 1], V[:, hd(h)], start=False, stop=True)
                    mm.then_inc(q["y_sum"], 1)

            def prepare(c, s):
                p_lora(c, s)
                p_cum(c, s)
                p_turn(c, s)
                r_products(c, bT, (2, 3))
                r_products(c, kT, (0, 1))

            def both(c, s):
                r_direct(c, s)
                p_lora(c + 1, 1 - s)
                r_level(c, s, 1)
                r_level(c, s, 2)
                r_level(c, s, 3)
                p_cum(c + 1, 1 - s)
                r_level(c, s, 4)
                r_level(c, s, 5)
                r_g(c, s)
                p_turn(c + 1, 1 - s)
                r_u(c, s)
                r_s(c, s)
                r_products(c + 1, bT, (2, 3))
                r_products(c + 1, kT, (0, 1))
                r_y(c, s)

            def recur(c, s):
                r_direct(c, s)
                for l in range(1, 6):
                    r_level(c, s, l)
                r_g(c, s)
                r_u(c, s)
                r_y(c, s)

            steps(pe, prepare, both, recur)

        @block.scalar
        def _(act):
            act.activation(lora[K[0], :, 0, :], per["wd"][K[0], :].rearrange("r (c t) -> r c t", t=C), ACT.Tanh)
            ins = act.copy(lora[K[0], :, 1, :], per["ad"][K[0], :].rearrange("r (c t) -> r c t", t=C))
            for c in range(NSTEP):
                t = LC - C * (c + 1) if c < LC // C else T + LC - C * (c + 1)
                act.activation(lora[K[1], c, 0, :], per["wd"][K[1], t:t + C], ACT.Tanh)
                ins = act.copy(lora[K[1], c, 1, :], per["ad"][K[1], t:t + C])
            ins.then_inc(q["lora_ready"], 1)
            act.wait_ge(q["lora_ready"], 1)

            def a_lora(c, s):
                wait(act, "lora_sum", c - 1, 1, 1)
                for d in range(2):
                    ins = act.copy(lnow[K[d], :, d, :], lora[K[d], bass.ds(c, 1)].rearrange("p o a t -> p (o a) t"))
                ins.then_inc(q["lora_now"], 1)

            def a_sig(c, s):
                wait(act, "pre_done", c, 2, 2)
                act.activation(sig[:], sig[:], ACT.Sigmoid).then_inc(q["sig_done"], 1)

            def a_root(c, s):
                wait(act, "clamped", c, 1, 1)
                wait(act, "kk_done", c - 1, 1, 1)
                act.activation(rn[:], ss[:], ACT.Sqrt).then_inc(q["rooted"], 1)

            def a_exp(c, s):
                wait(act, "cum_done", c, 1, 1)
                wait(act, "op_done", c - 1, 6, 6)
                wait(act, "less_done", c, 1, 1)
                act.activation(e_in[:], B[2][:], ACT.Exp).then_inc(q["exp_done"], 1)
                act.activation(e_ng[:], B[2][:], ACT.Exp, scale=-1.0).then_inc(q["exp_done"], 1)
                act.activation(e_ex[:], e_ex[:], ACT.Exp).then_inc(q["exp_done"], 1)
                wait(act, "s_done", c - 2, 2, 2)
                for d in range(2):
                    act.activation(dec[s][K[d], :], B[0][0:64, 0:2 * NH].rearrange("k (h d) -> k h d", d=2)[:, :, d], ACT.Exp
                                   ).then_inc(q["exp_done"], 1)

            def turn_copies(eng, copy, c, s, bank, dst, sem):
                v = B[bank][:].rearrange("p (a d t) -> p a d t", a=4, d=2)
                for par in range(2):
                    for d in range(2):
                        copy(dst(d, par), v[K[par], :, d, :]).then_inc(q[sem], 1)

            def a_turn(c, s):
                wait(act, "arb_done", c - 1, 2, 2)
                wait(act, "turned_up", c, 6, 1)
                turn_copies(act, act.copy, c, s, 1, lambda d, par: arT[K[d], par::2, 0, :], "tev_a")
                wait(act, "turned_up", c, 6, 4)
                turn_copies(act, act.copy, c, s, 2, lambda d, par: arT[K[d], par::2, 1, :], "tev_r")

            def a_arb(c, s):
                wait(act, "y_sum", c - 1, 2, 2)
                wait(act, "tev_r", c, 4, 4)
                for d in range(2):
                    act.copy(arb[K[d], :, :, d, :].rearrange("p h a t -> p (h a) t"), arT[K[d]].rearrange("p h a t -> p (h a) t")
                             ).then_inc(q["arb_done"], 1)

            def a_level(c, s, l):
                for g in range(2):
                    wait(act, "d_sum", c, 10, 2 * (l - 1) + g + 1)
                    if l < 5:
                        act.copy(dd[:, g].rearrange("p a x -> p (a x)"), B[6 + g][:]).then_inc(q["d_copied"], 1)
                    for d in range(2):
                        act.copy(dtb[K[d], g * H2:(g + 1) * H2, d, :], B[6 + g][K[d], H2 * C:].rearrange("p (h t) -> p h t", h=H2)
                                 ).then_inc(q["d_copied" if l < 5 else "d5_copied"], 1)

            def a_g(c, s):
                for g in range(2):
                    wait(act, "g_sum", c, 2, g + 1)
                    act.copy(half(gs, g), B[4 + g][:, 0:H2 * C]).then_inc(q["g_copied"], 1)

            def a_state(c, s):
                for g in range(2):
                    wait(act, "u_sum", c, 2, g + 1)
                    act.copy(half(us, g), B[6 + g][:, 0:H2 * C]).then_inc(q["u_copied"], 1)
                y_free(c, s)
                for g in range(2):
                    wait(act, "y_sum", c, 2, g + 1)
                    act.copy(yb[s][:, g * H2 * C:(g + 1) * H2 * C], B[4 + g][:, 0:H2 * C]).then_inc(q["y_copied"], 1)

            def y_free(c, s):
                v = 16 * (c - s - LC // C)
                if not (isinstance(v, int) and v <= 0):
                    act.wait_ge(y_out[s], v)

            def prepare(c, s):
                a_lora(c, s)
                a_sig(c, s)
                a_root(c, s)
                a_exp(c, s)
                a_turn(c, s)

            def both(c, s):
                a_lora(c + 1, 1 - s)
                a_arb(c, s)
                a_level(c, s, 1)
                a_sig(c + 1, 1 - s)
                a_root(c + 1, 1 - s)
                a_level(c, s, 2)
                a_level(c, s, 3)
                a_exp(c + 1, 1 - s)
                a_level(c, s, 4)
                a_level(c, s, 5)
                a_g(c, s)
                a_turn(c + 1, 1 - s)
                a_state(c, s)

            def recur(c, s):
                a_arb(c, s)
                for l in range(1, 6):
                    a_level(c, s, l)
                a_g(c, s)
                a_state(c, s)

            act.wait_ge(q["zeroed1"], 2)
            act.wait_ge(q["zeroed2"], 5)
            prepare(0, 0)
            for c in range(6):
                both(c, c % 2)
            with act.Fori(3, NSTEP // 2 - 1) as j:
                for s in range(2):
                    both(2 * j + s, s)
            both(NSTEP - 2, 0)
            recur(NSTEP - 1, 1)

        @block.gpsimd
        def _(pool):
            pool.memset(lnow[:], 0.0).then_inc(q["zeroed1"], 1)
            pool.memset(dtb[:], 0.0).then_inc(q["zeroed1"], 1)
            pool.memset(arb[:], 0.0).then_inc(q["zeroed2"], 1)
            for s in range(2):
                pool.memset(beta[s][:], 0.0).then_inc(q["zeroed2"], 1)
                pool.memset(kap[s][:], 0.0).then_inc(q["zeroed2"], 1)
            pool.wait_ge(q["zeroed2"], 5)
            pool.wait_ge(con_in, 176)

            def keys(c, s):
                k = rkv[s][:, 1, :]
                pool.wait_ge(rk_in[s], 32 * (c - s) + 64)
                wait(pool, "kk_done", c - 1, 1, 1)
                pool.tensor_tensor(kkr[:], k, rows[:, 0, :], ALU.mult).then_inc(q["pool_k"], 1)
                wait(pool, "pool_k", c, 5, 1)
                wait(pool, "ssd", c - 1, 1, 1)
                pool.tensor_tensor(sq[:], kkr[:], kkr[:], ALU.mult).then_inc(q["pool_k"], 1)
                wait(pool, "kd_done", c - 1, 1, 1)
                pool.tensor_tensor(kka[:], k, rows[:, 1, :], ALU.mult).then_inc(q["pool_k"], 1)
                wait(pool, "pool_k", c, 5, 3)
                pool.tensor_tensor(krest[:], k, kka[:], ALU.subtract).then_inc(q["pool_k"], 1)
                wait(pool, "bon_done", c - 1, 1, 1)
                pool.tensor_tensor(rrk[:], rkv[s][:, 0, :], rows[:, 2, :], ALU.mult).then_inc(q["pool_k"], 1)

            def rate(c, s):
                wait(pool, "sig_done", c, 1, 1)
                wait(pool, "kk_done", c, 1, 1)
                wait(pool, "op_done", c - 1, 6, 3)
                pool.tensor_tensor(akk[:], sig[:, 1], kk[:], ALU.mult).then_inc(q["akk_done"], 1)
                wait(pool, "pool_k", c, 5, 5)
                wait(pool, "kd_done", c, 1, 1)
                pool.tensor_tensor(rrk[:], rrk[:], kd[:], ALU.mult).then_inc(q["bon_m"], 1)

            def first(c, s):
                for g in range(2):
                    hs = slice(g * H2, (g + 1) * H2)
                    wait(pool, "a_masked", c, 4, g + 1)
                    if g == 0:
                        wait(pool, "z_sum", c - 1, 10, 10)
                        wait(pool, "dt0", c - 1, 4, 4)
                        wait(pool, "dtb0", c - 1, 2, 2)
                    pool.tensor_tensor(abi[:, hs], ab[s][:, hs, 0], bc(eyebd[:], 1, H2), ALU.add).then_inc(q["abi_done"], 1)
                for g in range(2):
                    hs = slice(g * H2, (g + 1) * H2)
                    wait(pool, "abi_done", c, 2, g + 1)
                    if g == 0:
                        wait(pool, "u_sum", c - 1, 2, 2)
                    pool.tensor_tensor(bdm(dtb[:, hs].rearrange("p h d t -> p (h d) t")).rearrange("p (h x) -> p h x", h=H2), abi[:, hs],
                                       bc(levelbd[:, 0].rearrange("p d t -> p (d t)"), 1, H2), ALU.mult).then_inc(q["dtb0"], 1)

            def prepare(c, s):
                keys(c, s)
                rate(c, s)
                first(c, s)

            def bdm(ap):
                return ap.rearrange("p x t -> p (x t)")

            def both(c, s):
                prepare(c + 1, 1 - s)

            steps(pool, prepare, both, lambda c, s: None)

        @block.vector
        def _(dve):
            dve.memset(st[:], 0.0).then_inc(q["zeroed0"], 1)
            dve.wait_ge(con_in, 176)
            dve.wait_ge(q["zeroed0"], 1)
            dve.wait_ge(q["zeroed2"], 5)

            def d_pre(c, s):
                wait(dve, "lora_sum", c, 1, 1)
                wait(dve, "cum_done", c - 1, 1, 1)
                wait(dve, "less_done", c - 1, 1, 1)
                wait(dve, "akk_done", c - 1, 1, 1)
                wait(dve, "kd_done", c - 1, 1, 1)
                for i in range(2):
                    dve.tensor_tensor(sig[:, i], B[i][:], wa0[:, i], ALU.add).then_inc(q["pre_done"], 1)

            def d_keys(c, s):
                wait(dve, "pool_k", c, 5, 2)
                wait(dve, "rooted", c - 1, 1, 1)
                dve.tensor_reduce(ss[:], sq[:].rearrange("p (h k) -> p h k", h=NH), AX_X, ALU.add).then_inc(q["ssd"], 1)
                wait(dve, "ssd", c, 1, 1)
                dve.tensor_scalar(ss[:], ss[:], 1e-24, None, ALU.max).then_inc(q["clamped"], 1)

            def d_unit(c, s):
                wait(dve, "rooted", c, 1, 1)
                dve.reciprocal(rn[:], rn[:]).then_inc(q["rnd"], 1)
                wait(dve, "rnd", c, 1, 1)
                wait(dve, "akk_done", c - 1, 1, 1)
                dve.tensor_tensor(kk[:].rearrange("p (h k) -> p h k", h=NH), kkr[:].rearrange("p (h k) -> p h k", h=NH),
                                  bc(rn[:], 2, HD), ALU.mult).then_inc(q["kk_done"], 1)

            def d_rate(c, s):
                wait(dve, "sig_done", c, 1, 1)
                wait(dve, "pool_k", c, 5, 4)
                wait(dve, "bon_m", c - 1, 1, 1)
                dve.tensor_tensor(kd[:], sig[:, 1], kka[:], ALU.mult).then_inc(q["kd_part"], 1)
                wait(dve, "kd_part", c, 1, 1)
                dve.tensor_tensor(kd[:], kd[:], krest[:], ALU.add).then_inc(q["kd_done"], 1)

            def d_less(c, s):
                wait(dve, "cum_done", c, 1, 1)
                wait(dve, "exp_done", c - 1, 5, 5)
                dve.scalar_tensor_tensor(e_ex[:], sig[:, 0], -LD, B[2][:], ALU.mult, ALU.add).then_inc(q["less_done"], 1)

            def d_ops(c, s):
                v3 = lambda ap: ap.rearrange("p (h k) -> p h k", h=NH)
                wait(dve, "exp_done", c, 5, 3)
                wait(dve, "turned_up", c - 1, 6, 6)
                wait(dve, "s_sum", c - 2, 2, 2)
                dve.tensor_tensor(alpha[:], kk[:], e_ex[:], ALU.mult).then_inc(q["op_done"], 1)
                wait(dve, "akk_done", c, 1, 1)
                for d in range(2):
                    dve.scalar_tensor_tensor(beta[s][K[d], :, d, :], v3(akk[K[d], :]), -1.0, v3(e_ng[K[d], :]), ALU.mult, ALU.mult
                                             ).then_inc(q["op_done"], 1)
                wait(dve, "kd_done", c, 1, 1)
                for d in range(2):
                    dve.tensor_tensor(kap[s][K[d], :, d, :], v3(kd[K[d], :]), v3(e_ng[K[d], :]), ALU.mult).then_inc(q["op_done"], 1)
                dve.tensor_tensor(rho[:], rkv[s][:, 0, :], e_in[:], ALU.mult).then_inc(q["op_done"], 1)

            def d_turn(c, s):
                wait(dve, "a_sum", c - 1, 4, 4)
                for n, bank, dst, g, name in ((2, 3, bT, 0, "tev_b"), (3, 0, bT, 1, "tev_b"), (5, 1, kT, 0, "tev_k"), (6, 3, kT, 1, "tev_k")):
                    wait(dve, "turned_up", c, 6, n)
                    dve.tensor_copy(dst[:, g * H2:(g + 1) * H2].rearrange("p h x -> p (h x)"), B[bank][:]).then_inc(q[name], 1)

            def d_bonus(c, s):
                wait(dve, "bon_m", c, 1, 1)
                v = 16 * (c - s - LC // C)
                if not (isinstance(v, int) and v <= 0):
                    dve.wait_ge(y_out[s], v)
                dve.tensor_reduce(yb[s][:, RC:], rrk[:].rearrange("p (h k) -> p h k", h=NH), AX_X, ALU.add).then_inc(q["bon_done"], 1)

            def d_masks(c, s):
                wait(dve, "y_sum", c - 2, 2, 2)
                wait(dve, "abi_done", c - 2, 2, 2)
                for n, dst, g, bank in ((0, ab[s], 0, 2), (1, ab[s], 1, 3), (2, ak[s], 0, 0), (3, ak[s], 1, 1)):
                    wait(dve, "a_sum", c, 4, n + 1)
                    dve.tensor_tensor(dst[:, g * H2:(g + 1) * H2].rearrange("p h a (d t) -> p (h a) d t", d=2),
                                      bc(B[bank][:].rearrange("p (x t) -> p x t", t=C), 2, 2),
                                      causal[:].rearrange("p h a d t -> p (h a) d t"), ALU.mult).then_inc(q["a_masked"], 1)

            def d_first(c, s):
                h4 = lambda ap: ap.rearrange("p (h t) -> p h t", h=H2)
                wait(dve, "d_sum", c - 1, 10, 10)
                for g in range(2):
                    wait(dve, "abi_done", c, 2, g + 1)
                    for d in range(2):
                        dve.tensor_tensor(h4(dd[K[d], g, 1]), abi[K[d], g * H2:(g + 1) * H2, d * C:(d + 1) * C],
                                          bc(levelbd[K[d], 0, d], 1, H2), ALU.mult).then_inc(q["dt0"], 1)
                for g in range(2):
                    wait(dve, "adir", c, 2, g + 1)
                    dve.tensor_tensor(h4(dd[:, g, 0]), h4(B[6 + g][:, 0:H2 * C]), bc(level[:, 0], 1, H2), ALU.mult).then_inc(q["d0"], 1)

            def d_level(c, s, l):
                h4 = lambda ap: ap.rearrange("p (h t) -> p h t", h=H2)
                for g in range(2):
                    wait(dve, "z_sum", c, 10, 2 * (l - 1) + g + 1)
                    if l > 1:
                        wait(dve, "d_sum", c, 10, 2 * (l - 2) + g + 1)
                    z = h4(B[4 + g][:, 0:H2 * C])
                    if l < 5:
                        dve.tensor_tensor(h4(xm[:, g]), z, bc(level[:, l], 1, H2), ALU.mult).then_inc(q["x_done"], 1)
                    else:
                        dve.sem_inc(q["x_done"], 1)
                    dve.tensor_tensor(xb[:, g * H2:(g + 1) * H2], bc(z, 2, 2), bc(levelbd[:, l], 1, H2), ALU.mult).then_inc(q["xb_done"], 1)

            def d_added(c, s):
                for g in range(2):
                    wait(dve, "s_sum", c, 2, g + 1)
                    if g == 0:
                        wait(dve, "s_done", c - 1, 2, 2)
                    dve.tensor_tensor(half(sm, g), half(st, g), B[6 + g][:, 0:H2 * C], ALU.add).then_inc(q["s_added"], 1)

            def d_decay(c, s):
                h4 = lambda ap: ap.rearrange("p (h t) -> p h t", h=H2)
                if isinstance(c, int) and c < 0:
                    return
                wait(dve, "exp_done", c, 5, 5)
                wait(dve, "y_sum", c, 2, 2)
                for g in range(2):
                    wait(dve, "s_added", c, 2, g + 1)
                    dve.tensor_tensor(h4(half(st, g)), h4(half(sm, g)), bc(dec[s][:, g * H2:(g + 1) * H2], 2, HD), ALU.mult
                                      ).then_inc(q["s_done"], 1)

            def prepare(c, s):
                d_pre(c, s)
                d_keys(c, s)
                d_unit(c, s)
                d_rate(c, s)
                d_less(c, s)
                d_ops(c, s)
                d_turn(c, s)
                d_masks(c, s)
                d_bonus(c, s)

            def both(c, s):
                d_first(c, s)
                d_decay(c - 1, 1 - s)
                d_keys(c + 1, 1 - s)
                d_level(c, s, 1)
                d_pre(c + 1, 1 - s)
                d_level(c, s, 2)
                d_unit(c + 1, 1 - s)
                d_level(c, s, 3)
                d_rate(c + 1, 1 - s)
                d_less(c + 1, 1 - s)
                d_level(c, s, 4)
                d_level(c, s, 5)
                d_ops(c + 1, 1 - s)
                d_turn(c + 1, 1 - s)
                d_added(c, s)
                d_masks(c + 1, 1 - s)
                d_bonus(c + 1, 1 - s)

            def recur(c, s):
                d_first(c, s)
                d_decay(c - 1, 1 - s)
                for l in range(1, 6):
                    d_level(c, s, l)

            prepare(0, 0)
            for c in range(6):
                both(c, c % 2)
            with dve.Fori(3, NSTEP // 2 - 1) as j:
                for s in range(2):
                    both(2 * j + s, s)
            both(NSTEP - 2, 0)
            recur(NSTEP - 1, 1)


class Chain:

    def __init__(self, eng, sem, per):
        self.eng, self.sem, self.per = eng, sem, per

    def start(self, i):
        self.i, self.k = i, 0

    def do(self, ins):
        ins.then_inc(self.sem, 1)
        self.k += 1
        return self.k

    def wait(self, k=None):
        self.eng.wait_ge(self.sem, self.i * self.per + (self.k if k is None else k))

    def end(self):
        assert self.k == self.per, (self.k, self.per)


def merge(nc, sems, io, per):
    with ExitStack() as ctx:
        m = Mem(nc, ctx, "mg")
        wout = m.sb("wout", [P, KD, D])
        rows = m.sb("mrows", [P, 3 * CH + 2 * CH + 2 * RC])
        lnr = m.sb("lnr", [P, 2, D])
        gup = m.sb("gup", [P, RC])
        wrt = m.sb("wrt", [P, KD, NE])
        ebias = m.sb("ebias", [P, NE])
        wsgu = m.sb("wsgu", [P, KD, 2 * FF])
        wsd = m.sb("wsd", [P, 2, D])
        tri = m.sb("rtri", [P, P])
        ones = m.sb("ones", [P, P])
        iota = m.sb("iota", [P, NE])
        iotap = m.sb("iotap", [P, 1])
        thresh = m.sb("thresh", [P, 8])
        b = m.sb("b", [P, CH])
        cx = m.sb("cx", [P, 3, 2, CH])
        ycat = m.sb("ycat", [P, D])
        yh = m.sb("yh", [P, CH])
        ya = m.sb("ya", [P, CH])
        y01 = m.sb("y01", [P, 2, RC + NH])
        ysum = m.sb("ysum", [P, RC + NH])
        v = m.sb("v", [P, RC])
        z3 = m.sb("z3", [P, 3, CH])
        za = m.sb("za", [P, CH])
        yn = m.sb("yn", [P, RC])
        sqr = m.sb("sqr", [P, RC])
        bonus = m.sb("bonus", [P, RC])
        junk = m.sb("junk", [P, D])
        mean8 = m.sb("mean8", [P, NH])
        var = m.sb("var", [P, 2 + NH])
        rstd = m.sb("rstd", [P, 2 + NH])
        sgd = m.sb("sgd", [P, P])
        ycT = m.sb("ycT", [P, KD, P])
        x = m.sb("x", [P, D])
        t = m.sb("t", [P, D])
        x1 = m.sb("x1", [P, D])
        h2 = m.sb("h2", [P, D])
        base = m.sb("base", [P, D])
        h2T = m.sb("h2T", [P, KD, P])
        stat = m.sb("stat", [P, 4])
        sgm = m.sb("sgm", [P, FF])
        hid = m.sb("hid", [P, FF])
        hidT = m.sb("hidT", [P, 2, P])
        sc = m.sb("sc", [P, NE])
        biased = m.sb("biased", [P, NE])
        top = m.sb("top", [P, 8])
        topi = m.sb("topi", [P, 8], U32)
        topf = m.sb("topf", [P, 8])
        sel3 = m.sb("sel3", [P, TOPK, NE])
        mem = m.sb("mem", [P, NE])
        gsum = m.sb("gsum", [P, 2])
        rank = m.sb("rank", [P, NE])
        carry = m.sb("carry", [P, NE])
        OH = m.sb("OH", [P, NT, TOPK, NE])
        rnk = m.sb("rnk", [P, NT, TOPK])
        gates, slots, slots_i = per["gates"], m.sb("slots", [P, NT, TOPK]), per["slots_i"]
        names = ("G", "T0", "T1", "O0", "O1", "R", "S", "H")
        G, T0, T1, O0, O1, R, S, H = (m.ps(x) for x in names)
        w_in, big_in, a_in, x_in = sems("w_in"), sems("big_in"), sems("a_in"), sems("x_in")
        q = {n: sems(n) for n in (
            "gate_sum gd_sig za2 sq_done vars rooted1 mixed turnedY ycT_done out_sum out_read mean_sum var_sum mu ln_var "
            "rooted2 h2_done turnedH h2T_done logits gu sig_gu hid_done turnedS hidT_done down_sum base_done scored routed "
            "member rank_sum rank_read shifted bon_done x_free tail "
            "dmix dout pmix h2_st base_st zt tok_in passed passed_pool").split()}
        tiling = ExitStack()
        block = tiling.enter_context(nc.Block())
        MIX, OUT, PMIX = 18, 20, 4

        def wait(eng, name, i, per_tile, k):
            val = i * per_tile + k
            if not (isinstance(val, int) and val <= 0):
                eng.wait_ge(q[name], val)

        def tiles(eng, mix, both, out):
            mix(0)
            mix(1)
            both(0)
            with eng.Fori(1, NT - 2) as i:
                both(i)
            out(NT - 2)
            out(NT - 1)

        @block.sync
        def _(sp):
            for dst, src in ((rows[:], io["mix_rows"].partition_broadcast(P)), (gup[:], io["g_up"]),
                             (lnr[:].rearrange("p a d -> p (a d)"), io["ln_rows"][0:2 * D].partition_broadcast(P)),
                             (wrt[:], io["w_router"]), (ebias[:], io["e_bias"].partition_broadcast(P)), (tri[:], io["rank_tri"]),
                             (iota[:], io["iota_e"]), (iotap[:], io["iota_p"]), (thresh[:], io["thresh"])):
                sp.dma_start(dst, src).then_inc(w_in, 16)

            def big_weights():
                for dst, src in ((wout[:], io["w_out"]), (wsgu[:], io["w_s_gu"]), (wsd[:], io["w_s_down"])):
                    sp.dma_start(dst, src).then_inc(big_in, 16)

            def load_mix(i):
                wait(sp, "mixed", i - 1, 1, 1)
                wait(sp, "bon_done", i - 1, 1, 1)
                wait(sp, "sq_done", i - 1, 2, 2)
                r0 = LC + i * P
                sp.dma_start(b[:], io["u"][bass.ds(r0, P), 0:CH]).then_inc(a_in, 16)
                for n in range(3):
                    sp.dma_start(cx[:, n], io["u"][bass.ds(r0 + (n - 1) * GRID, P), CH:3 * CH]
                                 .rearrange("t (a c) -> t a c", a=2)).then_inc(a_in, 16)
                sp.dma_start(yh[:], io["yh"][bass.ds(i * P, P)]).then_inc(a_in, 16)
                sp.dma_start(y01[:, 0], io["ys0"][bass.ds(i * P, P)]).then_inc(a_in, 16)
                sp.dma_start(y01[:, 1], io["ys1"][bass.ds(i * P, P)]).then_inc(a_in, 16)
                sp.dma_start(v[:], io["u"][bass.ds(r0, P), UW - RC:UW]).then_inc(a_in, 16)

            def load_out(i):
                wait(sp, "x_free", i - 1, 1, 1)
                sp.dma_start(x[:], io["x"][bass.ds(i * P, P)]).then_inc(x_in, 16)

            def both(i):
                load_out(i)
                load_mix(i + 2)

            def begin(i):
                load_mix(i)
                if i == 0:
                    big_weights()

            tiles(sp, begin, both, load_out)

        @block.tensor
        def _(pe):
            ident = per["ident"]
            pe.wait_ge(w_in, 144)

            def gate(i):
                wait(pe, "gd_sig", i, 1, 1)
                wait(pe, "mixed", i - 1, 1, 1)
                pe.matmul(G[:], sgd[:], gup[:], start=True, stop=True).then_inc(q["gate_sum"], 1)

            def turn(i):
                wait(pe, "mixed", i, 1, 1)
                wait(pe, "ycT_done", i - 1, 2, 2)
                wait(pe, "base_done", i - 2, 2, 2)
                for k in range(KD):
                    bank = (T0, T1)[k // 4]
                    mm = pe.transpose(bank[:, (k % 4) * P:(k % 4 + 1) * P], ycat[:, k * P:(k + 1) * P], ident[:])
                    if k % 4 == 3:
                        mm.then_inc(q["turnedY"], 1)

            def project_out(i):
                if isinstance(i, int) and i == 0:
                    pe.wait_ge(big_in, 48)
                wait(pe, "ycT_done", i, 2, 2)
                wait(pe, "out_read", i - 1, 2, 2)
                for n, bank in enumerate((O0, O1)):
                    for k in range(KD):
                        mm = pe.matmul(bank[:], ycT[:, k, :], wout[:, k, n * 512:(n + 1) * 512], start=(k == 0), stop=(k == KD - 1))
                    mm.then_inc(q["out_sum"], 1)

            def after(i, more):
                wait(pe, "h2_done", i, 1, 1)
                if more:
                    wait(pe, "ycT_done", i + 1, 2, 2)
                for k in range(KD):
                    bank = (T0, T1)[k // 4]
                    mm = pe.transpose(bank[:, (k % 4) * P:(k % 4 + 1) * P], h2[:, k * P:(k + 1) * P], ident[:])
                    if k % 4 == 3:
                        mm.then_inc(q["turnedH"], 1)
                wait(pe, "h2T_done", i, 2, 2)
                wait(pe, "rank_read", i - 1, 2, 2)
                for k in range(KD):
                    mm = pe.matmul(R[:, 0:NE], h2T[:, k, :], wrt[:, k, :], start=(k == 0), stop=(k == KD - 1))
                mm.then_inc(q["logits"], 1)
                wait(pe, "hid_done", i - 1, 1, 1)
                for k in range(KD):
                    mm = pe.matmul(S[:], h2T[:, k, :], wsgu[:, k, :], start=(k == 0), stop=(k == KD - 1))
                mm.then_inc(q["gu"], 1)
                wait(pe, "member", i, 1, 1)
                pe.matmul(R[:, 128:128 + NE], tri[:], mem[:], start=True, stop=True)
                pe.matmul(R[:, 256:256 + NE], ones[:], mem[:], start=True, stop=True).then_inc(q["rank_sum"], 1)
                wait(pe, "hid_done", i, 1, 1)
                wait(pe, "hidT_done", i - 1, 1, 1)
                for k in range(2):
                    mm = pe.transpose(H[:, k * P:(k + 1) * P], hid[:, k * P:(k + 1) * P], ident[:])
                mm.then_inc(q["turnedS"], 1)
                wait(pe, "hidT_done", i, 1, 1)
                for n, bank in enumerate((T0, T1)):
                    for k in range(2):
                        mm = pe.matmul(bank[:], hidT[:, k, :], wsd[:, k, n * 512:(n + 1) * 512], start=(k == 0), stop=(k == 1))
                    mm.then_inc(q["down_sum"], 1)

            def mix(i):
                gate(i)
                turn(i)
                if i == 0:
                    project_out(i)

            def both(i):
                project_out(i + 1)
                gate(i + 2)
                after(i, True)
                turn(i + 2)

            def out(i):
                if i + 1 < NT:
                    project_out(i + 1)
                after(i, i + 1 < NT)

            tiles(pe, mix, both, out)

        @block.scalar
        def _(act):
            def mix1(i):
                wait(act, "gate_sum", i - 1, 1, 1)
                act.activation(sgd[:], per["gd"][:, bass.ds(LC + i * P, P)], ACT.Sigmoid).then_inc(q["gd_sig"], 1)

            def mix2(i):
                act.wait_ge(a_in, 128 * i + 128)
                wait(act, "vars", i - 1, 1, 1)
                act.activation(junk[:, 0:CH], yh[:], ACT.Square, accum_out=var[:, 1:2]).then_inc(q["sq_done"], 1)
                wait(act, "za2", i, 1, 1)
                act.activation(junk[:, CH:2 * CH], ya[:], ACT.Square, accum_out=var[:, 0:1]).then_inc(q["sq_done"], 1)
                wait(act, "vars", i, 1, 1)
                act.activation(rstd[:], var[:], ACT.Sqrt).then_inc(q["rooted1"], 1)

            def mix3(i):
                wait(act, "out_sum", i - 1, 2, 2)
                for g, bank in enumerate((T0, T1)):
                    wait(act, "turnedY", i, 2, g + 1)
                    act.copy(ycT[:, 4 * g:4 * g + 4].rearrange("p k t -> p (k t)"), bank[:]).then_inc(q["ycT_done"], 1)

            def norm(i):
                wait(act, "out_read", i, 2, 2)
                wait(act, "shifted", i, 1, 1)
                act.activation(junk[:], t[:], ACT.Identity, accum_out=stat[:, 0:1]).then_inc(q["mean_sum"], 1)
                wait(act, "mu", i, 1, 1)
                wait(act, "mean_sum", i, 1, 1)
                act.activation(junk[:], t[:], ACT.Square, bias=stat[:, 1:2], accum_out=stat[:, 2:3]).then_inc(q["var_sum"], 1)
                wait(act, "ln_var", i, 1, 1)
                act.activation(stat[:, 3:4], stat[:, 2:3], ACT.Sqrt).then_inc(q["rooted2"], 1)

            def h2_copy(i):
                wait(act, "gu", i - 1, 1, 1)
                for g, bank in enumerate((T0, T1)):
                    wait(act, "turnedH", i, 2, g + 1)
                    act.copy(h2T[:, 4 * g:4 * g + 4].rearrange("p k t -> p (k t)"), bank[:]).then_inc(q["h2T_done"], 1)
                wait(act, "logits", i, 1, 1)
                wait(act, "routed", i - 1, 1, 1)
                act.activation(sc[:], R[:, 0:NE], ACT.Sigmoid).then_inc(q["scored"], 1)

            def after(i):
                wait(act, "gu", i, 1, 1)
                wait(act, "hid_done", i - 1, 1, 1)
                act.activation(sgm[:], S[:, 0:FF], ACT.Sigmoid).then_inc(q["sig_gu"], 1)
                wait(act, "turnedS", i, 1, 1)
                act.copy(hidT[:].rearrange("p k t -> p (k t)"), H[:, 0:2 * P]).then_inc(q["hidT_done"], 1)

            def mix(i):
                mix1(i)
                mix2(i)
                mix3(i)

            def both(i):
                mix1(i + 2)
                norm(i)
                h2_copy(i)
                mix2(i + 2)
                after(i)
                mix3(i + 2)

            def out(i):
                norm(i)
                h2_copy(i)
                after(i)

            tiles(act, mix, both, out)

        @block.gpsimd
        def _(pool):
            pool.memset(ones[:], 1.0).then_inc(q["tok_in"], 1)
            pool.wait_ge(w_in, 144)
            pool.wait_ge(q["tok_in"], 1)
            ch = Chain(pool, q["pmix"], PMIX)
            v3 = lambda ap: ap.rearrange("p (h k) -> p h k", h=NH)

            def mix(i):
                ch.start(i)
                pool.wait_ge(a_in, 128 * i + 128)
                wait(pool, "za2", i - 1, 1, 1)
                ch.do(pool.tensor_tensor(z3[:], cx[:, :, 0], cx[:, :, 1], ALU.mult))
                ch.wait()
                ch.do(pool.tensor_tensor(z3[:].rearrange("p a c -> p (a c)"), z3[:].rearrange("p a c -> p (a c)"), rows[:, 0:3 * CH], ALU.mult))
                ch.wait()
                wait(pool, "mixed", i - 1, 1, 1)
                ch.do(pool.tensor_tensor(za[:], z3[:, 0], z3[:, 1], ALU.add))
                ch.wait()
                pool.wait_ge(q["dmix"], i * MIX + 1)
                ch.do(pool.tensor_tensor(v3(bonus[:]), bc(ysum[:, RC:], 2, HD), v3(v[:]), ALU.mult))
                ch.wait()
                pool.sem_inc(q["bon_done"], 1)
                ch.end()

            def out(i):
                wait(pool, "h2_done", i, 1, 1)
                pool.sem_inc(q["passed_pool"], 1)
                pool.dma_start(io["h2"][bass.ds(i * P, P)], h2[:]).then_inc(q["h2_st"], 16)
                wait(pool, "base_done", i, 2, 2)
                pool.sem_inc(q["passed_pool"], 1)
                pool.dma_start(io["base"][bass.ds(i * P, P)], base[:]).then_inc(q["base_st"], 16)

            def both(i):
                mix(i + 2)
                out(i)

            tiles(pool, mix, both, out)
            pool.wait_ge(q["h2_st"], 16 * NT)
            pool.wait_ge(q["base_st"], 16 * NT)

        @block.vector
        def _(dve):
            dve.memset(carry[:], 0.0).then_inc(q["zt"], 1)
            dve.wait_ge(w_in, 144)
            dve.wait_ge(q["zt"], 1)
            dve.wait_ge(q["tok_in"], 1)
            cm, co = Chain(dve, q["dmix"], MIX), Chain(dve, q["dout"], OUT)
            v3 = lambda ap: ap.rearrange("p (h k) -> p h k", h=NH)
            o = 3 * CH

            def mix(i):
                c = cm
                c.start(i)
                dve.wait_ge(a_in, 128 * i + 128)
                wait(dve, "bon_done", i - 1, 1, 1)
                c.do(dve.tensor_tensor(ysum[:], y01[:, 0], y01[:, 1], ALU.add))
                c.wait()
                c.do(dve.tensor_reduce(mean8[:], v3(ysum[:, 0:RC]), AX_X, ALU.add))
                c.wait()
                c.do(dve.tensor_scalar(mean8[:], mean8[:], 1.0 / HD, None, ALU.mult))
                c.wait()
                c.do(dve.tensor_tensor(v3(yn[:]), v3(ysum[:, 0:RC]), bc(mean8[:], 2, HD), ALU.subtract))
                c.wait()
                c.do(dve.tensor_tensor(sqr[:], yn[:], yn[:], ALU.mult))
                dve.wait_ge(q["pmix"], i * PMIX + 3)
                c.do(dve.tensor_tensor(za[:], za[:], z3[:, 2], ALU.add))
                c.wait()
                c.do(dve.tensor_tensor(ya[:], za[:], b[:], ALU.mult))
                c.wait()
                dve.sem_inc(q["za2"], 1)
                wait(dve, "rooted1", i - 1, 1, 1)
                c.do(dve.tensor_reduce(var[:, 2:], v3(sqr[:]), AX_X, ALU.add))
                c.wait()
                c.do(dve.tensor_scalar(var[:, 2:], var[:, 2:], 1.0 / HD, GN_EPS, ALU.mult, ALU.add))
                wait(dve, "sq_done", i, 2, 2)
                c.do(dve.tensor_scalar(var[:, 0:2], var[:, 0:2], 1.0 / CH, LN_EPS, ALU.mult, ALU.add))
                c.wait()
                dve.sem_inc(q["vars"], 1)
                wait(dve, "rooted1", i, 1, 1)
                c.do(dve.reciprocal(rstd[:], rstd[:]))
                c.wait()
                wait(dve, "turnedY", i - 1, 2, 2)
                c.do(dve.scalar_tensor_tensor(ycat[:, 0:CH], ya[:], rstd[:, 0:1], rows[:, o:o + CH], ALU.mult, ALU.mult))
                c.do(dve.scalar_tensor_tensor(ycat[:, CH:2 * CH], yh[:], rstd[:, 1:2], rows[:, o + CH:o + 2 * CH], ALU.mult, ALU.mult))
                c.do(dve.tensor_tensor(v3(yn[:]), v3(yn[:]), bc(rstd[:, 2:], 2, HD), ALU.mult))
                c.wait()
                g0 = o + 2 * CH
                c.do(dve.tensor_tensor(yn[:], yn[:], rows[:, g0:g0 + RC], ALU.mult))
                c.wait()
                c.do(dve.tensor_tensor(yn[:], yn[:], rows[:, g0 + RC:g0 + 2 * RC], ALU.add))
                c.wait()
                wait(dve, "bon_done", i, 1, 1)
                c.do(dve.tensor_tensor(yn[:], yn[:], bonus[:], ALU.add))
                c.wait()
                wait(dve, "gate_sum", i, 1, 1)
                c.do(dve.tensor_tensor(ycat[:, 2 * CH:], yn[:], G[:], ALU.mult))
                c.wait()
                dve.sem_inc(q["mixed"], 1)
                c.end()

            def norm(i):
                c = co
                c.start(i)
                dve.wait_ge(x_in, 16 * i + 16)
                g1 = per["rows"][:, 0:D]
                wait(dve, "var_sum", i - 1, 1, 1)
                for n, bank in enumerate((O0, O1)):
                    wait(dve, "out_sum", i, 2, n + 1)
                    dve.tensor_tensor(t[:, n * 512:(n + 1) * 512], bank[:], g1[:, n * 512:(n + 1) * 512], ALU.mult).then_inc(q["out_read"], 1)
                wait(dve, "out_read", i, 2, 2)
                dve.scalar_tensor_tensor(t[:], x[:], ALPHA, t[:], ALU.mult, ALU.add).then_inc(q["shifted"], 1)
                wait(dve, "mean_sum", i, 1, 1)
                dve.sem_inc(q["x_free"], 1)
                c.do(dve.tensor_scalar(stat[:, 1:2], stat[:, 0:1], -1.0 / D, None, ALU.mult))
                c.wait()
                dve.sem_inc(q["mu"], 1)
                wait(dve, "var_sum", i, 1, 1)
                c.do(dve.tensor_scalar(stat[:, 2:3], stat[:, 2:3], 1.0 / D, LN_EPS, ALU.mult, ALU.add))
                c.wait()
                dve.sem_inc(q["ln_var"], 1)
                wait(dve, "rooted2", i, 1, 1)
                c.do(dve.reciprocal(stat[:, 3:4], stat[:, 3:4]))
                c.wait()
                c.do(dve.tensor_scalar(x1[:], t[:], stat[:, 1:2], stat[:, 3:4], ALU.add, ALU.mult))
                c.wait()
                c.do(dve.tensor_tensor(x1[:], x1[:], lnr[:, 0], ALU.mult))
                c.wait()
                c.do(dve.tensor_tensor(x1[:], x1[:], lnr[:, 1], ALU.add))
                c.wait()
                wait(dve, "turnedH", i - 1, 2, 2)
                wait(dve, "h2_st", i - 1, 16, 16)
                c.do(dve.tensor_tensor(h2[:], x1[:], per["rows"][:, 2 * D:3 * D], ALU.mult))
                c.wait()
                dve.tensor_tensor(h2[:], h2[:], per["rows"][:, D:2 * D], ALU.add).then_inc(q["h2_done"], 1)

            def after(i):
                c = co
                wait(dve, "scored", i, 1, 1)
                c.do(dve.tensor_tensor(biased[:], sc[:], ebias[:], ALU.add))
                c.wait()
                dve.sem_inc(q["passed"], 1)
                c.do(dve.max(top[:], biased[:]))
                c.wait()
                dve.sem_inc(q["passed"], 1)
                c.do(dve.max_index(topi[:], top[:], biased[:]))
                c.wait()
                c.do(dve.tensor_copy(topf[:], topi[:]))
                c.wait()
                oh = OH[:, bass.ds(i, 1)].rearrange("p o j e -> p (o j) e")
                c.do(dve.tensor_tensor(oh, bc(iota[:], 1, TOPK), bc(topf[:], 2, NE), ALU.is_equal))
                c.wait()
                dve.sem_inc(q["passed"], 1)
                dve.tensor_reduce(mem[:], oh.rearrange("p j e -> p e j"), AX_X, ALU.add).then_inc(q["member"], 1)
                c.do(dve.tensor_tensor(sel3[:], oh, bc(sc[:], 1, TOPK), ALU.mult))
                c.wait()
                gt = gates[:, bass.ds(i, 1)].rearrange("p o j -> p (o j)")
                c.do(dve.tensor_reduce(gt, sel3[:], AX_X, ALU.add))
                c.wait()
                dve.sem_inc(q["routed"], 1)
                c.do(dve.tensor_reduce(gsum[:, 0:1], gt, AX_X, ALU.add))
                c.wait()
                c.do(dve.reciprocal(gsum[:, 1:2], gsum[:, 0:1]))
                c.wait()
                c.do(dve.tensor_scalar(gt, gt, gsum[:, 1:2], ROUTED, ALU.mult, ALU.mult))
                wait(dve, "sig_gu", i, 1, 1)
                wait(dve, "turnedS", i - 1, 1, 1)
                c.do(dve.tensor_tensor(hid[:], sgm[:], S[:, 0:FF], ALU.mult))
                c.wait()
                dve.tensor_tensor(hid[:], hid[:], S[:, FF:2 * FF], ALU.mult).then_inc(q["hid_done"], 1)
                wait(dve, "rank_sum", i, 1, 1)
                dve.tensor_tensor(rank[:], R[:, 128:128 + NE], carry[:], ALU.add).then_inc(q["rank_read"], 1)
                wait(dve, "rank_read", i, 2, 1)
                dve.tensor_tensor(carry[:], R[:, 256:256 + NE], carry[:], ALU.add).then_inc(q["rank_read"], 1)
                c.do(dve.tensor_tensor(sel3[:], oh, bc(rank[:], 1, TOPK), ALU.mult))
                c.wait()
                c.do(dve.tensor_reduce(rnk[:, bass.ds(i, 1)].rearrange("p o j -> p (o j)"), sel3[:], AX_X, ALU.add))
                c.wait()
                wait(dve, "rank_read", i, 2, 2)
                wait(dve, "base_st", i - 1, 16, 16)
                g2 = per["rows"][:, 3 * D:4 * D]
                for n, bank in enumerate((T0, T1)):
                    wait(dve, "down_sum", i, 2, n + 1)
                    dve.tensor_tensor(base[:, n * 512:(n + 1) * 512], bank[:], g2[:, n * 512:(n + 1) * 512], ALU.mult).then_inc(q["tail"], 1)
                    wait(dve, "tail", i, 2, n + 1)
                    dve.scalar_tensor_tensor(base[:, n * 512:(n + 1) * 512], x1[:, n * 512:(n + 1) * 512], ALPHA,
                                             base[:, n * 512:(n + 1) * 512], ALU.mult, ALU.add).then_inc(q["base_done"], 1)
                wait(dve, "base_done", i, 2, 2)
                c.end()

            def both(i):
                norm(i)
                mix(i + 2)
                after(i)

            def out(i):
                norm(i)
                after(i)

            tiles(dve, mix, both, out)

        tiling.close()

        nb = m.sb("nb", [P, NE])
        ends = [m.sb(f"ends{n}", [P, NE]) for n in range(2)]
        first = m.sb("first", [P, NE])
        tab = m.sb("tab", [P, TAB + 4])
        tabi = m.sb("tabi", [P, TAB], I32)
        npairs = m.sb("npairs", [P, 2])
        npi = m.sb("npi", [P, 2], I32)
        tok = m.sb("tok", [P, NT], I32)
        zi = m.sb("zi", [P, P], I32)
        route = sems("route")
        slots_ready, be_ready, zero_ready, tok_ready = (sems(x) for x in ("slots_ready", "be_ready", "zero_ready", "tok_ready"))
        zero_out, be_out, tok_out = sems("zero_out"), sems("be_out"), sems("tok_out")
        tables = ExitStack()
        block = tables.enter_context(nc.Block())

        @block.vector
        def _(dve):
            c = Chain(dve, route, 0)
            c.start(0)

            def do(ins):
                c.do(ins)
                c.wait()

            dve.memset(zi[:], 0).then_inc(zero_ready, 1)
            cmp = sel3[:].rearrange("p j e -> p (j e)").rearrange("p (e n) -> p e n", n=8)
            do(dve.tensor_tensor(cmp, bc(carry[:], 2, 8), bc(thresh[:], 1, NE), ALU.is_gt))
            do(dve.tensor_reduce(nb[:], cmp, AX_X, ALU.add))
            do(dve.tensor_copy(ends[0][:], nb[:]))
            for n in range(6):
                a, z, sh = ends[n % 2], ends[(n + 1) % 2], 2 ** n
                do(dve.tensor_copy(z[:, 0:sh], a[:, 0:sh]))
                do(dve.tensor_tensor(z[:, sh:], a[:, sh:], a[:, 0:NE - sh], ALU.add))
            do(dve.tensor_tensor(first[:], ends[0][:], nb[:], ALU.subtract))
            do(dve.tensor_scalar(first[:], first[:], float(P), None, ALU.mult))
            for i in range(NT):
                do(dve.tensor_tensor(sel3[:], OH[:, i], bc(first[:], 1, TOPK), ALU.mult))
                do(dve.tensor_reduce(slots[:, i], sel3[:], AX_X, ALU.add))
            do(dve.tensor_tensor(slots[:], slots[:], rnk[:], ALU.add))
            dve.tensor_copy(slots_i[:], slots[:]).then_inc(slots_ready, 1)
            do(dve.tensor_tensor(rank[:], ends[0][:], iotap[:].broadcast_to([P, NE]), ALU.is_le))
            do(dve.tensor_reduce(tab[:, 0:1], rank[:], AX_X, ALU.add))
            do(dve.tensor_scalar(tab[:, 0:1], tab[:, 0:1], float(NE - 1), None, ALU.min))
            do(dve.tensor_scalar(biased[:], nb[:], 0.0, None, ALU.is_gt))
            do(dve.tensor_tensor(rank[:], rank[:], biased[:], ALU.mult))
            do(dve.tensor_reduce(tab[:, 6:7], rank[:], AX_X, ALU.add))
            do(dve.tensor_scalar(rank[:], iota[:], 2.0, tab[:, 6:7], ALU.mult, ALU.is_lt))
            do(dve.tensor_reduce(tab[:, 7:8], rank[:], AX_X, ALU.add))
            do(dve.tensor_scalar(tab[:, 5:6], tab[:, 7:8], 2.0, tab[:, 6:7], ALU.mult, ALU.subtract))
            do(dve.tensor_tensor(rank[:], ends[0][:], iotap[:].broadcast_to([P, NE]), ALU.is_equal))
            do(dve.tensor_tensor(rank[:], rank[:], biased[:], ALU.mult))
            do(dve.tensor_reduce(tab[:, 6:7], rank[:], AX_X, ALU.add))
            do(dve.tensor_scalar(tab[:, 7:8], iotap[:], 0.0, None, ALU.is_equal))
            do(dve.tensor_tensor(tab[:, 6:7], tab[:, 6:7], tab[:, 7:8], ALU.add))
            do(dve.tensor_tensor(tab[:, 2:3], tab[:, 6:7], tab[:, 5:6], ALU.mult))
            do(dve.tensor_tensor(tab[:, 1:2], tab[:, 6:7], tab[:, 2:3], ALU.subtract))
            do(dve.tensor_scalar(tab[:, 7:8], iotap[:], 2.0, None, ALU.mult))
            for column, op in ((3, ALU.is_lt), (4, ALU.is_equal), (5, ALU.is_equal)):
                if column == 5:
                    do(dve.tensor_scalar(tab[:, 7:8], tab[:, 7:8], 1.0, None, ALU.add))
                do(dve.tensor_tensor(rank[:], ends[0][:], tab[:, 7:8].broadcast_to([P, NE]), op))
                do(dve.tensor_tensor(rank[:], rank[:], biased[:], ALU.mult))
                do(dve.tensor_reduce(tab[:, column:column + 1], rank[:], AX_X, ALU.add))
            do(dve.tensor_scalar(tab[:, 3:4], tab[:, 3:4], 2.0, tab[:, 4:5], ALU.mult, ALU.add))
            do(dve.tensor_scalar(tab[:, 3:4], tab[:, 3:4], 2.0, tab[:, 5:6], ALU.mult, ALU.add))
            dve.tensor_copy(tabi[:], tab[:, 0:TAB]).then_inc(be_ready, 1)
            do(dve.tensor_scalar(rank[:], iota[:], 2.0, ends[0][:, NE - 1:NE], ALU.mult, ALU.is_lt))
            do(dve.tensor_reduce(npairs[:, 0:1], rank[:], AX_X, ALU.add))
            do(dve.tensor_scalar(npairs[:, 1:2], npairs[:, 0:1], -1.0, (NBLK + 1) / 2, ALU.mult, ALU.add))
            do(dve.tensor_scalar(npairs[:, 0:1], npairs[:, 0:1], L * TOPK / P / 2, None, ALU.subtract))
            dve.tensor_copy(npi[:], npairs[:]).then_inc(be_ready, 1)

        @block.sync
        def _(sp):
            sp.wait_ge(zero_ready, 1)
            sp.dma_start(io["slot_token"].rearrange("(b p) o -> b (p o)", p=P), zi[:]).then_inc(zero_out, 16)
            sp.wait_ge(be_ready, 1)
            sp.dma_start(io["block_table"].rearrange("o (b x) -> b (o x)", x=TAB), tabi[:]).then_inc(be_out, 16)
            sp.wait_ge(be_ready, 2)
            sp.dma_start(io["n_pairs"], npi[0:1, :]).then_inc(be_out, 16)
            sp.wait_ge(zero_out, 16)
            sp.wait_ge(be_out, 32)

        @block.gpsimd
        def _(pool):
            pool.iota(tok[:], [[P, NT]], base=0, channel_multiplier=1).then_inc(tok_ready, 1)
            pool.wait_ge(tok_ready, 1)
            pool.wait_ge(slots_ready, 1)
            pool.wait_ge(zero_out, 16)
            for i in range(NT):
                for j in range(TOPK):
                    pool.indirect_dma_start(out=io["slot_token"], out_offset=bass.IndirectOffsetOnAxis(ap=slots_i[:, i, j:j + 1], axis=0),
                                            in_=tok[:, i:i + 1], in_offset=None).then_inc(tok_out, 16)
            pool.wait_ge(tok_out, 16 * NT * TOPK)

        tables.close()


def experts(nc, sems, io, per):
    with ExitStack() as ctx:
        m = Mem(nc, ctx, "ex")
        NB = NBLK + 1
        SURE = L * TOPK // P
        wg = m.sb("wg", [P, 2, KD, FF])
        wu = m.sb("wu", [P, 2, KD, FF])
        wd = m.sb("wd", [P, 2, 2, D])
        xg = [m.sb(f"xg{s}", [P, D]) for s in range(2)]
        xT = [m.sb(f"xT{s}", [P, KD, P]) for s in range(2)]
        y = [m.sb(f"y{s}", [P, D]) for s in range(2)]
        sg = m.sb("sg", [P, FF])
        hid = m.sb("hid", [P, FF])
        hidT = m.sb("hidT", [P, 2, P])
        zero = m.sb("zero", [P, D])
        table = m.sb("table", [1, P * TAB], I32)
        idx_b = m.sb("idx_b", [P, P], I32)
        idx_f = m.sb("idx_f", [P, P])
        idx = m.sb("idx", [P, P + 1], I32)
        n_pairs = m.sb("n_pairs", [1, 2], I32)
        idx_now = [m.sb(f"idx_now{s}", [P, 1], I32) for s in range(2)]
        T0, T1, H, O0, O1 = (m.ps(x) for x in ("T0", "T1", "H", "O0", "O1"))
        S = [m.ps(f"S{s}") for s in range(2)]
        q = {n: sems(n) for n in ("be_in idx_in idx_conv idx_turned idx_ready turned xT_done gu_sum sig_done hid_part hid_done "
                                  "pairs_in zeroed spare_out turnedS hidT_done down_sum y_done idx_copied passed").split()}
        wg_in, wd_in, x_in, y_out = ([sems(f"{x}{s}") for s in range(2)] for x in ("wg_in", "wd_in", "x_in", "y_out"))
        block = ctx.enter_context(nc.Block())

        def first(b):
            return isinstance(b, int) and b == 0

        def wait(eng, name, b, per_block, k):
            v = b * per_block + k
            if not (isinstance(v, int) and v <= 0):
                eng.wait_ge(q[name], v)

        def entry(eng, b, column, most):
            return eng.value_load(table[0:1, bass.ds(TAB * b + column, 1)], min_val=0, max_val=most)

        def blocks(eng, body, beside=None, record=None):
            eng.wait_ge(q["pairs_in"], 16)
            more = eng.value_load(n_pairs[0:1, 0:1], min_val=0, max_val=(NB - SURE) // 2)
            def pair(j):
                info = (record(j),) if record else ()
                for s in range(2):
                    body(2 * j + s, s, *info)

            for p in range(2):
                pair(p)
                if beside:
                    beside(more, (NB // 2 - SURE // 2, NB // 2 - 1)[p])
            with eng.Fori(1, SURE // 4) as j:
                for p in range(2):
                    pair(2 * j + p)
                    if beside:
                        beside(more, NB // 2 - (2 * j + p))
            with eng.Fori(SURE // 2, NB // 2) as j:
                with eng.If(j < more + SURE // 2):
                    pair(j)
            return more

        @block.sync
        def _(sp):
            sp.dma_start(n_pairs[:], io["n_pairs"]).then_inc(q["pairs_in"], 16)
            sp.dma_start(table[:], io["block_table"]).then_inc(q["be_in"], 16)
            sp.dma_start(idx_b[:], io["slot_token"].rearrange("(b p) o -> b (p o)", p=P)).then_inc(q["idx_in"], 16)
            sp.wait_ge(q["be_in"], 16)
            sp.sem_inc(wg_in[1], 16)
            sp.sem_inc(wd_in[1], 16)

            def load(b, s):
                e, to0, to1 = (entry(sp, b, n, most) for n, most in ((0, NE - 1), (1, 1), (2, 1)))
                wait(sp, "gu_sum", b - 2, 1, 1)
                sp.sem_inc(q["passed"], 1)
                for slot, here in enumerate((to0, to1)):
                    with sp.If(here > 0):
                        for dst, src in ((wg, "w_e_gate"), (wu, "w_e_up")):
                            sp.dma_start(dst[:, slot].rearrange("p k f -> p (k f)"),
                                         io[src][bass.ds(e, 1)].rearrange("o (p k) f -> p (o k f)", p=P)).then_inc(wg_in[slot], 16)
                wait(sp, "down_sum", b - 2, 2, 2)
                sp.sem_inc(q["passed"], 1)
                for slot, here in enumerate((to0, to1)):
                    with sp.If(here > 0):
                        sp.dma_start(wd[:, slot].rearrange("p k f -> p (k f)"),
                                     io["w_e_down"][bass.ds(e, 1)].rearrange("o (p k) d -> p (o k d)", p=P)).then_inc(wd_in[slot], 16)

            sp.wait_ge(q["zeroed"], 1)
            sp.sem_inc(q["spare_out"], 16)

            def spare(more, p):
                with sp.If(more + SURE // 2 <= p):
                    for s in range(2):
                        sp.dma_start(io["eslots"][bass.ds((2 * p + s) * P, P)], zero[:]).then_inc(q["spare_out"], 16)

            blocks(sp, load, spare)
            n_spare = sp.value_load(n_pairs[0:1, 1:2], min_val=0, max_val=(NB - SURE) // 2)
            sp.wait_ge(q["spare_out"], 32 * n_spare + 16)
            sp.sem_inc(q["passed"], 1)

        @block.gpsimd
        def _(pool):
            pool.wait_ge(q["idx_ready"], 1)

            def gather(b, s):
                wait(pool, "turned", b - 2, 2, 2)
                if isinstance(b, int) and b < 2:
                    pass
                else:
                    pool.wait_ge(x_in[s], 16 * (b - s) // 2 if isinstance(b, int) else 8 * (b - s))
                pool.tensor_copy(idx_now[s][:], idx[:, bass.ds(b, 1)]).then_inc(q["idx_copied"], 1)
                wait(pool, "idx_copied", b, 1, 1)
                pool.sem_inc(q["passed"], 1)
                pool.indirect_dma_start(out=xg[s][:], out_offset=None, in_=io["h2"],
                                        in_offset=bass.IndirectOffsetOnAxis(ap=idx_now[s][:], axis=0)).then_inc(x_in[s], 16)

            gather(0, 0)
            blocks(pool, lambda b, s: gather(b + 1, 1 - s))

        @block.tensor
        def _(pe):
            ident = per["ident"]
            pe.wait_ge(q["idx_conv"], 1)
            pe.transpose(H[:, 0:P], idx_f[:], ident[:]).then_inc(q["idx_turned"], 1)
            pe.wait_ge(q["idx_ready"], 1)
            pe.wait_ge(q["be_in"], 16)

            def turn(b, s):
                pe.wait_ge(x_in[s], 8 * (b - s) + 16)
                wait(pe, "xT_done", b - 1, 2, 2)
                for k in range(KD):
                    mm = pe.transpose((T0, T1)[k // 4][:, (k % 4) * P:(k % 4 + 1) * P], xg[s][:, k:D:KD], ident[:])
                    if k % 4 == 3:
                        mm.then_inc(q["turned"], 1)

            def record(j):
                pe.sem_inc(q["passed"], 1)
                r = entry(pe, j, 3, 4 * NE + 3)
                before = r // 4
                first_ = before + r // 2 % 2
                return before, first_, first_ + r % 2

            def gate_up(b, s, n):
                slot = n % 2
                pe.wait_ge(wg_in[0], 32 * ((n + 2) // 2))
                pe.wait_ge(wg_in[1], 32 * ((n + 1) // 2) + 16)
                wait(pe, "xT_done", b, 2, 2)
                wait(pe, "hid_done", b - 2, 1, 1)
                for w, c0 in ((wg, 0), (wu, FF)):
                    for k in range(KD):
                        mm = pe.matmul(S[s][:, c0:c0 + FF], xT[s][:, k, :], w[:, bass.ds(slot, 1), k, :].rearrange("p o f -> p (o f)"), start=(k == 0), stop=(k == KD - 1))
                mm.then_inc(q["gu_sum"], 1)

            def turn_hid(b, s):
                wait(pe, "hid_done", b, 1, 1)
                wait(pe, "hidT_done", b - 1, 1, 1)
                for k in range(2):
                    mm = pe.transpose(H[:, k * P:(k + 1) * P], hid[:, k:FF:2], ident[:])
                mm.then_inc(q["turnedS"], 1)

            def down(b, s, n):
                wait(pe, "hidT_done", b, 1, 1)
                slot = n % 2
                pe.wait_ge(wd_in[0], 16 * ((n + 2) // 2))
                pe.wait_ge(wd_in[1], 16 * ((n + 1) // 2) + 16)
                for half, bank in enumerate((O0, O1)):
                    wait(pe, "y_done", b - 1, 2, half + 1)
                    for k in range(2):
                        mm = pe.matmul(bank[:], hidT[:, k, :], wd[:, bass.ds(slot, 1), k, half * 512:(half + 1) * 512].rearrange("p o d -> p (o d)"), start=(k == 0), stop=(k == 1))
                    mm.then_inc(q["down_sum"], 1)

            turn(0, 0)

            def body(b, s, ordinals):
                gate_up(b, s, ordinals[1 + s])
                if not first(b):
                    turn_hid(b - 1, 1 - s)
                turn(b + 1, 1 - s)
                if not first(b):
                    down(b - 1, 1 - s, ordinals[s])

            more = blocks(pe, body, record=record)
            last = 2 * more + SURE - 1
            turn_hid(last, 1)
            down(last, 1, record(more + SURE // 2 - 1)[2])

        @block.scalar
        def _(act):
            def x_copy(b, s):
                wait(act, "gu_sum", b - 2, 1, 1)
                for n, bank in enumerate((T0, T1)):
                    wait(act, "turned", b, 2, n + 1)
                    act.copy(xT[s][:, 4 * n:4 * n + 4].rearrange("p k t -> p (k t)"), bank[:]).then_inc(q["xT_done"], 1)

            def rest(b, s):
                wait(act, "gu_sum", b, 1, 1)
                wait(act, "hid_part", b - 1, 1, 1)
                act.activation(sg[:], S[s][:, 0:FF], ACT.Sigmoid).then_inc(q["sig_done"], 1)

            def hid_copy(b):
                wait(act, "turnedS", b, 1, 1)
                wait(act, "down_sum", b - 1, 2, 2)
                act.copy(hidT[:].rearrange("p k t -> p (k t)"), H[:, 0:2 * P]).then_inc(q["hidT_done"], 1)

            def store(b, s):
                wait(act, "y_done", b, 2, 2)
                act.sem_inc(q["passed"], 1)
                act.dma_start(io["eslots"][bass.ds(b * P, P)], y[s][:]).then_inc(y_out[s], 16)

            x_copy(0, 0)

            def body(b, s):
                rest(b, s)
                if not first(b):
                    hid_copy(b - 1)
                x_copy(b + 1, 1 - s)
                if not first(b):
                    store(b - 1, 1 - s)

            more = blocks(act, body)
            last = 2 * more + SURE - 1
            hid_copy(last)
            store(last, 1)
            for s in range(2):
                act.wait_ge(y_out[s], 16 * more + 8 * SURE)
                act.sem_inc(q["passed"], 1)

        @block.vector
        def _(dve):
            dve.memset(idx[:, P:], 0)
            dve.memset(zero[:], 0.0).then_inc(q["zeroed"], 1)
            dve.wait_ge(q["idx_in"], 16)
            dve.tensor_copy(idx_f[:], idx_b[:]).then_inc(q["idx_conv"], 1)
            dve.wait_ge(q["idx_turned"], 1)
            dve.tensor_copy(idx[:, 0:P], H[:, 0:P]).then_inc(q["idx_ready"], 1)

            def hidden(b, s):
                wait(dve, "sig_done", b, 1, 1)
                wait(dve, "turnedS", b - 1, 1, 1)
                dve.tensor_tensor(hid[:], sg[:], S[s][:, 0:FF], ALU.mult).then_inc(q["hid_part"], 1)
                wait(dve, "hid_part", b, 1, 1)
                dve.tensor_tensor(hid[:], hid[:], S[s][:, FF:2 * FF], ALU.mult).then_inc(q["hid_done"], 1)

            def rows(b, s):
                if not (isinstance(b, int) and b < 2):
                    dve.wait_ge(y_out[s], 8 * (b - s))
                for n, bank in enumerate((O0, O1)):
                    wait(dve, "down_sum", b, 2, n + 1)
                    dve.tensor_copy(y[s][:, n * 512:(n + 1) * 512], bank[:]).then_inc(q["y_done"], 1)

            def body(b, s):
                hidden(b, s)
                if not first(b):
                    rows(b - 1, 1 - s)

            last = 2 * blocks(dve, body) + SURE - 1
            rows(last, 1)


def combine(nc, sems, io, per):
    with ExitStack() as ctx:
        m = Mem(nc, ctx, "co")
        ONPE = 5
        yg = [m.sb(f"yg{s}", [P, TOPK, D]) for s in range(2)]
        idx_now = [m.sb(f"cidx{s}", [P, TOPK], U32) for s in range(2)]
        gnow = [m.sb(f"gnow{s}", [P, TOPK]) for s in range(2)]
        base = [m.sb(f"cbase{s}", [P, D]) for s in range(2)]
        acc = [m.sb(f"acc{s}", [P, D]) for s in range(2)]
        o = [m.sb(f"o{s}", [P, D]) for s in range(2)]
        stat = [m.sb(f"cstat{s}", [P, 4]) for s in range(2)]
        diag = [m.sb(f"diag{s}", [P, ONPE, P]) for s in range(2)]
        lnr = m.sb("clnr", [P, 2, D])
        junk = m.sb("cjunk", [P, D])
        O = [[m.ps(f"cO{s}{n}") for n in range(2)] for s in range(2)]
        q = {n: sems(n) for n in ("ln_in idx_copied gates_now diag_done pe_sum terms acc_done mean_sum mu var_sum ln_var "
                                  "rooted scaled normed out_done dfin passed").split()}
        base_in, stored = ([sems(f"{x}{s}") for s in range(2)] for x in ("base_in", "stored"))
        pe_in, dve_in = ([sems(f"{x}{s}") for s in range(2)] for x in ("pe_in", "dve_in"))
        block = ctx.enter_context(nc.Block())
        TERMS = TOPK - ONPE + 3
        FIN = 4

        def wait(eng, name, i, per_tile, k):
            v = i * per_tile + k
            if not (isinstance(v, int) and v <= 0):
                eng.wait_ge(q[name], v)

        def slot_wait(eng, sem, i, s, each, more):
            v = each // 2 * (i - s) + more
            if not (isinstance(v, int) and v <= 0):
                eng.wait_ge(sem[s], v)

        def tiles(eng, body, first=None):
            (first or body)(0, 0)
            body(1, 1)
            with eng.Fori(1, NT // 2) as j:
                for s in range(2):
                    body(2 * j + s, s)

        @block.sync
        def _(sp):
            sp.dma_start(lnr[:].rearrange("p a d -> p (a d)"), io["ln_rows"][2 * D:4 * D].partition_broadcast(P)).then_inc(q["ln_in"], 16)

            def load(i, s):
                wait(sp, "acc_done", i - 2, 1, 1)
                sp.dma_start(base[s][:], io["base"][bass.ds(i * P, P)]).then_inc(base_in[s], 16)

            def store(i, s):
                wait(sp, "out_done", i, 1, 1)
                sp.dma_start(io["out"][0, bass.ds(i * P, P)], o[s][:]).then_inc(stored[s], 16)

            def body(i, s):
                load(i, s)
                store(i - 1, 1 - s)

            tiles(sp, body, load)
            store(NT - 1, 1)
            for s in range(2):
                sp.wait_ge(stored[s], 16 * NT // 2)

        @block.gpsimd
        def _(pool):
            def body(i, s):
                slot_wait(pool, pe_in, i, s, 16 * ONPE, 0)
                slot_wait(pool, dve_in, i, s, 16 * (TOPK - ONPE), 0)
                pool.tensor_copy(idx_now[s][:], per["slots_i"][:, bass.ds(i, 1)].rearrange("p o j -> p (o j)")).then_inc(q["idx_copied"], 1)
                wait(pool, "pe_sum", i - 2, 1, 1)
                pool.sem_inc(q["passed"], 1)
                wait(pool, "terms", i - 2, TERMS, TOPK - ONPE)
                pool.sem_inc(q["passed"], 1)
                wait(pool, "idx_copied", i, 1, 1)
                pool.sem_inc(q["passed"], 1)
                for j in range(TOPK):
                    pool.indirect_dma_start(out=yg[s][:, j, :], out_offset=None, in_=io["eslots"],
                                            in_offset=bass.IndirectOffsetOnAxis(ap=idx_now[s][:, j:j + 1], axis=0)
                                            ).then_inc((pe_in if j < ONPE else dve_in)[s], 16)

            tiles(pool, body)

        @block.tensor
        def _(pe):
            def body(i, s):
                wait(pe, "diag_done", i, ONPE, ONPE)
                slot_wait(pe, pe_in, i, s, 16 * ONPE, 16 * ONPE)
                wait(pe, "terms", i - 2, TERMS, TOPK - ONPE + 2)
                for n in range(2):
                    for j in range(ONPE):
                        mm = pe.matmul(O[s][n][:], diag[s][:, j], yg[s][:, j, n * 512:(n + 1) * 512], start=(j == 0), stop=(j == ONPE - 1))
                mm.then_inc(q["pe_sum"], 1)

            tiles(pe, body)

        @block.vector
        def _(dve):
            dve.wait_ge(q["ln_in"], 16)
            ct, cf = Chain(dve, q["terms"], TERMS), Chain(dve, q["dfin"], FIN)

            def term(i, s, j):
                if j == ONPE:
                    ct.do(dve.tensor_scalar(acc[s][:], yg[s][:, j], gnow[s][:, j:j + 1], None, ALU.mult))
                else:
                    ct.wait()
                    ct.do(dve.scalar_tensor_tensor(acc[s][:], yg[s][:, j], gnow[s][:, j:j + 1], acc[s][:], ALU.mult, ALU.add))

            def finish1(i, s):
                cf.start(i)
                wait(dve, "mean_sum", i, 1, 1)
                dve.tensor_scalar(stat[s][:, 1:2], stat[s][:, 0:1], -1.0 / D, None, ALU.mult).then_inc(q["mu"], 1)

            def finish2(i, s):
                wait(dve, "var_sum", i, 1, 1)
                dve.tensor_scalar(stat[s][:, 2:3], stat[s][:, 2:3], 1.0 / D, LN_EPS, ALU.mult, ALU.add).then_inc(q["ln_var"], 1)

            def finish3(i, s):
                wait(dve, "rooted", i, 1, 1)
                cf.do(dve.reciprocal(stat[s][:, 3:4], stat[s][:, 3:4]))
                cf.wait()
                cf.do(dve.tensor_tensor(stat[s][:, 1:2], stat[s][:, 1:2], stat[s][:, 3:4], ALU.mult))
                cf.wait()
                dve.sem_inc(q["scaled"], 1)

            def finish4(i, s):
                wait(dve, "normed", i, 1, 1)
                cf.do(dve.tensor_tensor(o[s][:], o[s][:], lnr[:, 0], ALU.mult))
                cf.wait()
                cf.do(dve.tensor_tensor(o[s][:], o[s][:], lnr[:, 1], ALU.add))
                cf.wait()
                dve.sem_inc(q["out_done"], 1)
                cf.end()

            def body(i, s, finish=True):
                ct.start(i)
                wait(dve, "gates_now", i, 1, 1)
                slot_wait(dve, dve_in, i, s, 16 * (TOPK - ONPE), 16 * (TOPK - ONPE))
                wait(dve, "normed", i - 2, 1, 1)
                term(i, s, ONPE)
                term(i, s, ONPE + 1)
                if finish:
                    finish1(i - 1, 1 - s)
                for j in range(ONPE + 2, TOPK):
                    term(i, s, j)
                if finish:
                    finish2(i - 1, 1 - s)
                wait(dve, "pe_sum", i, 1, 1)
                ct.wait()
                for n in range(2):
                    half = acc[s][:, n * 512:(n + 1) * 512]
                    ct.do(dve.tensor_tensor(half, half, O[s][n][:], ALU.add))
                if finish:
                    finish3(i - 1, 1 - s)
                ct.wait()
                ct.do(dve.tensor_tensor(acc[s][:], acc[s][:], per["rows"][:, 3 * D:4 * D], ALU.mult))
                ct.wait()
                slot_wait(dve, base_in, i, s, 16, 16)
                dve.tensor_tensor(acc[s][:], acc[s][:], base[s][:], ALU.add).then_inc(q["acc_done"], 1)
                ct.end()
                if finish:
                    finish4(i - 1, 1 - s)

            tiles(dve, body, lambda i, s: body(i, s, False))
            for part in (finish1, finish2, finish3, finish4):
                part(NT - 1, 1)

        @block.scalar
        def _(act):
            def gates(i, s):
                wait(act, "terms", i - 2, TERMS, TOPK - ONPE)
                act.copy(gnow[s][:], per["gates"][:, bass.ds(i, 1)].rearrange("p o j -> p (o j)")).then_inc(q["gates_now"], 1)
                wait(act, "gates_now", i, 1, 1)
                wait(act, "pe_sum", i - 2, 1, 1)
                for j in range(ONPE):
                    act.activation(diag[s][:, j], per["ident"][:], ACT.Identity, scale=gnow[s][:, j:j + 1]).then_inc(q["diag_done"], 1)

            def finish(i, s):
                wait(act, "acc_done", i, 1, 1)
                wait(act, "normed", i - 1, 1, 1)
                act.activation(junk[:], acc[s][:], ACT.Identity, accum_out=stat[s][:, 0:1]).then_inc(q["mean_sum"], 1)
                wait(act, "mu", i, 1, 1)
                act.activation(junk[:], acc[s][:], ACT.Square, bias=stat[s][:, 1:2], accum_out=stat[s][:, 2:3]).then_inc(q["var_sum"], 1)
                wait(act, "ln_var", i, 1, 1)
                act.activation(stat[s][:, 3:4], stat[s][:, 2:3], ACT.Sqrt).then_inc(q["rooted"], 1)
                wait(act, "scaled", i, 1, 1)
                slot_wait(act, stored, i, s, 16, 0)
                act.activation(o[s][:], acc[s][:], ACT.Identity, scale=stat[s][:, 3:4], bias=stat[s][:, 1:2]).then_inc(q["normed"], 1)

            gates(0, 0)
            gates(1, 1)
            for i in range(1, 3):
                gates(i + 1, 1 - i % 2)
                finish(i - 1, 1 - i % 2)
            with act.Fori(1, NT // 2 - 1) as j:
                for s in range(2):
                    gates(2 * j + s + 2, s)
                    finish(2 * j + s, s)
            for i in range(NT - 2, NT):
                finish(i, i % 2)




def program(nc, io):
    def scratch(name, shape, dt=F32):
        io[name] = nc.dram_tensor(name, shape, dt, kind="Internal").ap()

    scratch("u", [T + PADR, UW])
    scratch("yh", [L, CH])
    scratch("ys0", [L, RC + NH])
    scratch("ys1", [L, RC + NH])
    scratch("h2", [L, D])
    scratch("base", [L, D])
    scratch("block_table", [1, P * TAB], I32)
    scratch("n_pairs", [1, 2], I32)
    scratch("slot_token", [(NBLK + 1) * P, 1], I32)
    scratch("eslots", [(NBLK + 1) * P, D])
    with ExitStack() as ctx:
        def sems(name):
            return ctx.enter_context(nc.semaphore(name))

        keep = Mem(nc, ctx, "keep")
        per = {
            "ident": keep.sb("ident", [P, P]),
            "rows": keep.sb("rows", [P, 4 * D]),
            "cols": keep.sb("cols", [P, 16, 2]),
            "gates": keep.sb("gates", [P, NT, TOPK]),
            "slots_i": keep.sb("slots_i", [P, NT, TOPK], U32),
            "coef_now": keep.sb("coef_now", [P, 4]),
            "wd": keep.sb("wd", [P, T]),
            "ad": keep.sb("ad", [P, T]),
            "gd": keep.sb("gd", [P, T]),
        }
        id_in = sems("id_in")
        with nc.Block() as block:
            @block.sync
            def _(sp):
                sp.dma_start(per["ident"][:], io["ident"]).then_inc(id_in, 16)
                sp.wait_ge(id_in, 16)
        until_hyena, early = ExitStack(), ExitStack()
        per["filters"] = Mem(nc, until_hyena, "early").sb("filters", [P, NT, 2, 2 * CH])
        per["hT"] = Mem(nc, early, "early").sb("hT", [P, KD, T])
        phases = [modulate, project, hyena, scan, merge, experts, combine]
        for phase in phases:
            own = []

            def sems_of_phase(name, own=own, tag=phase.__name__):
                own.append(nc.alloc_semaphore(f"{tag}_{name}"))
                return own[-1]

            phase(nc, sems_of_phase, io, per)
            nc.clear_and_free_semaphores(own)
            nc.all_engine_barrier()
            if phase is project:
                early.close()
            if phase is hyena:
                until_hyena.close()


def shape_constants():
    w = (np.arange(L) + 0.5) * np.pi / L
    n = np.arange(L)
    half = np.outer(n + 0.5, w)
    full = np.outer(n, w)
    col = lambda a: np.ascontiguousarray(a.reshape(8, P, 8, P).transpose(2, 1, 0, 3))
    con = {
        "ident": np.eye(P),
        "dft_cos": np.cos(half).reshape(8, P, L).transpose(1, 0, 2),
        "dft_sin": np.sin(half).reshape(8, P, L).transpose(1, 0, 2),
        "fil_cos": col(np.cos(full)),
        "fil_sin": col(-np.sin(full)),
    }
    t = np.linspace(0.0, 1.0, L)
    bands = np.linspace(1e-4, 15, 16)
    ang = (2.0 * np.pi / L) * n[:, None] * bands[None]
    con["posT"] = np.concatenate([t[:, None], np.cos(ang), -np.sin(ang)], 1).T
    deltas = np.abs(np.linspace(math.log(1e-2) / 1.5, math.log(1e-2) / 0.3, CH))
    dec = np.exp(-t[:, None] * deltas[None]) / L
    dec1 = dec.copy()
    dec1[0] = 0.0
    con["window"] = np.concatenate([dec, dec1], 1).reshape(8, P, 2 * CH).transpose(1, 0, 2)
    tri = np.zeros((P, 2, C))
    i = np.arange(C)
    tri[:C, 0] = i[:, None] <= i[None]
    tri[:C, 1] = i[:, None] < i[None]
    tri[C:, 0] = i[:, None] >= i[None]
    tri[C:, 1] = i[:, None] > i[None]
    both = lambda a: np.concatenate([np.where(np.arange(P)[:, None] < C, a, 0), np.where(np.arange(P)[:, None] < C, 0, a)], 1)
    bd = lambda a: np.stack([both(a[:, n]) for n in range(a.shape[1])], 1)
    con["tri"] = bd(tri)[:, 0] * LD
    con["tot"] = both(np.full((P, 1), LD))
    con["causal"] = np.tile(bd(tri[:, ::-1]).reshape(P, 1, 2, P), (1, 4, 1, 1))
    lv = np.zeros((P, 7, C))
    for s in range(6):
        same = (i[:, None] // 2 ** (s + 1)) == (i[None] // 2 ** (s + 1))
        off = same & ((i[:, None] // 2 ** s) != (i[None] // 2 ** s))
        lv[:C, s] = (off & (i[:, None] > i[None])) | (i[:, None] == i[None])
        lv[C:, s] = (off & (i[:, None] < i[None])) | (i[:, None] == i[None])
    lv[:C, 6] = lv[:C, 0].T
    lv[C:, 6] = lv[C:, 0].T
    con["level"] = lv[:, :6]
    con["levelbd"] = bd(lv[:, [6, 1, 2, 3, 4, 5]]).reshape(P, 6, 2, C)
    con["eye2"] = np.concatenate([np.eye(C), np.eye(C)], 0)
    con["rank_tri"] = (np.arange(P)[:, None] < np.arange(P)[None])
    con["iota_e"] = np.tile(np.arange(NE), (P, 1))
    con["iota_p"] = np.arange(P)[:, None]
    con["thresh"] = np.tile(np.arange(8) * P, (P, 1))
    con["causal"] = con["causal"].reshape(P, 4, 2, 2, C)
    return {k: np.ascontiguousarray(v, np.float32) for k, v in con.items()}


def layout(a):
    g = {k: np.asarray(v) for k, v in a.items()}
    v = {k: x[0] for k, x in g.items() if k not in ("c", "c_ctx", "x", "ctx")}
    both = np.concatenate([g["ctx"][0], g["x"][0]], 0)
    cols = lambda r, k: r.reshape(k, P).T
    coef = np.zeros((P, 27, 4), np.float32)
    coef[:, :6, 1] = 1.0
    for j in range(3):
        coef[:, 6:12, j] = cols(v["hy_sconv_w"][j], 6)
    coef[:, 6:12, 3] = cols(v["hy_sconv_b"], 6)
    coef[:, 12:, 0] = cols(v["rw_mu"][0], 15)
    coef[:, 12:, 1] = 1.0
    coef[:, 12:, 2] = cols(v["rw_mu"][1], 15)
    two = lambda a: np.concatenate([np.broadcast_to(a[0], (C, RC)), np.broadcast_to(a[1], (C, RC))], 0)
    out = {
        "c_cols": np.stack([cols(g["c"][0], KD), cols(g["c_ctx"], KD)], 2),
        "w_ada": v["w_ada"],
        "b_cols": cols(v["b_ada"][:2 * D], 16),
        "b_rows": v["b_ada"][2 * D:],
        "hT": both.T.reshape(KD, P, T).transpose(1, 0, 2),
        "x": g["x"][0],
        "w_in": v["w_in"].reshape(KD, P, 27, P).transpose(2, 1, 0, 3),
        "coef": coef,
        "hf_w1": v["hf_w1"], "hf_w2": v["hf_w2"], "hf_w3": v["hf_w3"],
        "hf_b": np.stack([v["hf_b1"], v["hf_b2"], v["hf_b3"], v["hf_freq"]], 1),
        "hf_wout": v["hf_wout"],
        "hf_skip": v["hf_skip"].reshape(-1),
        "w0": two(v["rw_w0"]), "a0": two(v["rw_a0"]),
        "w_up": v["rw_w_up"].reshape(P, RC), "a_up": v["rw_a_up"].reshape(P, RC),
        "g_up": v["rw_g_up"],
        "rw_rows": np.concatenate([v["rw_k_k"], v["rw_k_a"], v["rw_r_k"].reshape(-1)]),
        "mix_rows": np.concatenate([v["conv_a"].reshape(-1), v["mix_norm_g"], v["rw_lnx_g"], v["rw_lnx_b"]]),
        "w_out": v["w_out"].reshape(KD, P, D).transpose(1, 0, 2),
        "ln_rows": np.concatenate([v["ln_g"][0], v["ln_b"][0], v["ln_g"][1], v["ln_b"][1]]),
        "w_router": v["w_router"].reshape(KD, P, NE).transpose(1, 0, 2),
        "e_bias": v["e_bias"],
        "w_e_gate": v["w_e_gate"], "w_e_up": v["w_e_up"], "w_e_down": v["w_e_down"],
        "w_s_gu": np.concatenate([v["w_s_gate"], v["w_s_up"]], 1).reshape(KD, P, 2 * FF).transpose(1, 0, 2),
        "w_s_down": v["w_s_down"].reshape(2, P, D).transpose(1, 0, 2),
    }
    out.update(shape_constants())
    return {k: np.ascontiguousarray(x) for k, x in out.items()}


def kernel(**inputs):
    import concourse.bacc as bacc
    from concourse.bass_utils import run_bass_kernel_spmd

    nc = bacc.Bacc("TRN2", target_bir_lowering=False, num_devices=1)
    arrays = {f"in_{k}": v for k, v in layout(inputs).items()}
    io = {k[3:]: nc.dram_tensor(k, v.shape, mybir.dt.from_np(v.dtype), kind="ExternalInput").ap() for k, v in arrays.items()}
    io["out"] = nc.dram_tensor("out_0", [1, L, D], F32, kind="ExternalOutput").ap()
    program(nc, io)
    r = run_bass_kernel_spmd(nc, [arrays], core_ids=[0])
    return r.results[0]["out_0"]
```
